# Optimizing a Trainium2 kernel written in Bass

```python
import math
import jax
import jax.numpy as jnp
from jax import lax
import numpy as np

D_MODEL = 1024
BATCH = 1
SEQ = 1024
DEPTH = 2

GRID_W = 64
CTX_LEN = 256
EPS = 1e-6
ROPE_THETA = 10000.0
Q_BLOCK = 128
MIX_HALF = D_MODEL // 2

A_HEAD_DIM = 64
A_HEADS = MIX_HALF // A_HEAD_DIM
A_KV_HEADS = A_HEADS // 4
A_GROUP = A_HEADS // A_KV_HEADS
B_NOPE_DIM = 64
B_ROPE_DIM = 32
B_V_DIM = 64
B_HEADS = MIX_HALF // B_V_DIM
B_Q_RANK = D_MODEL // 4
B_KV_RANK = D_MODEL // 8
C_WIDTH = MIX_HALF
C_ORDER = 2
C_SHORT_K = 3
C_POS_EMB = 33
C_FILTER_HIDDEN = 64
C_DECAY_TARGET = 1e-2
C_DECAY_FRAC_SHORT = 0.3
C_DECAY_FRAC_LONG = 1.5
D_INNER = MIX_HALF
D_HEAD_DIM = 64
D_HEADS = D_INNER // D_HEAD_DIM
D_GROUPS = 2
D_STATE = 128
D_CONV_K = 3
D_CHUNK = 128
FF_HIDDEN = 4 * D_MODEL

A_SCALE = A_HEAD_DIM ** -0.5
B_SCALE = (B_NOPE_DIM + B_ROPE_DIM) ** -0.5

EVEN_KV_SIZES = (A_KV_HEADS * A_HEAD_DIM, A_KV_HEADS * A_HEAD_DIM, B_KV_RANK, B_ROPE_DIM)
EVEN_Q_SIZES = (A_HEADS * A_HEAD_DIM, B_Q_RANK)
EVEN_KV_COLS = sum(EVEN_KV_SIZES)
EVEN_IN = EVEN_KV_COLS + sum(EVEN_Q_SIZES)
EVEN_OUT = A_HEADS * A_HEAD_DIM + B_HEADS * B_V_DIM
ODD_HY = (C_ORDER + 1) * C_WIDTH
ODD_Z = D_INNER
ODD_XBC = D_INNER + 2 * D_GROUPS * D_STATE
ODD_DT = 2 * D_HEADS
ODD_IN = ODD_HY + ODD_Z + ODD_XBC + ODD_DT
ODD_CTX_START = ODD_HY + ODD_Z
ODD_OUT = C_WIDTH + D_INNER

kernel_name = 'hybrid_dit_gqa_mla_hyena_ssd'

def rms_norm(x, g):
    xf = x.astype(jnp.float32)
    y = xf * lax.rsqrt(jnp.mean(xf * xf, axis=-1, keepdims=True) + EPS)
    return (y * g.astype(jnp.float32)).astype(x.dtype)

def modulate(h, shift, scale):
    return h * (1.0 + scale) + shift

def split_cols(p, sizes):
    return jnp.split(p, np.cumsum(sizes)[:-1].tolist(), axis=-1)

def centred_dwconv(u, w, b):
    k, ch = w.shape
    r = k // 2
    y = lax.conv_general_dilated(u, w[:, None, :].astype(u.dtype), window_strides=(1,),
                                 padding=[(r, r)], dimension_numbers=('NWC', 'WIO', 'NWC'),
                                 feature_group_count=ch)
    return y + b

def sq_relu_mlp(h, w1, w2):
    return jnp.square(jax.nn.relu(h @ w1)) @ w2

def axial_rope(n_tokens, rot_dim):
    rows = n_tokens // GRID_W
    r_idx, c_idx = jnp.meshgrid(jnp.arange(rows), jnp.arange(GRID_W), indexing='ij')
    quarter = rot_dim // 4
    inv_freq = ROPE_THETA ** (-jnp.arange(quarter, dtype=jnp.float32) / quarter)
    ang = jnp.concatenate([r_idx.reshape(-1, 1).astype(jnp.float32) * inv_freq,
                           c_idx.reshape(-1, 1).astype(jnp.float32) * inv_freq], axis=-1)
    return jnp.cos(ang), jnp.sin(ang)

def apply_rope(t, cos, sin):
    half = t.shape[-1] // 2
    t1 = t[..., :half].astype(jnp.float32)
    t2 = t[..., half:].astype(jnp.float32)
    return jnp.concatenate([t1 * cos - t2 * sin, t2 * cos + t1 * sin], axis=-1).astype(t.dtype)

def heads_first(t):
    return t.transpose(0, 2, 1, 3)

def attend(q, k, v, scale):
    s = jnp.einsum('bhgqd,bhkd->bhgqk', q, k).astype(jnp.float32) * scale
    p = jax.nn.softmax(s, axis=-1).astype(v.dtype)
    return jnp.einsum('bhgqk,bhkd->bhgqd', p, v)

def blocked_attend(q, k, v, scale):
    b, hk, g, L, dk = q.shape
    nb = L // Q_BLOCK
    qb = jnp.moveaxis(q.reshape(b, hk, g, nb, Q_BLOCK, dk), 3, 0)
    o = lax.map(lambda qi: attend(qi, k, v, scale), qb)
    return jnp.moveaxis(o, 0, 3).reshape(b, hk, g, L, v.shape[-1])

def merge_heads(o):
    b, hk, g, L, d = o.shape
    return o.transpose(0, 3, 1, 2, 4).reshape(b, L, hk * g * d)

def even_kv(p_kv, a_kn, b_kvn, b_wkv, rope_a, rope_b):
    bsz, L, _ = p_kv.shape
    ak, av, bkva, bkr = split_cols(p_kv, EVEN_KV_SIZES)
    ak = heads_first(rms_norm(ak.reshape(bsz, L, A_KV_HEADS, A_HEAD_DIM), a_kn))
    av = heads_first(av.reshape(bsz, L, A_KV_HEADS, A_HEAD_DIM))
    bkv = heads_first((rms_norm(bkva, b_kvn) @ b_wkv).reshape(bsz, L, B_HEADS, B_NOPE_DIM + B_V_DIM))
    bkr = bkr[:, None]
    if rope_a is not None:
        ak = apply_rope(ak, *rope_a)
        bkr = apply_rope(bkr, *rope_b)
    bk = jnp.concatenate([bkv[..., :B_NOPE_DIM],
                          jnp.broadcast_to(bkr, (bsz, B_HEADS, L, B_ROPE_DIM))], axis=-1)
    return ak, av, bk, bkv[..., B_NOPE_DIM:]

def even_q(p_q, a_qn, b_qn, b_wq, rope_a, rope_b):
    bsz, L, _ = p_q.shape
    aq, bqa = split_cols(p_q, EVEN_Q_SIZES)
    aq = heads_first(rms_norm(aq.reshape(bsz, L, A_HEADS, A_HEAD_DIM), a_qn))
    bq = heads_first((rms_norm(bqa, b_qn) @ b_wq).reshape(bsz, L, B_HEADS, B_NOPE_DIM + B_ROPE_DIM))
    if rope_a is not None:
        aq = apply_rope(aq, *rope_a)
        bq = jnp.concatenate([bq[..., :B_NOPE_DIM], apply_rope(bq[..., B_NOPE_DIM:], *rope_b)], axis=-1)
    return aq.reshape(bsz, A_KV_HEADS, A_GROUP, L, A_HEAD_DIM), bq[:, :, None]

def attention_mixer(hx, hc, w_in, w_out, a_qn, a_kn, b_qn, b_kvn, b_wq, b_wkv, need_ctx):
    L = hx.shape[1]
    rope_a = axial_rope(L, A_HEAD_DIM)
    rope_b = axial_rope(L, B_ROPE_DIM)
    px = hx @ w_in
    ka_x, va_x, kb_x, vb_x = even_kv(px[..., :EVEN_KV_COLS], a_kn, b_kvn, b_wkv, rope_a, rope_b)
    qa_x, qb_x = even_q(px[..., EVEN_KV_COLS:], a_qn, b_qn, b_wq, rope_a, rope_b)
    pc = hc @ (w_in if need_ctx else w_in[:, :EVEN_KV_COLS])
    ka_c, va_c, kb_c, vb_c = even_kv(pc[..., :EVEN_KV_COLS], a_kn, b_kvn, b_wkv, None, None)
    cat = lambda s, t: jnp.concatenate([s, t], axis=2)
    oa = blocked_attend(qa_x, cat(ka_x, ka_c), cat(va_x, va_c), A_SCALE)
    ob = blocked_attend(qb_x, cat(kb_x, kb_c), cat(vb_x, vb_c), B_SCALE)
    out_x = jnp.concatenate([merge_heads(oa), merge_heads(ob)], axis=-1) @ w_out
    if not need_ctx:
        return out_x, None
    qa_c, qb_c = even_q(pc[..., EVEN_KV_COLS:], a_qn, b_qn, b_wq, None, None)
    oa_c = attend(qa_c, ka_c, va_c, A_SCALE)
    ob_c = attend(qb_c, kb_c, vb_c, B_SCALE)
    out_c = jnp.concatenate([merge_heads(oa_c), merge_heads(ob_c)], axis=-1) @ w_out
    return out_x, out_c

def hyena_filter_spectrum(n_tokens, w1, b1, w2, b2, w3, freq):
    f32 = jnp.float32
    L = n_tokens
    t = jnp.linspace(0.0, 1.0, L, dtype=f32)
    bands = (C_POS_EMB - 1) // 2
    w = 2.0 * math.pi * jnp.arange(L, dtype=f32) / L
    fb = jnp.linspace(1e-4, bands - 1, bands, dtype=f32)
    ph = w[:, None] * fb[None, :]
    z = jnp.concatenate([t[:, None], jnp.cos(ph), -jnp.sin(ph)], axis=-1)
    fr = freq.astype(f32)
    h = jnp.sin(fr * (z @ w1.astype(f32) + b1.astype(f32)))
    h = jnp.sin(fr * (h @ w2.astype(f32) + b2.astype(f32)))
    h = (h @ w3.astype(f32)).reshape(L, C_ORDER, 2, C_WIDTH)
    decay_max = math.log(C_DECAY_TARGET) / C_DECAY_FRAC_SHORT
    decay_min = math.log(C_DECAY_TARGET) / C_DECAY_FRAC_LONG
    deltas = jnp.abs(jnp.linspace(decay_min, decay_max, C_WIDTH, dtype=f32))
    h = h * jnp.exp(-t[:, None] * deltas[None, :])[:, None, None, :]
    fwd, bwd = h[:, :, 0], h[:, :, 1]
    two_sided = jnp.concatenate([fwd, jnp.zeros_like(fwd[:1]), bwd[:0:-1]], axis=0)
    return jnp.fft.rfft(two_sided, axis=0)

def fft_long_conv(u, spec, skip):
    L = u.shape[1]
    uf = jnp.fft.rfft(u.astype(jnp.float32), n=2 * L, axis=1)
    y = jnp.fft.irfft(uf * spec[None], n=2 * L, axis=1)[:, :L]
    return (y + u.astype(jnp.float32) * skip.astype(jnp.float32)).astype(u.dtype)

def hyena_sequence(u3, short_w, short_b, spec, skip):
    uc = centred_dwconv(u3, short_w, short_b)
    parts = jnp.split(uc, C_ORDER + 1, axis=-1)
    z = parts[0]
    for o in range(C_ORDER):
        z = parts[o + 1] * fft_long_conv(z, spec[:, o], skip[o])
    return z

def segsum(a):
    T = a.shape[-1]
    cs = jnp.cumsum(a, axis=-1)
    diff = cs[..., :, None] - cs[..., None, :]
    mask = jnp.tril(jnp.ones((T, T), dtype=bool))
    return jnp.where(mask, diff, -jnp.inf)

def ssd_chunked(xs, dt, a, bm, cm, init_state, want_y):
    f32 = jnp.float32
    bsz, L, H, P = xs.shape
    G, N = bm.shape[2], bm.shape[3]
    E = H // G
    nc = L // D_CHUNK
    x = (xs.astype(f32) * dt[..., None]).reshape(bsz, nc, D_CHUNK, G, E, P)
    adt = (dt * a).reshape(bsz, nc, D_CHUNK, G, E).transpose(0, 3, 4, 1, 2)
    bc = bm.astype(f32).reshape(bsz, nc, D_CHUNK, G, N)
    cc = cm.astype(f32).reshape(bsz, nc, D_CHUNK, G, N)
    acs = jnp.cumsum(adt, axis=-1)
    decay_states = jnp.exp(acs[..., -1:] - acs)
    states = jnp.einsum('bclgn,bgecl,bclgep->bcgepn', bc, decay_states, x)
    states = jnp.concatenate([init_state[:, None], states], axis=1)
    chunk_decay = jnp.exp(segsum(jnp.pad(acs[..., -1], ((0, 0), (0, 0), (0, 0), (1, 0)))))
    states = jnp.einsum('bgezc,bcgepn->bzgepn', chunk_decay, states)
    final = states[:, -1]
    if not want_y:
        return None, final
    wdiag = jnp.einsum('bclgn,bcsgn->bgcls', cc, bc)[:, :, None] * jnp.exp(segsum(adt))
    y_diag = jnp.einsum('bgecls,bcsgep->bclgep', wdiag, x)
    y_off = jnp.einsum('bclgn,bcgepn,bgecl->bclgep', cc, states[:, :-1], jnp.exp(acs))
    return (y_diag + y_off).reshape(bsz, L, H, P), final

def mamba_inputs(p, conv_w, conv_b, dt_bias):
    bsz, L, _ = p.shape
    xbc, dt = split_cols(p, (ODD_XBC, ODD_DT))
    xbc = jax.nn.silu(centred_dwconv(xbc, conv_w, conv_b))
    xs, bm, cm = split_cols(xbc, (D_INNER, D_GROUPS * D_STATE, D_GROUPS * D_STATE))
    dt = jax.nn.softplus(dt.astype(jnp.float32).reshape(bsz, L, 2, D_HEADS) + dt_bias.astype(jnp.float32))
    return (xs.reshape(bsz, L, D_HEADS, D_HEAD_DIM), bm.reshape(bsz, L, D_GROUPS, D_STATE),
            cm.reshape(bsz, L, D_GROUPS, D_STATE), dt)

def bidir_ssd(lat, cx, a_log, need_ctx):
    xs_x, b_x, c_x, dt_x = lat
    xs_c, b_c, c_c, dt_c = cx
    bsz = xs_x.shape[0]
    state0 = jnp.zeros((bsz, D_GROUPS, D_HEADS // D_GROUPS, D_HEAD_DIM, D_STATE), jnp.float32)
    outs_x, outs_c = [], []
    for d in range(2):
        a = -jnp.exp(a_log[d].astype(jnp.float32))
        orient = (lambda t: t) if d == 0 else (lambda t: jnp.flip(t, 1))
        yc, s_c = ssd_chunked(orient(xs_c), orient(dt_c[:, :, d]), a, orient(b_c), orient(c_c), state0, need_ctx)
        yx, _ = ssd_chunked(orient(xs_x), orient(dt_x[:, :, d]), a, orient(b_x), orient(c_x), s_c, True)
        outs_x.append(orient(yx))
        if need_ctx:
            outs_c.append(orient(yc))
    y_c = outs_c[0] + outs_c[1] if need_ctx else None
    return outs_x[0] + outs_x[1], y_c

def mamba_out(y, xs, z, d_skip, norm_g):
    bsz, L = z.shape[0], z.shape[1]
    y = (y + xs.astype(jnp.float32) * d_skip.astype(jnp.float32)[:, None]).reshape(bsz, L, D_INNER)
    return rms_norm(y.astype(z.dtype) * jax.nn.silu(z), norm_g)

def long_conv_ssd_mixer(hx, hc, w_in, w_out, hy_short_w, hy_short_b, hy_w1, hy_b1, hy_w2, hy_b2,
                        hy_w3, hy_freq, hy_skip, mb_conv_w, mb_conv_b, mb_a_log, mb_dt_bias,
                        mb_d_skip, mb_norm, need_ctx):
    px = hx @ w_in
    hy_x, z_x, m_x = split_cols(px, (ODD_HY, ODD_Z, ODD_XBC + ODD_DT))
    spec_x = hyena_filter_spectrum(hx.shape[1], hy_w1, hy_b1, hy_w2, hy_b2, hy_w3, hy_freq)
    yh_x = hyena_sequence(hy_x, hy_short_w, hy_short_b, spec_x, hy_skip)
    lat = mamba_inputs(m_x, mb_conv_w, mb_conv_b, mb_dt_bias)
    pc = hc @ (w_in if need_ctx else w_in[:, ODD_CTX_START:])
    if need_ctx:
        hy_c, z_c, m_c = split_cols(pc, (ODD_HY, ODD_Z, ODD_XBC + ODD_DT))
    else:
        m_c = pc
    cx = mamba_inputs(m_c, mb_conv_w, mb_conv_b, mb_dt_bias)
    ym_x, ym_c = bidir_ssd(lat, cx, mb_a_log, need_ctx)
    out_x = jnp.concatenate([yh_x, mamba_out(ym_x, lat[0], z_x, mb_d_skip, mb_norm)], axis=-1) @ w_out
    if not need_ctx:
        return out_x, None
    spec_c = hyena_filter_spectrum(hc.shape[1], hy_w1, hy_b1, hy_w2, hy_b2, hy_w3, hy_freq)
    yh_c = hyena_sequence(hy_c, hy_short_w, hy_short_b, spec_c, hy_skip)
    out_c = jnp.concatenate([yh_c, mamba_out(ym_c, cx[0], z_c, mb_d_skip, mb_norm)], axis=-1) @ w_out
    return out_x, out_c

def setup_inputs(seed: int = 0) -> dict:
    key = jax.random.key(seed)
    ks = iter(jax.random.split(key, 64))
    f32 = jnp.float32
    ne = (DEPTH + 1) // 2
    no = DEPTH // 2

    def nrm(shape, fan_in, scale=1.0):
        return scale * fan_in ** -0.5 * jax.random.normal(next(ks), shape, f32)

    def gain(shape):
        return 1.0 + 0.05 * jax.random.normal(next(ks), shape, f32)

    def small(shape):
        return 0.02 * jax.random.normal(next(ks), shape, f32)

    x = jax.random.normal(next(ks), (BATCH, SEQ, D_MODEL), f32)
    c = jax.random.normal(next(ks), (BATCH, D_MODEL), f32)
    ctx = jax.random.normal(next(ks), (BATCH, CTX_LEN, D_MODEL), f32)
    c_ctx = jax.random.normal(next(ks), (D_MODEL,), f32)
    ada_w = nrm((DEPTH, D_MODEL, 6 * D_MODEL), D_MODEL, 0.5)
    ada_b = small((DEPTH, 6 * D_MODEL))
    norm_g = gain((DEPTH, 4, D_MODEL))
    ff_w1 = nrm((DEPTH, D_MODEL, FF_HIDDEN), D_MODEL)
    ff_w2 = nrm((DEPTH, FF_HIDDEN, D_MODEL), FF_HIDDEN)
    at_w_in = nrm((ne, D_MODEL, EVEN_IN), D_MODEL)
    at_w_out = nrm((ne, EVEN_OUT, D_MODEL), EVEN_OUT)
    ga_q_norm = gain((ne, A_HEAD_DIM))
    ga_k_norm = gain((ne, A_HEAD_DIM))
    ml_q_norm = gain((ne, B_Q_RANK))
    ml_kv_norm = gain((ne, B_KV_RANK))
    ml_w_q_up = nrm((ne, B_Q_RANK, B_HEADS * (B_NOPE_DIM + B_ROPE_DIM)), B_Q_RANK)
    ml_w_kv_up = nrm((ne, B_KV_RANK, B_HEADS * (B_NOPE_DIM + B_V_DIM)), B_KV_RANK)
    lc_w_in = nrm((no, D_MODEL, ODD_IN), D_MODEL)
    lc_w_out = nrm((no, ODD_OUT, D_MODEL), ODD_OUT)
    hy_short_w = nrm((no, C_SHORT_K, ODD_HY), C_SHORT_K)
    hy_short_b = small((no, ODD_HY))
    hy_w1 = nrm((no, C_POS_EMB, C_FILTER_HIDDEN), C_POS_EMB)
    hy_b1 = nrm((no, C_FILTER_HIDDEN), C_POS_EMB)
    hy_w2 = nrm((no, C_FILTER_HIDDEN, C_FILTER_HIDDEN), C_FILTER_HIDDEN)
    hy_b2 = nrm((no, C_FILTER_HIDDEN), C_FILTER_HIDDEN)
    hy_w3 = nrm((no, C_FILTER_HIDDEN, C_ORDER * 2 * C_WIDTH), C_FILTER_HIDDEN, 0.1)
    hy_freq = gain((no, C_FILTER_HIDDEN))
    hy_skip = jax.random.normal(next(ks), (no, C_ORDER, C_WIDTH), f32)
    mb_conv_w = nrm((no, D_CONV_K, ODD_XBC), D_CONV_K)
    mb_conv_b = small((no, ODD_XBC))
    mb_a_log = jnp.log(jax.random.uniform(next(ks), (no, 2, D_HEADS), f32, 1.0, 16.0))
    dt0 = jnp.exp(jax.random.uniform(next(ks), (no, 2, D_HEADS), f32, math.log(1e-3), math.log(1e-1)))
    mb_dt_bias = dt0 + jnp.log(-jnp.expm1(-dt0))
    mb_d_skip = gain((no, D_HEADS))
    mb_norm = gain((no, D_INNER))
    return {'x': x, 'c': c, 'ctx': ctx, 'c_ctx': c_ctx, 'ada_w': ada_w, 'ada_b': ada_b,
            'norm_g': norm_g, 'ff_w1': ff_w1, 'ff_w2': ff_w2, 'at_w_in': at_w_in, 'at_w_out': at_w_out,
            'ga_q_norm': ga_q_norm, 'ga_k_norm': ga_k_norm, 'ml_q_norm': ml_q_norm,
            'ml_kv_norm': ml_kv_norm, 'ml_w_q_up': ml_w_q_up, 'ml_w_kv_up': ml_w_kv_up,
            'lc_w_in': lc_w_in, 'lc_w_out': lc_w_out, 'hy_short_w': hy_short_w, 'hy_short_b': hy_short_b,
            'hy_w1': hy_w1, 'hy_b1': hy_b1, 'hy_w2': hy_w2, 'hy_b2': hy_b2, 'hy_w3': hy_w3,
            'hy_freq': hy_freq, 'hy_skip': hy_skip, 'mb_conv_w': mb_conv_w, 'mb_conv_b': mb_conv_b,
            'mb_a_log': mb_a_log, 'mb_dt_bias': mb_dt_bias, 'mb_d_skip': mb_d_skip, 'mb_norm': mb_norm}

def reference(x, c, ctx, c_ctx, ada_w, ada_b, norm_g, ff_w1, ff_w2, at_w_in, at_w_out,
              ga_q_norm, ga_k_norm, ml_q_norm, ml_kv_norm, ml_w_q_up, ml_w_kv_up,
              lc_w_in, lc_w_out, hy_short_w, hy_short_b, hy_w1, hy_b1, hy_w2, hy_b2, hy_w3,
              hy_freq, hy_skip, mb_conv_w, mb_conv_b, mb_a_log, mb_dt_bias, mb_d_skip, mb_norm):
    cond_x = jax.nn.silu(c)[:, None, :]
    cond_c = jax.nn.silu(c_ctx)
    for i in range(DEPTH):
        need_ctx = i < DEPTH - 1
        j = i // 2
        g = norm_g[i]
        mx = jnp.split(cond_x @ ada_w[i] + ada_b[i], 6, axis=-1)
        mc = jnp.split(cond_c @ ada_w[i] + ada_b[i], 6, axis=-1)
        hx = modulate(rms_norm(x, g[0]), mx[0], mx[1])
        hc = modulate(rms_norm(ctx, g[0]), mc[0], mc[1])
        if i % 2 == 0:
            ox, oc = attention_mixer(hx, hc, at_w_in[j], at_w_out[j], ga_q_norm[j], ga_k_norm[j],
                                     ml_q_norm[j], ml_kv_norm[j], ml_w_q_up[j], ml_w_kv_up[j], need_ctx)
        else:
            ox, oc = long_conv_ssd_mixer(hx, hc, lc_w_in[j], lc_w_out[j], hy_short_w[j], hy_short_b[j],
                                         hy_w1[j], hy_b1[j], hy_w2[j], hy_b2[j], hy_w3[j], hy_freq[j],
                                         hy_skip[j], mb_conv_w[j], mb_conv_b[j], mb_a_log[j],
                                         mb_dt_bias[j], mb_d_skip[j], mb_norm[j], need_ctx)
        x = x + mx[2] * rms_norm(ox, g[1])
        x = x + mx[5] * rms_norm(sq_relu_mlp(modulate(rms_norm(x, g[2]), mx[3], mx[4]),
                                             ff_w1[i], ff_w2[i]), g[3])
        if need_ctx:
            ctx = ctx + mc[2] * rms_norm(oc, g[1])
            ctx = ctx + mc[5] * rms_norm(sq_relu_mlp(modulate(rms_norm(ctx, g[2]), mc[3], mc[4]),
                                                     ff_w1[i], ff_w2[i]), g[3])
    return x


_drawn_inputs = setup_inputs


def setup_inputs(seed=0):
    import zlib

    import numpy as np

    out = dict(_drawn_inputs(seed))
    spreads = {}
    factors = {'ga_q_norm': 8.0,
     'ga_k_norm': 8.0,
     'ml_q_norm': 8.0,
     'ml_kv_norm': 3.942,
     'hy_short_b': 69.906,
     'hy_freq': 22.61,
     'mb_conv_b': 8.0,
     'mb_dt_bias': 15.276,
     'mb_d_skip': 157.865,
     'mb_norm': 148.958,
     'mb_a_log': 8.0,
     'hy_b2': 3.849,
     'hy_skip': 3.139}
    for name, (base, spread) in spreads.items():
        noise = np.random.default_rng([zlib.crc32(name.encode()), seed]).standard_normal(out[name].shape)
        drawn = base * np.exp(spread * noise) if base else spread * noise
        out[name] = jnp.asarray(drawn.astype(out[name].dtype))
    for name, factor in factors.items():
        out[name] = (out[name] * factor).astype(out[name].dtype)
    return out
```

```python
from contextlib import ExitStack, contextmanager
import math

import numpy as np
import concourse.bass as bass
from concourse import mybir

F32 = mybir.dt.float32
ACT = mybir.ActivationFunctionType
ALU = mybir.AluOpType
AX = mybir.AxisListType

P = 128
D = 1024
KT = D // P
LAT, CTX = 1024, 256
TOK = LAT + CTX
CHUNKS = [(0, 512), (512, 512), (1024, 256)]
STREAMS = [(0, LAT), (LAT, CTX)]
EPS = 1e-6
FF = 4 * D
GRID_W = 64
THETA = 10000.0
BANK = 512

A_DIM, A_HEADS = 64, 8
B_NOPE, B_ROPE, B_V, B_HEADS = 64, 32, 64, 8
B_DK = B_NOPE + B_ROPE
A_SCALE = A_DIM ** -0.5
B_SCALE = B_DK ** -0.5
KTILES = TOK // P
SHIFT_A, SCALE_A, GATE_A, SHIFT_M, SCALE_M, GATE_M = range(6)

VEC = {}
_at = 0
for _name, _n in (("ada_b", 2 * 96), ("norm_g", 2 * 4 * 16), ("gain_k", 1), ("gain_q", 1), ("mlq", 2), ("mlkv", 1),
                  ("short_w", 36), ("short_b", 12), ("skip", 8), ("conv_w", 24), ("conv_b", 8),
                  ("d_skip", 4), ("mb_norm", 4), ("dt_bias", 16), ("a_log", 16), ("hy_b1", 1), ("hy_b2", 1), ("freq", 1)):
    VEC[_name] = (_at, _n)
    _at += _n
NVEC = _at


STAGES = []


def tile(nc, mem, name, shape):
    return mem.enter_context(nc.sbuf_tensor(name, shape, F32, allow_name_mangling=True))


@contextmanager
def stage(nc, names):
    STAGES.append(names)
    sems = [nc.alloc_semaphore(f"{n}_{len(STAGES)}") for n in names.split()]
    with ExitStack() as mem:
        yield mem, sems
    nc.clear_and_free_semaphores(sems)
    nc.all_engine_barrier(sem_only=True)


def vec(g, name, i=0, n=1):
    at = VEC[name][0] + i
    return g.vec[:, at:at + n]


class Globals:
    pass


def load_constants(nc, g, d):
    with stage(nc, "loaded cond_ready gain_ready") as (mem, (loaded, cond_ready, gain_ready)):
        with nc.Block() as block:
            @block.sync
            def _(sp):
                for dst, src in ((g.vec, d["vec"]), (g.ident, d["ident"]), (g.ones, d["ones"]), (g.cond, d["cond"])):
                    sp.dma_start(dst[:], src).then_inc(loaded, 16)

            @block.scalar
            def _(act):
                act.wait_ge(loaded, 64)
                act.activation(g.cond[:], g.cond[:], ACT.Silu).then_inc(cond_ready, 1)

            @block.vector
            def _(dve):
                dve.memset(g.eps[:], EPS).then_inc(gain_ready, 1)
                dve.wait_ge(loaded, 64)
                dve.tensor_scalar(vec(g, "gain_q"), vec(g, "gain_q"), A_SCALE, None, ALU.mult).then_inc(gain_ready, 1)


def adaln(nc, g, d, layer):
    SLOTS, PIECES = 4, 24
    names = "w_loaded0 w_loaded1 w_loaded2 w_loaded3 w_used biased folded"
    with stage(nc, names) as (mem, sems):
        w_loaded, (w_used, biased, folded) = sems[:4], sems[4:]
        w = tile(nc, mem, "ada_ring", [P, SLOTS, KT, 256])
        src = d["ada_w"][layer]
        mod = g.mod[:, layer]
        acc = g.ps[:, 0, 0:96]
        with nc.Block() as block:
            @block.sync
            def _(sp):
                for s in range(SLOTS):
                    sp.dma_start(w[:, s], src[s]).then_inc(w_loaded[s], 16)
                with sp.Fori(1, PIECES // SLOTS) as i:
                    for s in range(SLOTS):
                        sp.wait_ge(w_used, (i - 1) * SLOTS + s + 1)
                        sp.dma_start(w[:, s], src[bass.ds(i * SLOTS + s, 1)].rearrange("a p k n -> p (a k) n")).then_inc(w_loaded[s], 16)

            @block.tensor
            def _(pe):
                with pe.Fori(0, PIECES // SLOTS) as i:
                    for s in range(SLOTS):
                        pe.wait_ge(w_loaded[s], (i + 1) * 16)
                        for m in range(2):
                            for k in range(KT):
                                mm = pe.matmul(g.ps[:, 0, bass.ds(i * (4 * SLOTS) + (4 * s + 2 * m), 2)],
                                               w[:, s, k, m * P:(m + 1) * P], g.cond[:, k, :],
                                               start=(k == 0), stop=(k == KT - 1))
                        mm.then_inc(w_used, 1)

            @block.vector
            def _(dve):
                dve.wait_ge(w_used, PIECES)
                flat = mod.rearrange("p a k s -> p (a k s)")
                dve.tensor_tensor(flat, acc, vec(g, "ada_b", 96 * layer, 96), ALU.add).then_inc(biased, 1)
                dve.wait_ge(biased, 1)
                for n, part in enumerate((SCALE_A, GATE_A, SCALE_M, GATE_M)):
                    gains = vec(g, "norm_g", (layer * 4 + n) * 16, 16)
                    now = mod[:, part].rearrange("p k s -> p (k s)")
                    if part in (SCALE_A, SCALE_M):
                        dve.scalar_tensor_tensor(out=now, in0=now, scalar=1.0, in1=gains, op0=ALU.add, op1=ALU.mult).then_inc(folded, 1)
                    else:
                        dve.tensor_tensor(now, now, gains, ALU.mult).then_inc(folded, 1)


def load(nc, pairs):
    with stage(nc, "loaded") as (mem, (loaded,)):
        with nc.Block() as block:
            @block.sync
            def _(sp):
                n = 0
                for dst, src in pairs:
                    for k in range(src.shape[1]):
                        sp.dma_start(dst[:, k, :], src[:, k, :]).then_inc(loaded, 16)
                        n += 1
                sp.wait_ge(loaded, 16 * n)


def chunks_of(tokens):
    return [(a, n) for a, n in CHUNKS if a < tokens]


def norm_modulate(nc, g, layer, scale_part, shift_part, tokens):
    streams = [(a, n) for a, n in STREAMS if a < tokens]
    with stage(nc, "squared square_used logged rstd scaled shifted") as (mem, (squared, square_used, logged, rstd, scaled, shifted)):
        sq = tile(nc, mem, "norm_sq", [P, 2, tokens])
        rs = tile(nc, mem, "norm_rs", [P, tokens])
        total = g.ps[:, 0:3, :].rearrange("p b n -> p (b n)")[:, 0:tokens]
        with nc.Block() as block:
            @block.scalar
            def _(act):
                for k in range(KT):
                    if k >= 2:
                        act.wait_ge(square_used, k - 1)
                    act.activation(sq[:, k % 2, :], g.x[:, k, 0:tokens], ACT.Square).then_inc(squared, 1)
                act.wait_ge(square_used, KT)
                act.activation(rs[:], total, ACT.Ln, bias=g.eps[:], scale=1.0 / D).then_inc(logged, 1)
                act.wait_ge(logged, 1)
                act.activation(rs[:], rs[:], ACT.Exp, scale=-0.5).then_inc(rstd, 1)
                for k in range(KT):
                    act.wait_ge(scaled, len(streams) * (k + 1))
                    for s, (a, n) in enumerate(streams):
                        act.activation(g.h[:, k, a:a + n], g.h[:, k, a:a + n], ACT.Identity,
                                       bias=g.mod[:, layer, shift_part, k, s:s + 1]).then_inc(shifted, 1)

            @block.tensor
            def _(pe):
                for k in range(KT):
                    pe.wait_ge(squared, k + 1)
                    for a, n in chunks_of(tokens):
                        mm = pe.matmul(total[:, a:a + n], g.ones[:], sq[:, k % 2, a:a + n], start=(k == 0), stop=(k == KT - 1))
                    mm.then_inc(square_used, 1)

            @block.vector
            def _(dve):
                dve.wait_ge(rstd, 1)
                for k in range(KT):
                    for s, (a, n) in enumerate(streams):
                        dve.scalar_tensor_tensor(out=g.h[:, k, a:a + n], in0=g.x[:, k, a:a + n],
                                                 scalar=g.mod[:, layer, scale_part, k, s:s + 1], in1=rs[:, a:a + n],
                                                 op0=ALU.mult, op1=ALU.mult).then_inc(scaled, 1)


def residual(nc, g, out, layer, gate_part, tokens):
    with stage(nc, "squared square_used logged rstd gated added") as (mem, (squared, square_used, logged, rstd, gated, added)):
        sq = tile(nc, mem, "norm_sq", [P, 2, tokens])
        rs = tile(nc, mem, "norm_rs", [P, tokens])
        total = g.ps[:, 0:3, :].rearrange("p b n -> p (b n)")[:, 0:tokens]
        with nc.Block() as block:
            @block.scalar
            def _(act):
                for k in range(KT):
                    if k >= 2:
                        act.wait_ge(square_used, k - 1)
                    act.activation(sq[:, k % 2, :], out[:, k, 0:tokens], ACT.Square).then_inc(squared, 1)
                act.wait_ge(square_used, KT)
                act.activation(rs[:], total, ACT.Ln, bias=g.eps[:], scale=1.0 / D).then_inc(logged, 1)
                act.wait_ge(logged, 1)
                act.activation(rs[:], rs[:], ACT.Exp, scale=-0.5).then_inc(rstd, 1)

            @block.tensor
            def _(pe):
                for k in range(KT):
                    pe.wait_ge(squared, k + 1)
                    for a, n in chunks_of(tokens):
                        mm = pe.matmul(total[:, a:a + n], g.ones[:], sq[:, k % 2, a:a + n], start=(k == 0), stop=(k == KT - 1))
                    mm.then_inc(square_used, 1)

            @block.vector
            def _(dve):
                dve.wait_ge(rstd, 1)
                n_gated = 0
                for k in range(KT):
                    for s, (a, n) in enumerate(STREAMS):
                        if a >= tokens:
                            continue
                        dve.scalar_tensor_tensor(out=out[:, k, a:a + n], in0=out[:, k, a:a + n],
                                                 scalar=g.mod[:, layer, gate_part, k, s:s + 1], in1=rs[:, a:a + n],
                                                 op0=ALU.mult, op1=ALU.mult).then_inc(gated, 1)
                        n_gated += 1
                    dve.wait_ge(gated, n_gated)
                    dve.tensor_tensor(g.x[:, k, 0:tokens], g.x[:, k, 0:tokens], out[:, k, 0:tokens], ALU.add).then_inc(added, 1)


def mlp(nc, g, out, hid, w1, w2, tokens):
    QUARTERS, SLOTS, BANKS = 4, 4, 4
    spans = chunks_of(tokens)
    units = [(m, a, n) for m in range(2 * SLOTS) for a, n in spans]
    U, PER_TILE = len(units), len(spans)
    PER_SLOT = 2 * PER_TILE
    names = "w_loaded0 w_loaded1 w_loaded2 w_loaded3 product up_free down_free rectified squared cleared summed"
    with stage(nc, names) as (mem, sems):
        w_loaded, (product, up_free, down_free, rectified, squared, cleared, summed) = sems[:4], sems[4:]
        ring = tile(nc, mem, "mlp_ring", [P, SLOTS, KT, 256])
        with nc.Block() as block:
            @block.sync
            def _(sp):
                def load(w, piece, s):
                    src = w[bass.ds(piece, 1)].rearrange("a p k n -> p (a k) n")
                    sp.dma_start(ring[:, s], src).then_inc(w_loaded[s], 16)
                for s in range(SLOTS):
                    load(w1, s, s)
                def down(q):
                    for s in range(SLOTS):
                        sp.wait_ge(product, q * (2 * U) + (s + 1) * PER_SLOT)
                        load(w2, q * SLOTS + s, s)
                with sp.Fori(0, QUARTERS - 1) as q:
                    down(q)
                    for s in range(SLOTS):
                        sp.wait_ge(product, q * (2 * U) + (U + (s + 1) * PER_SLOT))
                        load(w1, q * SLOTS + (SLOTS + s), s)
                down(QUARTERS - 1)

            @block.tensor
            def _(pe):
                with pe.Fori(0, QUARTERS) as q:
                    for half, (src, free) in enumerate(((g.h, up_free), (hid, down_free))):
                        for u, (m, a, n) in enumerate(units):
                            if u % PER_SLOT == 0:
                                pe.wait_ge(w_loaded[m // 2], q * 32 + 16 * (half + 1))
                            pe.wait_ge(free, q * U + (u + 1))
                            for k in range(KT):
                                if half == 1 and u == 0:
                                    pe.wait_ge(squared, q * U + (k + 1) * PER_TILE)
                                mm = pe.matmul(g.ps[:, half * BANKS + u % BANKS, 0:n],
                                               ring[:, m // 2, k, (m % 2) * P:(m % 2 + 1) * P],
                                               src[:, k, a:a + n], start=(k == 0), stop=(k == KT - 1))
                            mm.then_inc(product, 1)

            @block.scalar
            def _(act):
                act.sem_inc(up_free, BANKS)
                with act.Fori(0, QUARTERS) as q:
                    for u, (m, a, n) in enumerate(units):
                        act.wait_ge(product, q * (2 * U) + (u + 1))
                        act.activation(hid[:, m, a:a + n], g.ps[:, u % BANKS, 0:n], ACT.Relu).then_inc(up_free, 1)

            @block.vector
            def _(dve):
                dve.sem_inc(down_free, BANKS)
                dve.memset(out[:, :, 0:tokens], 0.0).then_inc(cleared, 1)
                dve.wait_ge(cleared, 1)
                with dve.Fori(0, QUARTERS) as q:
                    for u, (m, a, n) in enumerate(units):
                        dve.wait_ge(up_free, q * U + (BANKS + u + 1))
                        dve.tensor_tensor(hid[:, m, a:a + n], hid[:, m, a:a + n], hid[:, m, a:a + n], ALU.mult).then_inc(squared, 1)
                    for u, (m, a, n) in enumerate(units):
                        dve.wait_ge(product, q * (2 * U) + (U + u + 1))
                        dve.tensor_tensor(out[:, m, a:a + n], out[:, m, a:a + n],
                                          g.ps[:, BANKS + u % BANKS, 0:n], ALU.add).then_inc(down_free, 1)


def project_attention(nc, g, d, sc):
    TILES = 5
    units = [(t, a, n) for t in range(TILES) for a, n in CHUNKS]
    U = len(units)
    C = len(CHUNKS)

    names = "w_in tabs_in product raw_out squared meaned logged rstd normed rotated halves roped stored0 stored1"
    with stage(nc, names) as (mem, sems):
        w_in, tabs_in, product, raw_out, squared, meaned, logged, rstd, normed, rotated, halves, roped = sems[:12]
        stored = sems[12:]
        w = tile(nc, mem, "wa", [P, TILES, KT, P])
        cos, sin = tile(nc, mem, "cos_a", [P, TOK]), tile(nc, mem, "sin_a", [P, TOK])
        by_head, swap = tile(nc, mem, "ones_by_head", [P, P]), tile(nc, mem, "swap_halves", [P, P])
        raw, sq, rs, nrm, t1, t2, res = (tile(nc, mem, f"a_{x}", [P, 2, BANK]) for x in ("raw", "sq", "rs", "nrm", "t1", "t2", "res"))
        with nc.Block() as block:
            @block.sync
            def _(sp):
                for t in range(TILES):
                    sp.dma_start(w[:, t], d["w_qk"][t]).then_inc(w_in, 16)
                for dst, src in ((cos, "cos_a"), (sin, "sin_a"), (by_head, "by_head"), (swap, "swap_a")):
                    sp.dma_start(dst[:], d[src]).then_inc(tabs_in, 16)
                for u, (t, a, n) in enumerate(units):
                    sp.wait_ge(roped, u + 1)
                    sp.dma_start(sc.qk_a[t][:, a:a + n], res[:, u % 2, 0:n]).then_inc(stored[u % 2], 16)
                sp.wait_ge(stored[0], 16 * ((U + 1) // 2))
                sp.wait_ge(stored[1], 16 * (U // 2))

            @block.tensor
            def _(pe):
                pe.wait_ge(w_in, 16 * TILES)
                pe.wait_ge(tabs_in, 64)
                for step in range(U + 2):
                    if step < U:
                        t, a, n = units[step]
                        if step >= 3:
                            pe.wait_ge(squared, step - 2)
                        for k in range(KT):
                            mm = pe.matmul(g.ps[:, step % 3, 0:n], w[:, t, k, :], g.h[:, k, a:a + n], start=(k == 0), stop=(k == KT - 1))
                        mm.then_inc(product, 1)
                    if 0 <= step - 1 < U:
                        v = step - 1
                        n = units[v][2]
                        pe.wait_ge(squared, v + 1)
                        if v >= 2:
                            pe.wait_ge(logged, v - 1)
                        pe.matmul(g.ps[:, 3 + v % 2, 0:n], by_head[:], sq[:, v % 2, 0:n], start=True, stop=True).then_inc(meaned, 1)
                    if 0 <= step - 2 < U:
                        v = step - 2
                        n = units[v][2]
                        pe.wait_ge(normed, v + 1)
                        if v >= 2:
                            pe.wait_ge(halves, 2 * (v - 1))
                        pe.matmul(g.ps[:, 5 + v % 2, 0:n], swap[:], nrm[:, v % 2, 0:n], start=True, stop=True).then_inc(rotated, 1)

            @block.scalar
            def _(act):
                for step in range(U + 1):
                    if step < U:
                        n = units[step][2]
                        act.wait_ge(product, step + 1)
                        if step >= 2:
                            act.wait_ge(normed, step - 1)
                            act.wait_ge(meaned, step - 1)
                        act.activation(raw[:, step % 2, 0:n], g.ps[:, step % 3, 0:n], ACT.Copy).then_inc(raw_out, 1)
                        act.activation(sq[:, step % 2, 0:n], g.ps[:, step % 3, 0:n], ACT.Square).then_inc(squared, 1)
                    if step >= 1:
                        v = step - 1
                        n = units[v][2]
                        act.wait_ge(meaned, v + 1)
                        if v >= 2:
                            act.wait_ge(normed, v - 1)
                        act.activation(rs[:, v % 2, 0:n], g.ps[:, 3 + v % 2, 0:n], ACT.Ln, bias=g.eps[:], scale=1.0 / A_DIM).then_inc(logged, 1)
                        act.wait_ge(logged, v + 1)
                        act.activation(rs[:, v % 2, 0:n], rs[:, v % 2, 0:n], ACT.Exp, scale=-0.5).then_inc(rstd, 1)

            @block.vector
            def _(dve):
                dve.wait_ge(tabs_in, 64)
                for step in range(1, U + 2):
                    if step <= U:
                        v = step - 1
                        t, a, n = units[v]
                        dve.wait_ge(raw_out, v + 1)
                        dve.wait_ge(rstd, v + 1)
                        if v >= 2:
                            dve.wait_ge(rotated, v - 1)
                            dve.wait_ge(halves, 2 * (v - 1))
                        gain = vec(g, "gain_k" if t == 0 else "gain_q")
                        dve.scalar_tensor_tensor(out=nrm[:, v % 2, 0:n], in0=raw[:, v % 2, 0:n], scalar=gain,
                                                 in1=rs[:, v % 2, 0:n], op0=ALU.mult, op1=ALU.mult).then_inc(normed, 1)
                    if step >= 2:
                        v = step - 2
                        t, a, n = units[v]
                        dve.wait_ge(normed, v + 1)
                        dve.wait_ge(rotated, v + 1)
                        if v >= 2:
                            dve.wait_ge(roped, v - 1)
                            dve.wait_ge(stored[v % 2], 16 * (v // 2))
                        dve.tensor_tensor(t1[:, v % 2, 0:n], nrm[:, v % 2, 0:n], cos[:, a:a + n], ALU.mult).then_inc(halves, 1)
                        dve.tensor_tensor(t2[:, v % 2, 0:n], g.ps[:, 5 + v % 2, 0:n], sin[:, a:a + n], ALU.mult).then_inc(halves, 1)
                        dve.wait_ge(halves, 2 * (v + 1))
                        dve.tensor_tensor(res[:, v % 2, 0:n], t1[:, v % 2, 0:n], t2[:, v % 2, 0:n], ALU.add).then_inc(roped, 1)

    q_low = tile(nc, sc.mem, "q_low", [P, 2, TOK])
    kv_low = tile(nc, sc.mem, "kv_low", [P, TOK])
    groups = [((0, 1), (q_low[:, 0, :], q_low[:, 1, :]), ("mlq", 0), 256), ((2,), (kv_low[:],), ("mlkv", 0), 128)]
    gunits = [(gi, a, n) for gi in range(2) for a, n in CHUNKS]
    names = "w_in tabs_in product squared meaned logged rstd normed key_raw key_read key_rotated key_halves key_roped key_stored v_product v_out v_stored0 v_stored1"
    with stage(nc, names) as (mem, sems):
        (w_in, tabs_in, product, squared, meaned, logged, rstd, normed, key_raw, key_read, key_rotated, key_halves,
         key_roped, key_stored, v_product, v_out) = sems[:16]
        v_stored = sems[16:]
        w = tile(nc, mem, "w_low", [P, 3, KT, P])
        w_key = tile(nc, mem, "w_key", [P, KT, B_ROPE])
        w_v = tile(nc, mem, "w_v", [P, KT, P])
        cos, sin = tile(nc, mem, "cos_b", [P, TOK]), tile(nc, mem, "sin_b", [P, TOK])
        swap = tile(nc, mem, "swap_b", [P, P])
        sq = tile(nc, mem, "b_sq", [P, 3, BANK])
        raw = tile(nc, mem, "b_raw", [P, 3, BANK])
        rs = tile(nc, mem, "b_rs", [P, 2, BANK])
        key, kt1, kt2 = (tile(nc, mem, f"key_{x}", [P, TOK]) for x in ("raw", "t1", "t2"))
        vt = tile(nc, mem, "v_tile", [P, 2, P])
        tiles = [(gi, ti, a, n) for gi, a, n in gunits for ti in range(len(groups[gi][0]))]
        T = len(tiles)
        last_of = [max(i for i, x in enumerate(tiles) if (x[0], x[2]) == (gi, a)) for gi, a, n in gunits]
        rows = slice(B_NOPE, B_DK)
        with nc.Block() as block:
            @block.sync
            def _(sp):
                sp.dma_start(w[:], d["w_low"]).then_inc(w_in, 16)
                sp.dma_start(w_key[:], d["w_key"]).then_inc(w_in, 16)
                sp.dma_start(w_v[:], d["w_v_a"]).then_inc(w_in, 16)
                for dst, src in ((cos, "cos_b"), (sin, "sin_b"), (swap, "swap_b")):
                    sp.dma_start(dst[:], d[src]).then_inc(tabs_in, 16)
                sp.wait_ge(key_roped, C)
                for h in range(B_HEADS):
                    sp.dma_start(sc.k_b[h][rows, :], key[rows, :]).then_inc(key_stored, 16)
                for j in range(KTILES):
                    sp.wait_ge(v_out, j + 1)
                    sp.dma_start(sc.v_a[:, j, :], vt[:, j % 2, :]).then_inc(v_stored[j % 2], 16)
                sp.wait_ge(key_stored, 16 * B_HEADS)
                for s in range(2):
                    sp.wait_ge(v_stored[s], 16 * (KTILES // 2))

            @block.tensor
            def _(pe):
                pe.wait_ge(w_in, 48)
                pe.wait_ge(tabs_in, 48)
                for c, (a, n) in enumerate(CHUNKS):
                    for k in range(KT):
                        mm = pe.matmul(g.ps[rows, c, 0:n], w_key[:, k, :], g.h[:, k, a:a + n], start=(k == 0), stop=(k == KT - 1))
                    mm.then_inc(key_raw, 1)
                def mean(v):
                    gi, a, n = gunits[v]
                    pe.wait_ge(squared, last_of[v] + 1)
                    if v >= 2:
                        pe.wait_ge(logged, v - 1)
                    first = last_of[v] + 1 - len(groups[gi][0])
                    for i in range(first, last_of[v] + 1):
                        mm = pe.matmul(g.ps[:, 6 + v % 2, 0:n], g.ones[:], sq[:, i % 3, 0:n], start=(i == first), stop=(i == last_of[v]))
                    mm.then_inc(meaned, 1)
                due = 0
                for i, (gi, ti, a, n) in enumerate(tiles):
                    if i >= 3:
                        pe.wait_ge(squared, i - 2)
                    for k in range(KT):
                        mm = pe.matmul(g.ps[:, 3 + i % 3, 0:n], w[:, groups[gi][0][ti], k, :], g.h[:, k, a:a + n], start=(k == 0), stop=(k == KT - 1))
                    mm.then_inc(product, 1)
                    if due < len(gunits) and last_of[due] < i:
                        mean(due)
                        due += 1
                while due < len(gunits):
                    mean(due)
                    due += 1
                for c, (a, n) in enumerate(CHUNKS):
                    pe.wait_ge(key_read, c + 1)
                    pe.matmul(g.ps[rows, c, 0:n], swap[rows, rows], key[rows, a:a + n], start=True, stop=True).then_inc(key_rotated, 1)
                for j in range(KTILES):
                    if j < 3:
                        pe.wait_ge(squared, T)
                    else:
                        pe.wait_ge(v_out, j - 2)
                    for k in range(KT):
                        mm = pe.matmul(g.ps[:, 3 + j % 3, 0:P], g.h[:, k, j * P:(j + 1) * P], w_v[:, k, :], start=(k == 0), stop=(k == KT - 1))
                    mm.then_inc(v_product, 1)

            @block.scalar
            def _(act):
                for c, (a, n) in enumerate(CHUNKS):
                    act.wait_ge(key_raw, c + 1)
                    act.activation(key[rows, a:a + n], g.ps[rows, c, 0:n], ACT.Copy).then_inc(key_read, 1)
                due = 0
                def root(v):
                    gi, a, n = gunits[v]
                    act.wait_ge(meaned, v + 1)
                    if v >= 2:
                        act.wait_ge(normed, last_of[v - 2] + 1)
                    act.activation(rs[:, v % 2, 0:n], g.ps[:, 6 + v % 2, 0:n], ACT.Ln, bias=g.eps[:], scale=1.0 / groups[gi][3]).then_inc(logged, 1)
                    act.wait_ge(logged, v + 1)
                    act.activation(rs[:, v % 2, 0:n], rs[:, v % 2, 0:n], ACT.Exp, scale=-0.5).then_inc(rstd, 1)
                for i, (gi, ti, a, n) in enumerate(tiles):
                    act.wait_ge(product, i + 1)
                    if i >= 3:
                        act.wait_ge(normed, i - 2)
                        act.wait_ge(meaned, gunits.index((tiles[i - 3][0],) + tiles[i - 3][2:]) + 1)
                    act.activation(raw[:, i % 3, 0:n], g.ps[:, 3 + i % 3, 0:n], ACT.Copy).then_inc(key_read, 1)
                    act.activation(sq[:, i % 3, 0:n], g.ps[:, 3 + i % 3, 0:n], ACT.Square).then_inc(squared, 1)
                    if last_of[due] < i:
                        root(due)
                        due += 1
                while due < len(gunits):
                    root(due)
                    due += 1
                for j in range(KTILES):
                    act.wait_ge(v_product, j + 1)
                    if j >= 2:
                        act.wait_ge(v_stored[j % 2], 16 * (j // 2))
                    act.activation(vt[:, j % 2, :], g.ps[:, 3 + j % 3, 0:P], ACT.Copy).then_inc(v_out, 1)

            @block.vector
            def _(dve):
                for v, (gi, a, n) in enumerate(gunits):
                    dve.wait_ge(rstd, v + 1)
                    size = len(groups[gi][0])
                    for ti in range(size):
                        i = last_of[v] + 1 - size + ti
                        name, at = groups[gi][2]
                        dve.wait_ge(key_read, C + i + 1)
                        dve.scalar_tensor_tensor(out=groups[gi][1][ti][:, a:a + n], in0=raw[:, i % 3, 0:n], scalar=vec(g, name, at + ti),
                                                 in1=rs[:, v % 2, 0:n], op0=ALU.mult, op1=ALU.mult).then_inc(normed, 1)
                dve.wait_ge(tabs_in, 48)
                for c, (a, n) in enumerate(CHUNKS):
                    dve.wait_ge(key_rotated, c + 1)
                    dve.tensor_tensor(kt1[rows, a:a + n], key[rows, a:a + n], cos[rows, a:a + n], ALU.mult).then_inc(key_halves, 1)
                    dve.tensor_tensor(kt2[rows, a:a + n], g.ps[rows, c, 0:n], sin[rows, a:a + n], ALU.mult).then_inc(key_halves, 1)
                    dve.wait_ge(key_halves, 2 * (c + 1))
                    dve.tensor_tensor(key[rows, a:a + n], kt1[rows, a:a + n], kt2[rows, a:a + n], ALU.add).then_inc(key_roped, 1)

    names = "w_in w_head0 w_head1 tabs_in product raw_out rotated halves roped q_stored0 q_stored1 k_product k_out k_stored0 k_stored1 v_product v_out v_stored0 v_stored1"
    units = [(h, c, a, n) for h in range(B_HEADS) for c, (a, n) in enumerate(CHUNKS)]
    U = len(units)
    with stage(nc, names) as (mem, sems):
        (w_in, w_head0, w_head1, tabs_in, product, raw_out, rotated, halves, roped, q_stored0, q_stored1, k_product, k_out,
         k_stored0, k_stored1, v_product, v_out, v_stored0, v_stored1) = sems
        q_stored, k_stored, v_stored = (q_stored0, q_stored1), (k_stored0, k_stored1), (v_stored0, v_stored1)
        wq = tile(nc, mem, "w_q_up", [P, 2, B_HEADS * B_DK])
        wk = tile(nc, mem, "w_k_up", [P, B_HEADS * B_NOPE])
        wv = tile(nc, mem, "w_v_up", [P, B_HEADS * B_V])
        cos, sin = tile(nc, mem, "cos_b", [P, TOK]), tile(nc, mem, "sin_b", [P, TOK])
        swap = tile(nc, mem, "swap_b", [P, P])
        raw, t1, t2, res, kres, vres = (tile(nc, mem, f"u_{x}", [P, 2, BANK]) for x in ("raw", "t1", "t2", "res", "k", "v"))
        top = slice(0, B_DK)
        nope = slice(0, B_NOPE)
        with nc.Block() as block:
            @block.sync
            def _(sp):
                for dst, src in ((wq, "w_q_up"), (wk, "w_k_up"), (wv, "w_v_up"), (cos, "cos_b"), (sin, "sin_b"), (swap, "swap_b")):
                    sp.dma_start(dst[:], d[src]).then_inc(tabs_in, 16)
                for j in range(KTILES):
                    sp.wait_ge(v_out, j + 1)
                    sp.dma_start(sc.v_b[:, j, :], vres[:, j % 2, :]).then_inc(v_stored[j % 2], 16)
                for u, (h, c, a, n) in enumerate(units):
                    sp.wait_ge(k_out, u + 1)
                    sp.dma_start(sc.k_b[h][nope, a:a + n], kres[nope, u % 2, 0:n]).then_inc(k_stored[u % 2], 16)
                    sp.wait_ge(roped, u + 1)
                    sp.dma_start(sc.q_b[h][:, a:a + n], res[top, u % 2, 0:n]).then_inc(q_stored[u % 2], 16)
                for s in range(2):
                    sp.wait_ge(v_stored[s], 16 * (KTILES // 2))
                    sp.wait_ge(k_stored[s], 16 * (U // 2))
                    sp.wait_ge(q_stored[s], 16 * (U // 2))

            @block.tensor
            def _(pe):
                pe.wait_ge(tabs_in, 96)
                for j in range(KTILES):
                    if j >= 2:
                        pe.wait_ge(v_out, j - 1)
                    pe.matmul(g.ps[:, 6 + j % 2, :], kv_low[:, j * P:(j + 1) * P], wv[:], start=True, stop=True).then_inc(v_product, 1)
                for step in range(U + 1):
                    if step < U:
                        h, c, a, n = units[step]
                        if step >= 2:
                            pe.wait_ge(raw_out, step - 1)
                        for k in range(2):
                            mm = pe.matmul(g.ps[top, step % 2, 0:n], wq[:, k, h * B_DK:(h + 1) * B_DK], q_low[:, k, a:a + n], start=(k == 0), stop=(k == 1))
                        mm.then_inc(product, 1)
                        if step >= 2:
                            pe.wait_ge(k_out, step - 1)
                        pe.matmul(g.ps[nope, 4 + step % 2, 0:n], wk[:, h * B_NOPE:(h + 1) * B_NOPE], kv_low[:, a:a + n], start=True, stop=True).then_inc(k_product, 1)
                    if step >= 1:
                        v = step - 1
                        n = units[v][3]
                        pe.wait_ge(raw_out, v + 1)
                        if v >= 2:
                            pe.wait_ge(halves, 2 * (v - 1))
                        pe.matmul(g.ps[top, 2 + v % 2, 0:n], swap[top, top], raw[top, v % 2, 0:n], start=True, stop=True).then_inc(rotated, 1)

            @block.scalar
            def _(act):
                for j in range(KTILES):
                    act.wait_ge(v_product, j + 1)
                    if j >= 2:
                        act.wait_ge(v_stored[j % 2], 16 * (j // 2))
                    act.activation(vres[:, j % 2, :], g.ps[:, 6 + j % 2, :], ACT.Copy).then_inc(v_out, 1)
                for u, (h, c, a, n) in enumerate(units):
                    act.wait_ge(product, u + 1)
                    if u >= 2:
                        act.wait_ge(halves, 2 * (u - 1))
                        act.wait_ge(rotated, u - 1)
                    act.activation(raw[top, u % 2, 0:n], g.ps[top, u % 2, 0:n], ACT.Copy, scale=B_SCALE).then_inc(raw_out, 1)
                    act.wait_ge(k_product, u + 1)
                    if u >= 2:
                        act.wait_ge(k_stored[u % 2], 16 * (u // 2))
                    act.activation(kres[nope, u % 2, 0:n], g.ps[nope, 4 + u % 2, 0:n], ACT.Copy).then_inc(k_out, 1)

            @block.vector
            def _(dve):
                dve.wait_ge(tabs_in, 96)
                for v, (h, c, a, n) in enumerate(units):
                    dve.wait_ge(raw_out, v + 1)
                    dve.wait_ge(rotated, v + 1)
                    if v >= 2:
                        dve.wait_ge(roped, v - 1)
                        dve.wait_ge(q_stored[v % 2], 16 * (v // 2))
                    dve.tensor_tensor(t1[top, v % 2, 0:n], raw[top, v % 2, 0:n], cos[top, a:a + n], ALU.mult).then_inc(halves, 1)
                    dve.tensor_tensor(t2[top, v % 2, 0:n], g.ps[top, 2 + v % 2, 0:n], sin[top, a:a + n], ALU.mult).then_inc(halves, 1)
                    dve.wait_ge(halves, 2 * (v + 1))
                    dve.tensor_tensor(res[top, v % 2, 0:n], t1[top, v % 2, 0:n], t2[top, v % 2, 0:n], ALU.add).then_inc(roped, 1)


def attention(nc, g, sc, out):
    PAIRS = 4
    QB = 256
    steps = [(b, h, t) for b in range(TOK // QB) for h in range(2) for t in range(2)]
    S = len(steps)
    LAT_BLOCKS = LAT // QB

    def keys_of(b):
        return (0, KTILES) if b < LAT_BLOCKS else (LAT // P, KTILES)

    def turns(b):
        lo, hi = keys_of(b)
        return [(i, min(i + 4, hi)) for i in range(lo, hi, 4)]

    TURNS = sum(len(turns(b)) for b, h, t in steps)
    turn_at = []
    n = 0
    for b, h, t in steps:
        turn_at.append(n)
        n += len(turns(b))
    B = TOK // QB

    for kind in range(2):
        dk = (A_DIM, B_DK)[kind]
        names = "staged0 staged1 scores maxed exped inverse probs turned turned_out mixed mixed_out"
        with stage(nc, names) as (mem, sems):
            staged, (scores, maxed, exped, inverse, probs, turned, turned_out, mixed, mixed_out) = sems[:2], sems[2:]
            q = tile(nc, mem, "q_pair", [P, 2, 2, TOK])
            k = tile(nc, mem, "k_pair", [P, 2, 2, TOK])
            v = tile(nc, mem, "v_pair", [P, 2, KTILES, 2, B_V])
            p = tile(nc, mem, "probs", [P, 3, TOK])
            pt = tile(nc, mem, "probs_turned", [P, 2, 2, KTILES, QB])
            neg_max, total, inv = (tile(nc, mem, f"row_{x}", [P, 4]) for x in ("max", "sum", "inv"))
            LOADS = (4, 3)[kind]
            with nc.Block() as block:
                def rows(h):
                    return slice(64 * h, 64 * h + dk) if kind == 0 else slice(0, dk)

                def q_of(s, h, t0):
                    return q[rows(h), s, 0 if kind == 0 else h, t0:t0 + P]

                def k_of(s, h, a, n):
                    return k[rows(h), s, 0 if kind == 0 else h, a:a + n]

                @block.sync
                def _(sp):
                    for pair in range(PAIRS):
                        s = pair % 2
                        if pair >= 2:
                            sp.wait_ge(mixed, B * (pair - 1))
                        if kind == 0:
                            sp.dma_start(q[:, s, 0, :], sc.qk_a[1 + pair]).then_inc(staged[s], 16)
                            for h in range(2):
                                sp.dma_start(k[rows(h), s, 0, :], sc.qk_a[0][64 * (pair // 2):64 * (pair // 2) + 64, :]).then_inc(staged[s], 16)
                                sp.dma_start(v[:, s, :, h, :], sc.v_a[:, :, 64 * (pair // 2):64 * (pair // 2) + 64]).then_inc(staged[s], 16)
                        else:
                            sp.dma_start(q[0:dk, s], sc.q_b[2 * pair:2 * pair + 2].rearrange("h p n -> p h n")).then_inc(staged[s], 16)
                            sp.dma_start(k[0:dk, s], sc.k_b[2 * pair:2 * pair + 2].rearrange("h p n -> p h n")).then_inc(staged[s], 16)
                            sp.dma_start(v[:, s], sc.v_b[:, :, 128 * pair:128 * pair + 128].rearrange("p j (h n) -> p j h n", h=2)).then_inc(staged[s], 16)

                N_LOADS = 5 if kind == 0 else 3
                ALL = [(pair, i) for pair in range(PAIRS) for i in range(S)]

                def g_turn(x):
                    return (x // S) * TURNS + turn_at[x % S]

                @block.tensor
                def _(pe):
                    def score_parts(x):
                        pair, i = ALL[x]
                        b, h, t = steps[i]
                        lo, hi = keys_of(b)
                        parts = [(a, min(BANK, hi * P - a)) for a in range(lo * P, hi * P, BANK)]
                        for j, (a, n) in enumerate(parts):
                            if j == 0:
                                if i == 0:
                                    pe.wait_ge(staged[pair % 2], 16 * N_LOADS * (pair // 2 + 1))
                                if x >= 2:
                                    pe.wait_ge(exped, x - 1)
                            mm = pe.matmul(g.ps[:, 3 * (x % 2) + j, 0:n], q_of(pair % 2, h, b * QB + t * P), k_of(pair % 2, h, a, n), start=True, stop=True)
                            if j == len(parts) - 1:
                                mm.then_inc(scores, 1)
                            yield

                    def turn_parts(x):
                        pair, i = ALL[x]
                        b, h, t = steps[i]
                        for j, (lo, hi) in enumerate(turns(b)):
                            if j == 0:
                                pe.wait_ge(probs, x + 1)
                            n_turn = g_turn(x) + j
                            if n_turn >= 1:
                                pe.wait_ge(turned_out, n_turn)
                            for kt in range(lo, hi):
                                mm = pe.transpose(g.ps[:, 6, (kt - lo) * P:(kt - lo + 1) * P], p[:, x % 3, (kt - keys_of(b)[0]) * P:(kt - keys_of(b)[0] + 1) * P], g.ident[:])
                            mm.then_inc(turned, 1)
                            yield

                    def mix_parts(y):
                        pair, b = divmod(y, B)
                        lo, hi = keys_of(b)
                        last = pair * S + (b + 1) * 4 - 1
                        pe.wait_ge(turned_out, g_turn(last) + len(turns(b)))
                        if y >= 1:
                            pe.wait_ge(mixed_out, y)
                        for kt in range(lo, hi):
                            for h in range(2):
                                mm = pe.matmul(g.ps[64 * h:64 * h + 64, 7, 0:QB], v[:, pair % 2, kt, h, :], pt[:, y % 2, h, kt, :],
                                               start=(kt == lo), stop=(kt == hi - 1))
                            if kt == hi - 1:
                                mm.then_inc(mixed, 1)
                            yield

                    mixing = iter(())
                    N = len(ALL)
                    for x in range(N + 2):
                        sc_it = score_parts(x) if x < N else iter(())
                        tu_it = turn_parts(x - 2) if x >= 2 else iter(())
                        for _ in range(3):
                            next(sc_it, None)
                            next(tu_it, None)
                            next(mixing, None)
                        if x >= 2 and (x - 2) % 4 == 3:
                            for _ in mixing:
                                pass
                            mixing = mix_parts((x - 2) // 4)
                    for _ in mixing:
                        pass

                @block.vector
                def _(dve):
                    def wide(b):
                        lo, hi = keys_of(b)
                        return (hi - lo) * P

                    N = len(ALL)
                    for x in range(N + 1):
                        if x < N:
                            b, h, t = steps[ALL[x][1]]
                            dve.wait_ge(scores, x + 1)
                            if x >= 4:
                                dve.wait_ge(exped, x - 3)
                            flat = g.ps[:, 3 * (x % 2):3 * (x % 2) + 3, :].rearrange("p b n -> p (b n)")[:, 0:wide(b)]
                            dve.tensor_reduce(neg_max[:, x % 4:x % 4 + 1], flat, AX.X, ALU.max, negate=True).then_inc(maxed, 1)
                        if x >= 1:
                            y = x - 1
                            b = steps[ALL[y][1]][0]
                            dve.wait_ge(exped, y + 1)
                            if y >= 4:
                                dve.wait_ge(probs, y - 3)
                            dve.reciprocal(inv[:, y % 4:y % 4 + 1], total[:, y % 4:y % 4 + 1]).then_inc(inverse, 1)
                            dve.wait_ge(inverse, y + 1)
                            dve.tensor_scalar(p[:, y % 3, 0:wide(b)], p[:, y % 3, 0:wide(b)], inv[:, y % 4:y % 4 + 1], None, ALU.mult).then_inc(probs, 1)

                @block.scalar
                def _(act):
                    N = len(ALL)

                    def turn_out(x, j):
                        pair, i = ALL[x]
                        b, h, t = steps[i]
                        lo, hi = turns(b)[j]
                        y = pair * B + b
                        n_turn = g_turn(x) + j
                        act.wait_ge(turned, n_turn + 1)
                        if y >= 2 and h == 0 and t == 0 and j == 0:
                            act.wait_ge(mixed, y - 1)
                        act.activation(pt[:, y % 2, h, lo:hi, t * P:(t + 1) * P],
                                       g.ps[:, 6, 0:(hi - lo) * P].rearrange("p (k n) -> p k n", n=P), ACT.Copy).then_inc(turned_out, 1)

                    def mix_out(y):
                        pair, b = divmod(y, B)
                        act.wait_ge(mixed, y + 1)
                        act.activation(out[:, kind * PAIRS + pair, b * QB:(b + 1) * QB], g.ps[:, 7, 0:QB], ACT.Copy).then_inc(mixed_out, 1)

                    emitted = 0
                    for x in range(N + 2):
                        if x < N:
                            b, h, t = steps[ALL[x][1]]
                            lo, hi = keys_of(b)
                            w = (hi - lo) * P
                        if x >= 2:
                            y = x - 2
                            for j in range(len(turns(steps[ALL[y][1]][0]))):
                                turn_out(y, j)
                        if x < N:
                            act.wait_ge(maxed, x + 1)
                            if x >= 3:
                                act.wait_ge(turned, g_turn(x - 3) + len(turns(steps[ALL[x - 3][1]][0])))
                            if x >= 4:
                                act.wait_ge(inverse, x - 3)
                            flat = g.ps[:, 3 * (x % 2):3 * (x % 2) + 3, :].rearrange("p b n -> p (b n)")[:, 0:w]
                            act.activation(p[:, x % 3, 0:w], flat, ACT.Exp, bias=neg_max[:, x % 4:x % 4 + 1], accum_out=total[:, x % 4:x % 4 + 1]).then_inc(exped, 1)
                        if x >= 9 and (x - 9) % 4 == 0:
                            mix_out((x - 9) // 4)
                            emitted = (x - 9) // 4 + 1
                    while emitted < PAIRS * B:
                        mix_out(emitted)
                        emitted += 1


def project_out(nc, g, src, w, out, tokens):
    PIECES, BANKS = 4, 8
    spans = chunks_of(tokens)
    units = [(m, a, n) for m in range(2 * PIECES) for a, n in spans]
    with stage(nc, "w_in0 w_in1 w_in2 w_in3 product read_out") as (mem, sems):
        w_in, (product, read_out) = sems[:4], sems[4:]
        ring = tile(nc, mem, "w_out", [P, PIECES, KT, 256])
        with nc.Block() as block:
            @block.sync
            def _(sp):
                for s in range(PIECES):
                    sp.dma_start(ring[:, s], w[s]).then_inc(w_in[s], 16)

            @block.tensor
            def _(pe):
                for u, (m, a, n) in enumerate(units):
                    pe.wait_ge(w_in[m // 2], 16)
                    if u >= BANKS:
                        pe.wait_ge(read_out, u - BANKS + 1)
                    for k in range(KT):
                        mm = pe.matmul(g.ps[:, u % BANKS, 0:n], ring[:, m // 2, k, (m % 2) * P:(m % 2 + 1) * P], src[:, k, a:a + n],
                                       start=(k == 0), stop=(k == KT - 1))
                    mm.then_inc(product, 1)

            @block.scalar
            def _(act):
                for u, (m, a, n) in enumerate(units):
                    act.wait_ge(product, u + 1)
                    act.activation(out[:, m, a:a + n], g.ps[:, u % BANKS, 0:n], ACT.Copy).then_inc(read_out, 1)


def project_mamba(nc, g, d, xbc, gate, dt, adt):
    TILES, Z_TILES, BANKS = 8, 4, 4
    units = [(t, a, n) for t in range(TILES) for a, n in CHUNKS]
    zunits = [(t, a, n) for t in range(Z_TILES) for a, n in CHUNKS[:2]]
    U, C = len(units), len(CHUNKS)
    WIDE = LAT + CTX + 4
    LAT_AT, CTX_AT = 1, LAT + 3
    names = ("w_in0 w_in1 w_in2 w_z w_dt product z_product dt_product raw_out z_out padded conv conv_read dt_out steps "
             "magnitude decayed logged a_exp")
    with stage(nc, names) as (mem, sems):
        w_in, (w_z, w_dt, product, z_product, dt_product, raw_out, z_out, padded, conv, conv_read, dt_out, steps,
               magnitude, decayed, logged, a_exp) = sems[:3], sems[3:]
        ring = tile(nc, mem, "w_xbc", [P, 3, KT, P])
        wz = tile(nc, mem, "w_z", [P, Z_TILES, KT, P])
        wdt = tile(nc, mem, "w_dt", [P, KT, 16])
        raw = tile(nc, mem, "xbc_raw", [P, 2, WIDE])
        acc = tile(nc, mem, "conv_acc", [P, 2, WIDE])
        T16 = [P, KTILES, 16]
        mag, ex, one_e, lg, zero, den = (tile(nc, mem, f"dt_{x}", T16) for x in ("mag", "exp", "one", "log", "zero", "den"))
        rate = tile(nc, mem, "a_rate", [P, 16])
        over_tiles = lambda ap: ap.unsqueeze(1).to_broadcast(T16)
        with nc.Block() as block:
            def silu_conv(act, t):
                act.wait_ge(conv, t + 1)
                act.activation(xbc[:, t, 0:LAT], acc[:, t % 2, LAT_AT:LAT_AT + LAT], ACT.Silu, bias=vec(g, "conv_b", t)).then_inc(conv_read, 1)
                act.activation(xbc[:, t, LAT:TOK], acc[:, t % 2, CTX_AT:CTX_AT + CTX], ACT.Silu, bias=vec(g, "conv_b", t)).then_inc(conv_read, 1)

            @block.sync
            def _(sp):
                sp.dma_start(wdt[:], d["w_dt"]).then_inc(w_dt, 16)
                for t in range(TILES):
                    if t >= 3:
                        sp.wait_ge(product, C * (t - 2))
                    sp.dma_start(ring[:, t % 3], d["w_xbc"][t]).then_inc(w_in[t % 3], 16)
                sp.dma_start(wz[:], d["w_z"].rearrange("t p k n -> p t k n")).then_inc(w_z, 16)

            @block.tensor
            def _(pe):
                pe.wait_ge(w_dt, 16)
                for j in range(KTILES):
                    for k in range(KT):
                        mm = pe.matmul(g.ps[:, 7, j * 16:(j + 1) * 16], g.h[:, k, j * P:(j + 1) * P], wdt[:, k, :], start=(k == 0), stop=(k == KT - 1))
                mm.then_inc(dt_product, 1)
                for u, (t, a, n) in enumerate(units):
                    if u % C == 0:
                        pe.wait_ge(w_in[t % 3], 16 * (t // 3 + 1))
                    if u >= BANKS:
                        pe.wait_ge(raw_out, u - BANKS + 1)
                    for k in range(KT):
                        mm = pe.matmul(g.ps[:, u % BANKS, 0:n], ring[:, t % 3, k, :], g.h[:, k, a:a + n], start=(k == 0), stop=(k == KT - 1))
                    mm.then_inc(product, 1)
                pe.wait_ge(w_z, 16)
                for u, (t, a, n) in enumerate(zunits):
                    if u >= 2:
                        pe.wait_ge(z_out, u - 1)
                    for k in range(KT):
                        mm = pe.matmul(g.ps[:, 4 + u % 2, 0:n], wz[:, t, k, :], g.h[:, k, a:a + n], start=(k == 0), stop=(k == KT - 1))
                    mm.then_inc(z_product, 1)

            @block.scalar
            def _(act):
                act.wait_ge(steps, 1)
                act.activation(mag[:], dt[:], ACT.Abs).then_inc(magnitude, 1)
                act.wait_ge(magnitude, 1)
                act.activation(ex[:], mag[:], ACT.Exp, scale=-1.0).then_inc(decayed, 1)
                act.activation(rate[:], vec(g, "a_log", 0, 16), ACT.Exp).then_inc(a_exp, 1)
                act.wait_ge(steps, 2)
                act.activation(lg[:], one_e[:], ACT.Ln).then_inc(logged, 1)
                act.wait_ge(padded, 1)
                for u, (t, a, n) in enumerate(units):
                    act.wait_ge(product, u + 1)
                    if t >= 2 and u % C == 0:
                        act.wait_ge(conv, t - 1)
                    at = LAT_AT + a if a < LAT else CTX_AT + a - LAT
                    act.activation(raw[:, t % 2, at:at + n], g.ps[:, u % BANKS, 0:n], ACT.Copy).then_inc(raw_out, 1)
                    if u % C == C - 1 and t >= 1:
                        silu_conv(act, t - 1)
                silu_conv(act, TILES - 1)
                for u, (t, a, n) in enumerate(zunits):
                    act.wait_ge(z_product, u + 1)
                    act.activation(gate[:, t, a:a + n], g.ps[:, 4 + u % 2, 0:n], ACT.Silu).then_inc(z_out, 1)

            @block.vector
            def _(dve):
                dve.memset(raw[:], 0.0).then_inc(padded, 1)
                dve.wait_ge(dt_product, 1)
                dps = g.ps[:, 7, 0:160].rearrange("p (j c) -> p j c", c=16)
                dve.tensor_tensor(dt[:], dps, over_tiles(vec(g, "dt_bias", 0, 16)), ALU.add).then_inc(steps, 1)
                dve.wait_ge(decayed, 1)
                dve.tensor_scalar(one_e[:], ex[:], 1.0, None, ALU.add).then_inc(steps, 1)
                dve.wait_ge(steps, 2)
                dve.tensor_scalar(zero[:], one_e[:], 1.0, None, ALU.is_equal).then_inc(steps, 1)
                dve.wait_ge(steps, 3)
                dve.scalar_tensor_tensor(out=den[:], in0=one_e[:], scalar=-1.0, in1=zero[:], op0=ALU.add, op1=ALU.add).then_inc(steps, 1)
                dve.wait_ge(steps, 4)
                dve.reciprocal(den[:], den[:]).then_inc(steps, 1)
                dve.wait_ge(logged, 1)
                dve.tensor_tensor(lg[:], lg[:], zero[:], ALU.add).then_inc(steps, 1)
                dve.wait_ge(steps, 6)
                dve.tensor_tensor(lg[:], lg[:], den[:], ALU.mult).then_inc(steps, 1)
                dve.wait_ge(steps, 7)
                dve.tensor_tensor(lg[:], lg[:], ex[:], ALU.mult).then_inc(steps, 1)
                dve.wait_ge(steps, 8)
                dve.scalar_tensor_tensor(out=dt[:], in0=dt[:], scalar=0.0, in1=lg[:], op0=ALU.max, op1=ALU.add).then_inc(steps, 1)
                dve.wait_ge(a_exp, 1)
                dve.tensor_scalar(rate[:], rate[:], -1.0, None, ALU.mult).then_inc(steps, 1)
                dve.wait_ge(steps, 10)
                dve.tensor_tensor(adt[:], dt[:], over_tiles(rate[:]), ALU.mult).then_inc(steps, 1)
                made = 11
                for t in range(TILES):
                    dve.wait_ge(raw_out, C * (t + 1))
                    if t >= 2:
                        dve.wait_ge(conv_read, 2 * (t - 1))
                    out, n = acc[:, t % 2, 1:WIDE - 1], WIDE - 2
                    tap = lambda i: vec(g, "conv_w", i * TILES + t)
                    dve.tensor_scalar(out, raw[:, t % 2, 0:n], tap(0), None, ALU.mult).then_inc(steps, 1)
                    dve.wait_ge(steps, made + 1)
                    dve.scalar_tensor_tensor(out=out, in0=raw[:, t % 2, 1:1 + n], scalar=tap(1), in1=out, op0=ALU.mult, op1=ALU.add).then_inc(steps, 1)
                    dve.wait_ge(steps, made + 2)
                    made += 2
                    dve.scalar_tensor_tensor(out=out, in0=raw[:, t % 2, 2:2 + n], scalar=tap(2), in1=out, op0=ALU.mult, op1=ALU.add).then_inc(conv, 1)


def scan_states(nc, g, d, xbc, gate, dt, adt, out):
    CH, H, HD, G = P, 8, 64, 2
    LATC, NC = LAT // CH, TOK // CH
    fwd = list(range(LATC, NC)) + list(range(LATC))
    bwd = list(range(NC - 1, LATC - 1, -1)) + list(range(LATC - 1, -1, -1))
    units = [(dr, c) for pair in zip(fwd, bwd) for dr, c in enumerate(pair)]
    U = len(units)
    ys = [u for u, (dr, c) in enumerate(units) if c < LATC]
    Y = {u: i for i, u in enumerate(ys)}
    first_y = {}
    for u in ys:
        first_y.setdefault(units[u][1], u)

    xt = tile(nc, out.mem, "x_tokens", [P, NC, H * HD])
    bt = tile(nc, out.mem, "b_tokens", [P, NC, G * P])
    tri = tile(nc, out.mem, "triangles", [P, 2, P])
    with stage(nc, "tri_in turned read_out") as (mem, (tri_in, turned, read_out)):
        jobs = [(c, kind) for c in range(NC) for kind in range(2)]
        with nc.Block() as block:
            @block.sync
            def _(sp):
                sp.dma_start(tri[:], d["triangles"]).then_inc(tri_in, 16)
                sp.wait_ge(tri_in, 16)

            @block.tensor
            def _(pe):
                for i, (c, kind) in enumerate(jobs):
                    if i >= 4:
                        pe.wait_ge(read_out, i - 3)
                    for t in range(4 if kind == 0 else 2):
                        mm = pe.transpose(g.ps[:, i % 4, t * P:(t + 1) * P], xbc[:, 4 * kind + t, c * CH:(c + 1) * CH], g.ident[:])
                    mm.then_inc(turned, 1)

            @block.scalar
            def _(act):
                for i, (c, kind) in enumerate(jobs):
                    act.wait_ge(turned, i + 1)
                    dst = xt[:, c, :] if kind == 0 else bt[:, c, :]
                    act.activation(dst, g.ps[:, i % 4, 0:dst.shape[1]], ACT.Copy).then_inc(read_out, 1)

    names = ("spread sums acs_out act_read last_made seg_made decay_done clamped seg_exp decay_dt weighted x_dt c_scaled gram "
             "masked attended state_product kept state y_product y_out cleared")
    with stage(nc, names) as (mem, sems):
        (spread, sums, acs_out, act_read, last_made, seg_made, decay_done, clamped, seg_exp, decay_dt, weighted, x_dt,
         c_scaled, gram, masked, attended, state_product, kept, state, y_product, y_out, cleared) = sems
        HL = [P, H, CH]
        HX = [P, H, HD]
        au = tile(nc, mem, "adt_spread", [P, 2, H, CH])
        acs = tile(nc, mem, "acs_source", [P, 2, H])
        last = tile(nc, mem, "acs_left", [P, 2, H])
        dec = tile(nc, mem, "decay_source", [P, 2, H])
        whole = tile(nc, mem, "decay_chunk", [P, 2, H])
        xw = tile(nc, mem, "x_weighted", [P, 2, H, HD])
        xd = tile(nc, mem, "x_dt", [P, 2, H, HD])
        seg = tile(nc, mem, "segments", [P, 2, H, CH])
        ea = tile(nc, mem, "exp_acs", [P, 2, H, CH])
        gm = tile(nc, mem, "gram_masked", [P, 2, G, CH])
        st = tile(nc, mem, "states", [P, 2, 2, H, HD])
        tmp = tile(nc, mem, "state_kept", [P, H, HD])
        y = out.y
        acs_ps = g.ps[:, 0:2, :].rearrange("p b (h l) -> p (b h) l", l=CH)
        by_head = lambda ap, shape: ap.unsqueeze(2).to_broadcast(shape)
        ny = lambda u: sum(1 for v in ys if v < u)
        with nc.Block() as block:
            def y_read(dve, i):
                c = units[ys[i]][1]
                dve.wait_ge(y_product, i + 1)
                src = g.ps[:, 5 + i % 2, :].rearrange("p (t l) -> p t l", l=CH)
                dst = y[:, :, c * CH:(c + 1) * CH]
                if first_y[c] == ys[i]:
                    dve.tensor_copy(dst, src).then_inc(y_out, 1)
                else:
                    dve.wait_ge(y_out, Y[first_y[c]] + 1)
                    dve.tensor_tensor(dst, dst, src, ALU.add).then_inc(y_out, 1)

            @block.tensor
            def _(pe):
                def running_sums(u):
                    dr, c = units[u]
                    pe.wait_ge(spread, u + 1)
                    if u >= 1:
                        pe.wait_ge(act_read, u)
                        pe.wait_ge(last_made, u)
                        if ny(u):
                            pe.wait_ge(seg_made, ny(u))
                    for b in range(2):
                        pe.matmul(g.ps[:, b, :], g.ones[:], au[:, u % 2, 4 * b:4 * b + 4, :].rearrange("p h l -> p (h l)"), start=True, stop=True)
                    pe.matmul(g.ps[:, 2, 0:H], tri[:, dr, :], adt[:, c, 8 * dr:8 * dr + 8], start=True, stop=True).then_inc(sums, 1)

                running_sums(0)
                for u, (dr, c) in enumerate(units):
                    tok = slice(c * CH, (c + 1) * CH)
                    if u in Y:
                        i = Y[u]
                        if i >= 1:
                            pe.wait_ge(masked, i)
                        for grp in range(G):
                            mm = pe.matmul(g.ps[:, 4, grp * CH:(grp + 1) * CH], xbc[:, 4 + grp, tok], xbc[:, 6 + grp, tok], start=True, stop=True)
                        mm.then_inc(gram, 1)
                    pe.wait_ge(weighted, u + 1)
                    if u >= 1:
                        pe.wait_ge(state, u)
                    for grp in range(G):
                        mm = pe.matmul(g.ps[:, 3, grp * 256:(grp + 1) * 256], bt[:, c, grp * P:(grp + 1) * P],
                                       xw[:, u % 2, 4 * grp:4 * grp + 4, :].rearrange("p h x -> p (h x)"), start=True, stop=True)
                    mm.then_inc(state_product, 1)
                    if u + 1 < U:
                        running_sums(u + 1)
                    if u in Y:
                        i = Y[u]
                        pe.wait_ge(attended, i + 1)
                        pe.wait_ge(c_scaled, i + 1)
                        pe.wait_ge(x_dt, i + 1)
                        if i >= 2:
                            pe.wait_ge(y_out, i - 1)
                        for h in range(H):
                            dst = g.ps[64 * (h % 2):64 * (h % 2) + 64, 5 + i % 2, (h // 2) * CH:(h // 2 + 1) * CH]
                            pe.matmul(dst, xd[:, i % 2, h, :], seg[:, i % 2, h, :], start=True, stop=False)
                            mm = pe.matmul(dst, st[:, dr, (u // 2) % 2, h, :], ea[:, i % 2, h, :], start=False, stop=True)
                        mm.then_inc(y_product, 1)

            @block.scalar
            def _(act):
                for u, (dr, c) in enumerate(units):
                    end = CH - 1 if dr == 0 else 0
                    act.wait_ge(sums, u + 1)
                    if u >= 2:
                        act.wait_ge(last_made, u - 1)
                        if ny(u - 1):
                            act.wait_ge(seg_made, ny(u - 1))
                        act.wait_ge(kept, u - 1)
                    act.activation(acs[:, u % 2, :], g.ps[:, 2, 0:H], ACT.Copy).then_inc(acs_out, 1)
                    done = act.activation(whole[:, u % 2, :], acs_ps[:, :, end], ACT.Exp)
                    if u in Y:
                        i = Y[u]
                        if i >= 2:
                            act.wait_ge(y_product, i - 1)
                        done = act.activation(ea[:, i % 2], acs_ps, ACT.Exp)
                    done.then_inc(act_read, 1)
                    act.wait_ge(last_made, u + 1)
                    if u >= 2:
                        act.wait_ge(weighted, u - 1)
                    act.activation(dec[:, u % 2, :], last[:, u % 2, :], ACT.Exp).then_inc(decay_done, 1)
                    if u in Y:
                        act.wait_ge(clamped, i + 1)
                        act.activation(seg[:, i % 2], seg[:, i % 2], ACT.Exp).then_inc(seg_exp, 1)

            @block.vector
            def _(dve):
                def spread_adt(u):
                    dr, c = units[u]
                    if u >= 2:
                        dve.wait_ge(sums, u - 1)
                    dve.tensor_tensor(au[:, u % 2], tri[:, dr, :].unsqueeze(1).to_broadcast(HL),
                                      by_head(adt[:, c, 8 * dr:8 * dr + 8], HL), ALU.mult).then_inc(spread, 1)

                spread_adt(0)
                dve.memset(st[:], 0.0).then_inc(cleared, 1)
                dve.wait_ge(cleared, 1)
                for u, (dr, c) in enumerate(units):
                    end = CH - 1 if dr == 0 else 0
                    tok = slice(c * CH, (c + 1) * CH)
                    if u + 1 < U:
                        spread_adt(u + 1)
                    dve.wait_ge(acs_out, u + 1)
                    dve.wait_ge(act_read, u + 1)
                    if u >= 2:
                        dve.wait_ge(decay_done, u - 1)
                    dve.tensor_tensor(last[:, u % 2, :], acs_ps[:, :, end], acs[:, u % 2, :], ALU.subtract).then_inc(last_made, 1)
                    if u in Y:
                        i = Y[u]
                        if i >= 2:
                            dve.wait_ge(y_product, i - 1)
                        dve.tensor_tensor(seg[:, i % 2], acs_ps, by_head(acs[:, u % 2, :], HL), ALU.subtract).then_inc(seg_made, 1)
                        dve.wait_ge(seg_made, i + 1)
                        dve.tensor_scalar(seg[:, i % 2], seg[:, i % 2], 0.0, None, ALU.min).then_inc(clamped, 1)
                    dve.wait_ge(decay_done, u + 1)
                    dve.tensor_tensor(dec[:, u % 2, :], dec[:, u % 2, :], dt[:, c, 8 * dr:8 * dr + 8], ALU.mult).then_inc(decay_dt, 1)
                    dve.wait_ge(decay_dt, u + 1)
                    if u >= 2:
                        dve.wait_ge(state_product, u - 1)
                    xh = xt[:, c, :].rearrange("p (h x) -> p h x", x=HD)
                    dve.tensor_tensor(xw[:, u % 2], xh, by_head(dec[:, u % 2, :], HX), ALU.mult).then_inc(weighted, 1)
                    if u in Y:
                        dve.tensor_tensor(xd[:, i % 2], xh, by_head(dt[:, c, 8 * dr:8 * dr + 8], HX), ALU.mult).then_inc(x_dt, 1)
                        dve.wait_ge(act_read, u + 1)
                        grouped = [P, G, H // G, CH]
                        ea4 = ea[:, i % 2].rearrange("p (g e) l -> p g e l", g=G)
                        dve.tensor_tensor(ea4, ea4, by_head(xbc[:, 6:8, tok], grouped), ALU.mult).then_inc(c_scaled, 1)
                        dve.wait_ge(gram, i + 1)
                        g2 = g.ps[:, 4, 0:G * CH].rearrange("p (g l) -> p g l", g=G)
                        dve.tensor_tensor(gm[:, i % 2], g2, tri[:, dr, :].unsqueeze(1).to_broadcast([P, G, CH]), ALU.mult).then_inc(masked, 1)
                        dve.wait_ge(masked, i + 1)
                        dve.wait_ge(seg_exp, i + 1)
                        s4 = seg[:, i % 2].rearrange("p (g e) l -> p g e l", g=G)
                        dve.tensor_tensor(s4, s4, by_head(gm[:, i % 2], grouped), ALU.mult).then_inc(attended, 1)
                    dve.wait_ge(act_read, u + 1)
                    if u >= 2:
                        dve.wait_ge(state, u - 1)
                    old, new = st[:, dr, (u // 2) % 2], st[:, dr, (u // 2 + 1) % 2]
                    dve.tensor_tensor(tmp[:], old, by_head(whole[:, u % 2, :], HX), ALU.mult).then_inc(kept, 1)
                    dve.wait_ge(kept, u + 1)
                    dve.wait_ge(state_product, u + 1)
                    if u - 2 in Y:
                        dve.wait_ge(y_product, Y[u - 2] + 1)
                    dve.tensor_tensor(new, tmp[:], g.ps[:, 3, :].rearrange("p (h x) -> p h x", x=HD), ALU.add).then_inc(state, 1)
                    if u in Y and i >= 1:
                        y_read(dve, i - 1)
                y_read(dve, len(ys) - 1)


def gate_norm(nc, g, xbc, gate, y, out):
    T = 4
    with stage(nc, "skipped gated squared square_used logged rstd normed") as (mem, (skipped, gated, squared, square_used, logged, rstd, normed)):
        sq = tile(nc, mem, "norm_sq", [P, 2, LAT])
        rs = tile(nc, mem, "norm_rs", [P, LAT])
        total = g.ps[:, 0:2, :].rearrange("p b n -> p (b n)")
        with nc.Block() as block:
            @block.vector
            def _(dve):
                for t in range(T):
                    dve.scalar_tensor_tensor(out=y[:, t, :], in0=xbc[:, t, 0:LAT], scalar=vec(g, "d_skip", t), in1=y[:, t, :], op0=ALU.mult, op1=ALU.add).then_inc(skipped, 1)
                    dve.wait_ge(skipped, t + 1)
                    dve.tensor_tensor(y[:, t, :], y[:, t, :], gate[:, t, :], ALU.mult).then_inc(gated, 1)
                dve.wait_ge(rstd, 1)
                for t in range(T):
                    dve.scalar_tensor_tensor(out=out[:, t, 0:LAT], in0=y[:, t, :], scalar=vec(g, "mb_norm", t), in1=rs[:], op0=ALU.mult, op1=ALU.mult).then_inc(normed, 1)

            @block.scalar
            def _(act):
                for t in range(T):
                    act.wait_ge(gated, t + 1)
                    if t >= 2:
                        act.wait_ge(square_used, t - 1)
                    act.activation(sq[:, t % 2, :], y[:, t, :], ACT.Square).then_inc(squared, 1)
                act.wait_ge(square_used, T)
                act.activation(rs[:], total, ACT.Ln, bias=g.eps[:], scale=1.0 / (T * P)).then_inc(logged, 1)
                act.wait_ge(logged, 1)
                act.activation(rs[:], rs[:], ACT.Exp, scale=-0.5).then_inc(rstd, 1)

            @block.tensor
            def _(pe):
                for t in range(T):
                    pe.wait_ge(squared, t + 1)
                    for a, n in CHUNKS[:2]:
                        mm = pe.matmul(total[:, a:a + n], g.ones[:], sq[:, t % 2, a:a + n], start=(t == 0), stop=(t == T - 1))
                    mm.then_inc(square_used, 1)


FOLD = LAT // 2
FT = FOLD // P
W_HY = 512
PARTS = [("cos_even", "sum", True), ("sin_even", "diff", False), ("cos_odd", "diff", False), ("sin_odd", "sum", True)]
PI2_A, PI2_B = 6.28125, 0.0019350051879882812
PI2_C = 2 * math.pi - PI2_A - PI2_B
ROUND = 1.5 * 2 ** 23
BELOW_PI = 3.1415925


def hyena_spectra(nc, g, d, spectra):
    ORD = 2
    HID = 64
    with stage(nc, "loaded product biased reduced sines flipped zeroed") as (mem, (loaded, product, biased, reduced, sines, flipped, zeroed)):
        w1, w2 = tile(nc, mem, "hy_w1", [P, HID]), tile(nc, mem, "hy_w2", [P, HID])
        zt = tile(nc, mem, "positions", [P, LAT])
        h1 = tile(nc, mem, "hy_h1", [P, LAT])
        ang, turns = tile(nc, mem, "angles", [P, LAT]), tile(nc, mem, "turns", [P, LAT])
        h2, h2r, h2b = spectra.h2, spectra.h2r, spectra.h2b
        rows = slice(0, HID)
        with nc.Block() as block:
            @block.sync
            def _(sp):
                sp.dma_start(w1[0:33, :], d["hy_w1"]).then_inc(loaded, 16)
                sp.dma_start(w2[rows, :], d["hy_w2"]).then_inc(loaded, 16)
                sp.dma_start(zt[0:33, :], d["positions"]).then_inc(loaded, 16)

            @block.tensor
            def _(pe):
                pe.wait_ge(loaded, 48)
                for layer in range(2):
                    for c in range(2):
                        if layer:
                            pe.wait_ge(sines, 1)
                        w, src, kk = ((w1, zt, 33), (w2, h1, HID))[layer]
                        mm = pe.matmul(g.ps[rows, 2 * layer + c, :], w[0:kk, :], src[0:kk, c * BANK:(c + 1) * BANK], start=True, stop=True)
                    mm.then_inc(product, 1)

            @block.vector
            def _(dve):
                dve.memset(h2[rows, LAT:LAT + 1], 0.0).then_inc(zeroed, 1)
                n = 0
                for layer in range(2):
                    dve.wait_ge(product, layer + 1)
                    flat = g.ps[rows, 2 * layer:2 * layer + 2, :].rearrange("p b n -> p (b n)")
                    a, k = ang[rows, :], turns[rows, :]
                    b = vec(g, ("hy_b1", "hy_b2")[layer])[rows, :]
                    dve.tensor_scalar(a, flat, b, vec(g, "freq")[rows, :], ALU.add, ALU.mult).then_inc(biased, 1)
                    dve.wait_ge(biased, layer + 1)
                    dve.tensor_scalar(k, a, 1 / (2 * math.pi), ROUND, ALU.mult, ALU.add).then_inc(reduced, 1)
                    dve.wait_ge(reduced, n + 1)
                    dve.tensor_scalar(k, k, -ROUND, None, ALU.add).then_inc(reduced, 1)
                    dve.wait_ge(reduced, n + 2)
                    for j, part in enumerate((PI2_A, PI2_B, PI2_C)):
                        dve.scalar_tensor_tensor(out=a, in0=k, scalar=-part, in1=a, op0=ALU.mult, op1=ALU.add).then_inc(reduced, 1)
                        dve.wait_ge(reduced, n + 3 + j)
                    dve.tensor_scalar(a, a, BELOW_PI, -BELOW_PI, ALU.min, ALU.max).then_inc(reduced, 1)
                    n += 6
                dve.wait_ge(sines, 2)
                dve.wait_ge(zeroed, 1)
                dve.tensor_copy(h2r[rows, :], h2[rows, LAT:LAT - FOLD:-1]).then_inc(flipped, 1)
                dve.tensor_copy(h2b[rows, :], h2[rows, 0:P]).then_inc(flipped, 1)
                dve.wait_ge(flipped, 2)
                dve.memset(h2b[rows, 0:1], 0.0).then_inc(flipped, 1)

            @block.scalar
            def _(act):
                for layer in range(2):
                    act.wait_ge(reduced, 6 * (layer + 1))
                    act.activation((h1, h2)[layer][rows, 0:LAT], ang[rows, :], ACT.Sin).then_inc(sines, 1)

    names = "loaded taps row_taps weighed row_weighed paired row_paired folded product read_out first_halved halved stored0 stored1 stored2"
    with stage(nc, names) as (mem, sems):
        loaded, taps, row_taps, weighed, row_weighed, paired, row_paired, folded, product, read_out, first_halved, halved = sems[:12]
        stored = sems[12:]
        w3 = tile(nc, mem, "hy_w3", [P, ORD * 2 * W_HY])
        dec = tile(nc, mem, "decay", [P, 2, FT, W_HY])
        dec_row = tile(nc, mem, "decay_middle", [1, W_HY])
        tabs = tile(nc, mem, "dft", [P, 4, FT, FOLD])
        alt_row, alt_col = spectra.alt_row, spectra.alt_col
        four = tile(nc, mem, "taps_weighed", [P, 4, W_HY])
        two = tile(nc, mem, "taps_paired", [P, 4, W_HY])
        pm = tile(nc, mem, "taps_folded", [P, 4, ORD, FT, W_HY])
        mid = tile(nc, mem, "taps_middle", [1, 2, W_HY])
        mid_sum = tile(nc, mem, "taps_middle_paired", [1, ORD, 2, W_HY])
        sp_out = tile(nc, mem, "spectrum_out", [P, 3, W_HY])
        SRC = {"cos_even": 0, "cos_odd": 1, "sin_odd": 2, "sin_even": 3}
        units = [(o, i, q) for o in range(ORD) for i in range(FT) for q in range(4)]
        per_order = 4 * FT + 1
        rows = slice(0, 64)
        with nc.Block() as block:
            @block.sync
            def _(sp):
                for dst, src in ((w3[rows, :], d["hy_w3"]), (dec[:], d["decay"]), (dec_row[:], d["decay_middle"]), (tabs[:], d["dft"]),
                                 (alt_row[:], d["alt_row"]), (alt_col[:], d["alt_col"])):
                    sp.dma_start(dst, src).then_inc(loaded, 16)
                for o in range(ORD):
                    for n in range(per_order):
                        e = o * per_order + n
                        sp.wait_ge(halved, o + 1) if n == 0 else sp.wait_ge(read_out, e + 1)
                        if n < 4 * FT:
                            i, q = divmod(n, 4)
                            parity, kind = q // 2, q % 2
                            sp.dma_start(spectra.h[o, parity * 8 + kind * 4 + i], sp_out[:, e % 3, :]).then_inc(stored[e % 3], 16)
                        else:
                            sp.dma_start(spectra.last[o:o + 1], sp_out[0:1, e % 3, :]).then_inc(stored[e % 3], 16)
                E = ORD * per_order
                for s in range(3):
                    sp.wait_ge(stored[s], 16 * len(range(s, E, 3)))

            @block.tensor
            def _(pe):
                pe.wait_ge(loaded, 96)

                def tap_products(o, jt):
                    q = o * FT + jt
                    if q:
                        pe.wait_ge(weighed, 4 * q)
                    f, b = w3[rows, (2 * o) * W_HY:(2 * o + 1) * W_HY], w3[rows, (2 * o + 1) * W_HY:(2 * o + 2) * W_HY]
                    js = slice(jt * P, (jt + 1) * P)
                    pe.matmul(g.ps[:, 0, :], h2[rows, js], f, start=True, stop=True)
                    pe.matmul(g.ps[:, 1, :], h2b[rows, :] if jt == 0 else h2[rows, js], b, start=True, stop=True)
                    pe.matmul(g.ps[:, 2, :], h2r[rows, js], f, start=True, stop=True)
                    pe.matmul(g.ps[:, 3, :], h2r[rows, js], b, start=True, stop=True).then_inc(taps, 1)

                def middle_products(o):
                    for n in range(2):
                        if 2 * o + n:
                            pe.wait_ge(row_weighed, 2 * o + n)
                        pe.matmul(g.ps[0:1, 4, :], h2[rows, FOLD:FOLD + 1], w3[rows, (2 * o + n) * W_HY:(2 * o + n + 1) * W_HY],
                                  start=True, stop=True).then_inc(row_taps, 1)

                def spectrum(o, n):
                    e = o * per_order + n
                    if e >= 3:
                        pe.wait_ge(read_out, e - 2)
                    if n == 0:
                        pe.wait_ge(folded, 4 * FT * (o + 1))
                        pe.wait_ge(row_paired, 2 * (o + 1))
                    bank = 5 + e % 3
                    if n < 4 * FT:
                        i, q = divmod(n, 4)
                        part, fold, middle = PARTS[q]
                        for jt in range(FT):
                            mm = pe.matmul(g.ps[:, bank, :], tabs[:, q, jt, i * P:(i + 1) * P], pm[:, SRC[part], o, jt, :], start=(jt == 0), stop=(jt == FT - 1 and not middle))
                        if middle:
                            mm = pe.matmul(g.ps[:, bank, :], alt_row[:, 0:P], mid_sum[:, o, 0 if part == "cos_even" else 1, :], start=False, stop=True)
                    else:
                        for jt in range(FT):
                            pe.matmul(g.ps[0:1, bank, :], alt_col[:], pm[:, 0, o, jt, :], start=(jt == 0), stop=False)
                        mm = pe.matmul(g.ps[0:1, bank, :], alt_row[:, 0:1], mid_sum[:, o, 0, :], start=False, stop=True)
                    mm.then_inc(product, 1)

                for jt in range(FT):
                    tap_products(0, jt)
                middle_products(0)
                for n in range(per_order):
                    if n % 4 == 0 and n // 4 < FT:
                        tap_products(1, n // 4)
                    spectrum(0, n)
                middle_products(1)
                for n in range(per_order):
                    spectrum(1, n)

            @block.scalar
            def _(act):
                for e in range(ORD * per_order):
                    o, n = divmod(e, per_order)
                    act.wait_ge(product, e + 1)
                    if e >= 3:
                        act.wait_ge(stored[e % 3], 16 * (e // 3))
                    if n < 4 * FT:
                        act.activation(sp_out[:, e % 3, :], g.ps[:, 5 + e % 3, :], ACT.Copy, scale=1.0 / LAT).then_inc(read_out, 1)
                        if n == 0:
                            act.wait_ge(read_out, e + 1)
                            act.activation(sp_out[0:1, e % 3, :], sp_out[0:1, e % 3, :], ACT.Copy, scale=0.5).then_inc(halved, 1)
                    else:
                        act.activation(sp_out[0:1, e % 3, :], g.ps[0:1, 5 + e % 3, :], ACT.Copy, scale=0.5 / LAT).then_inc(read_out, 1)

            @block.vector
            def _(dve):
                dve.wait_ge(loaded, 96)
                for o in range(ORD):
                    for jt in range(FT):
                        q = o * FT + jt
                        dve.wait_ge(taps, q + 1)
                        if q:
                            dve.wait_ge(paired, 4 * q)
                            dve.wait_ge(folded, 4 * q)
                        for n in range(4):
                            dve.tensor_tensor(four[:, n, :], g.ps[:, n, :], dec[:, n // 2, jt, :], ALU.mult).then_inc(weighed, 1)
                        dve.wait_ge(weighed, 4 * (q + 1))
                        for n, (x, op) in enumerate(((0, ALU.add), (2, ALU.add), (0, ALU.subtract), (2, ALU.subtract))):
                            dve.tensor_tensor(two[:, n, :], four[:, x, :], four[:, x + 1, :], op).then_inc(paired, 1)
                        dve.wait_ge(paired, 4 * (q + 1))
                        for n, (x, op) in enumerate(((0, ALU.add), (0, ALU.subtract), (2, ALU.add), (2, ALU.subtract))):
                            dve.tensor_tensor(pm[:, n, o, jt, :], two[:, x, :], two[:, x + 1, :], op).then_inc(folded, 1)
                    for n in range(2):
                        dve.wait_ge(row_taps, 2 * o + n + 1)
                        if o and n == 0:
                            dve.wait_ge(row_paired, 2 * o)
                        dve.tensor_tensor(mid[:, n, :], g.ps[0:1, 4, :], dec_row[:], ALU.mult).then_inc(row_weighed, 1)
                    dve.wait_ge(row_weighed, 2 * (o + 1))
                    dve.tensor_tensor(mid_sum[:, o, 0, :], mid[:, 0, :], mid[:, 1, :], ALU.add).then_inc(row_paired, 1)
                    dve.tensor_tensor(mid_sum[:, o, 1, :], mid[:, 0, :], mid[:, 1, :], ALU.subtract).then_inc(row_paired, 1)


def project_hyena(nc, g, d, u3):
    TILES, BANKS = 12, 8
    units = [(t, a, n) for t in range(TILES) for a, n in CHUNKS[:2]]
    C = 2
    with stage(nc, "w_in0 w_in1 w_in2 product raw_out padded steps conv stored0 stored1") as (mem, sems):
        w_in, (product, raw_out, padded, steps, conv), stored = sems[:3], sems[3:8], sems[8:]
        ring = tile(nc, mem, "w_hy", [P, 3, KT, P])
        raw = tile(nc, mem, "hy_raw", [P, 2, LAT + 2])
        res = tile(nc, mem, "hy_conv", [P, 2, LAT])
        with nc.Block() as block:
            @block.sync
            def _(sp):
                for t in range(TILES + 3):
                    if t < TILES:
                        if t >= 3:
                            sp.wait_ge(product, C * (t - 2))
                        sp.dma_start(ring[:, t % 3], d["w_hy"][t]).then_inc(w_in[t % 3], 16)
                    if t >= 3:
                        v = t - 3
                        sp.wait_ge(conv, v + 1)
                        sp.dma_start(u3[:, v, :], res[:, v % 2, :]).then_inc(stored[v % 2], 16)
                for s in range(2):
                    sp.wait_ge(stored[s], 16 * (TILES // 2))

            @block.tensor
            def _(pe):
                for u, (t, a, n) in enumerate(units):
                    if u % C == 0:
                        pe.wait_ge(w_in[t % 3], 16 * (t // 3 + 1))
                    if u >= BANKS:
                        pe.wait_ge(raw_out, u - BANKS + 1)
                    for k in range(KT):
                        mm = pe.matmul(g.ps[:, u % BANKS, 0:n], ring[:, t % 3, k, :], g.h[:, k, a:a + n], start=(k == 0), stop=(k == KT - 1))
                    mm.then_inc(product, 1)

            @block.scalar
            def _(act):
                act.wait_ge(padded, 1)
                for u, (t, a, n) in enumerate(units):
                    act.wait_ge(product, u + 1)
                    if t >= 2 and u % C == 0:
                        act.wait_ge(conv, t - 1)
                    act.activation(raw[:, t % 2, 1 + a:1 + a + n], g.ps[:, u % BANKS, 0:n], ACT.Copy).then_inc(raw_out, 1)

            @block.vector
            def _(dve):
                dve.memset(raw[:], 0.0).then_inc(padded, 1)
                for t in range(TILES):
                    dve.wait_ge(raw_out, C * (t + 1))
                    if t >= 2:
                        dve.wait_ge(stored[t % 2], 16 * (t // 2))
                    tap = lambda i: vec(g, "short_w", i * TILES + t)
                    dve.tensor_scalar(res[:, t % 2, :], raw[:, t % 2, 0:LAT], tap(0), vec(g, "short_b", t), ALU.mult, ALU.add).then_inc(steps, 1)
                    dve.wait_ge(steps, 2 * t + 1)
                    dve.scalar_tensor_tensor(out=res[:, t % 2, :], in0=raw[:, t % 2, 1:1 + LAT], scalar=tap(1), in1=res[:, t % 2, :], op0=ALU.mult, op1=ALU.add).then_inc(steps, 1)
                    dve.wait_ge(steps, 2 * t + 2)
                    dve.scalar_tensor_tensor(out=res[:, t % 2, :], in0=raw[:, t % 2, 2:2 + LAT], scalar=tap(2), in1=res[:, t % 2, :], op0=ALU.mult, op1=ALU.add).then_inc(conv, 1)


def long_convs(nc, g, d, spectra, u3_src, u3):
    ORD, CT = 2, W_HY // P
    names = ("tabs_in u3_in0 u3_in1 u3_in2 h_in0 h_in1 h_in2 last_in folded first_copied turned turned_out mid_turned mid_out product mult combined last_made "
             "inverse sym_out times mirrored middle skipped gated")
    with stage(nc, names) as (mem, sems):
        (tabs_in, u3_in0, u3_in1, u3_in2, h_in0, h_in1, h_in2, last_in, folded, first_copied, turned, turned_out, mid_turned, mid_out, product, mult, combined, last_made,
         inverse, sym_out, times, mirrored, middle, skipped, gated) = sems
        u3_in, h_in = (u3_in0, u3_in1, u3_in2), (h_in0, h_in1, h_in2)
        tabs = tile(nc, mem, "dft", [P, 4, FT, FOLD])
        back = tile(nc, mem, "dft_back", [P, 2, FT, FOLD])
        alt_row, alt_col = spectra.alt_row, spectra.alt_col
        fold = tile(nc, mem, "folded", [P, 2, CT, FOLD])
        tim = tile(nc, mem, "folded_turned", [P, 2, FT, W_HY])
        mid = tile(nc, mem, "middle_time", [1, W_HY])
        h = tile(nc, mem, "filter_ring", [P, 3, 2, W_HY])
        hl = tile(nc, mem, "filter_last", [1, W_HY])
        yv = tile(nc, mem, "output_spectrum", [P, 4, FT, W_HY])
        yl = tile(nc, mem, "output_last", [1, W_HY])
        pr = tile(nc, mem, "products", [P, 4, W_HY])
        sym = tile(nc, mem, "symmetric", [P, 2, FOLD + 1])
        tm = tile(nc, mem, "convolved", [P, 2, LAT])
        z = u3
        with nc.Block() as block:
            @block.sync
            def _(sp):
                sp.dma_start(u3[:, 0:CT, :], u3_src[:, 0:CT, :]).then_inc(u3_in[0], 16)
                for dst, src in ((tabs, "dft"), (back, "dft_back")):
                    sp.dma_start(dst[:], d[src]).then_inc(tabs_in, 16)
                for o in range(ORD):
                    if o:
                        sp.wait_ge(last_made, 1)
                    sp.dma_start(hl[:], spectra.last[o:o + 1]).then_inc(last_in, 16)
                    filters = spectra.h[o].rearrange("(q k i) p n -> q i p k n", q=2, k=2)
                    for n in range(2 * FT):
                        w = o * 2 * FT + n
                        if w >= 3:
                            sp.wait_ge(mult, 4 * (w - 2))
                        sp.dma_start(h[:, w % 3], filters[n // FT, n % FT]).then_inc(h_in[w % 3], 16)
                        if w in (3, 4):
                            sp.dma_start(u3[:, CT * (w - 2):CT * (w - 1), :], u3_src[:, CT * (w - 2):CT * (w - 1), :]).then_inc(u3_in[w - 2], 16)

            @block.tensor
            def _(pe):
                pe.wait_ge(tabs_in, 32)
                n_turn = 0
                for o in range(ORD):
                    for s in range(2):
                        for jt in range(FT):
                            pe.wait_ge(folded, 2 * CT * (o + 1))
                            if n_turn >= 2:
                                pe.wait_ge(turned_out, n_turn - 1)
                            for ct in range(CT):
                                mm = pe.transpose(g.ps[:, n_turn % 2, ct * P:(ct + 1) * P], fold[:, s, ct, jt * P:(jt + 1) * P], g.ident[:])
                            mm.then_inc(turned, 1)
                            n_turn += 1
                    for ct in range(CT):
                        src = z[:, ct, FOLD:FOLD + 1]
                        mm = pe.transpose(g.ps[0:1, 2, ct * P:(ct + 1) * P], src, g.ident[:])
                    mm.then_inc(mid_turned, 1)
                    pe.wait_ge(turned_out, 2 * FT * (o + 1))
                    pe.wait_ge(mid_out, o + 1)
                    n = 0
                    for parity in range(2):
                        for i in range(FT):
                            w = o * 2 * FT + n
                            for kind in range(2):
                                q = 2 * parity + kind
                                part, src, middle_counts = PARTS[q]
                                bank = 3 + 2 * (n % 2) + kind
                                if n >= 2 and kind == 0:
                                    pe.wait_ge(mult, 4 * (w - 1))
                                for jt in range(FT):
                                    mm = pe.matmul(g.ps[:, bank, :], tabs[:, q, jt, i * P:(i + 1) * P], tim[:, 0 if src == "sum" else 1, jt, :],
                                                   start=(jt == 0), stop=(jt == FT - 1 and not middle_counts))
                                if middle_counts:
                                    mm = pe.matmul(g.ps[:, bank, :], alt_row[:, 0:P], mid[:], start=False, stop=True)
                            mm.then_inc(product, 1)
                            n += 1
                    for jt in range(FT):
                        pe.matmul(g.ps[0:1, 7, :], alt_col[:], tim[:, 0, jt, :], start=(jt == 0), stop=False)
                    pe.matmul(g.ps[0:1, 7, :], alt_row[:, 0:1], mid[:], start=False, stop=True).then_inc(product, 1)
                    pe.wait_ge(combined, 4 * FT * (o + 1))
                    pe.wait_ge(last_made, o + 1)
                    for ct in range(CT):
                        v = o * CT + ct
                        cs = slice(ct * P, (ct + 1) * P)
                        a_bank, b_bank, c_bank = (0, 1, 2) if v % 2 == 0 else (3, 4, 5)
                        if ct >= 2:
                            pe.wait_ge(mirrored, v - 1)
                            pe.wait_ge(sym_out, 2 * (v - 1))
                        for bank, (p0, t0), (p1, t1) in ((a_bank, (0, tabs[:, 0]), (3, back[:, 1])), (b_bank, (2, back[:, 0]), (1, tabs[:, 1]))):
                            for pp, tab in ((p0, t0), (p1, t1)):
                                for i in range(FT):
                                    mm = pe.matmul(g.ps[:, bank, :], yv[:, pp, i, cs], tab[:, i, :], start=(pp == p0 and i == 0),
                                                   stop=(bank == b_bank and pp == p1 and i == FT - 1))
                            if bank == a_bank:
                                pe.matmul(g.ps[:, bank, :], yl[:, cs], alt_row[:], start=False, stop=True)
                        for pp in (0, 3):
                            for i in range(FT):
                                pe.matmul(g.ps[:, c_bank, 0:1], yv[:, pp, i, cs], alt_col[:], start=(pp == 0 and i == 0), stop=False)
                        pe.matmul(g.ps[:, c_bank, 0:1], yl[:, cs], alt_row[:, 0:1], start=False, stop=True).then_inc(inverse, 1)

            @block.scalar
            def _(act):
                n_turn = 0
                for o in range(ORD):
                    for s in range(2):
                        for jt in range(FT):
                            act.wait_ge(turned, n_turn + 1)
                            if o and n_turn == 2 * FT:
                                act.wait_ge(product, 2 * FT + 1)
                            act.activation(tim[:, s, jt, :], g.ps[:, n_turn % 2, :], ACT.Copy).then_inc(turned_out, 1)
                            n_turn += 1
                    act.wait_ge(mid_turned, o + 1)
                    act.activation(mid[:], g.ps[0:1, 2, :], ACT.Copy).then_inc(mid_out, 1)
                    for ct in range(CT):
                        v = o * CT + ct
                        act.wait_ge(inverse, v + 1)
                        if v >= 2:
                            act.wait_ge(mirrored, v - 1)
                            act.wait_ge(middle, v - 1)
                        a_bank, c_bank = (0, 2) if v % 2 == 0 else (3, 5)
                        act.activation(sym[:, v % 2, 0:FOLD], g.ps[:, a_bank, :], ACT.Copy).then_inc(sym_out, 1)
                        act.activation(sym[:, v % 2, FOLD:FOLD + 1], g.ps[:, c_bank, 0:1], ACT.Copy).then_inc(sym_out, 1)

            @block.vector
            def _(dve):
                def fold_tile(src, ct):
                    x = src[:, ct, :]
                    head, tail = x[:, 1:FOLD], x[:, LAT - 1:FOLD:-1]
                    dve.tensor_tensor(fold[:, 0, ct, 1:FOLD], head, tail, ALU.add).then_inc(first_copied, 1)
                    dve.tensor_tensor(fold[:, 1, ct, 1:FOLD], head, tail, ALU.subtract).then_inc(first_copied, 1)
                    dve.tensor_copy(fold[:, 0, ct, 0:1], x[:, 0:1]).then_inc(folded, 1)
                    dve.tensor_copy(fold[:, 1, ct, 0:1], x[:, 0:1]).then_inc(folded, 1)

                dve.wait_ge(u3_in[0], 16)
                for ct in range(CT):
                    fold_tile(z, ct)
                for o in range(ORD):
                    n = 0
                    for parity in range(2):
                        for i in range(FT):
                            w = o * 2 * FT + n
                            dve.wait_ge(product, o * (2 * FT + 1) + n + 1)
                            dve.wait_ge(h_in[w % 3], 16 * (w // 3 + 1))
                            if w:
                                dve.wait_ge(combined, 2 * w)
                            if o and n == 0:
                                dve.wait_ge(inverse, CT * o)
                            c_ps, s_ps = g.ps[:, 3 + 2 * (n % 2), :], g.ps[:, 4 + 2 * (n % 2), :]
                            ch, sh = h[:, w % 3, 0, :], h[:, w % 3, 1, :]
                            for m, (x, y_) in enumerate(((c_ps, ch), (s_ps, sh), (c_ps, sh), (s_ps, ch))):
                                dve.tensor_tensor(pr[:, m, :], x, y_, ALU.mult).then_inc(mult, 1)
                            dve.wait_ge(mult, 4 * (w + 1))
                            dve.tensor_tensor(yv[:, 2 * parity, i, :], pr[:, 0, :], pr[:, 1, :], ALU.subtract).then_inc(combined, 1)
                            dve.tensor_tensor(yv[:, 2 * parity + 1, i, :], pr[:, 2, :], pr[:, 3, :], ALU.add).then_inc(combined, 1)
                            n += 1
                    dve.wait_ge(product, (o + 1) * (2 * FT + 1))
                    dve.wait_ge(last_in, 16 * (o + 1))
                    if o:
                        dve.wait_ge(inverse, CT * o)
                    dve.tensor_tensor(yl[:], g.ps[0:1, 7, :], hl[:], ALU.mult).then_inc(last_made, 1)
                    dve.wait_ge(u3_in[o + 1], 16)
                    for ct in range(CT):
                        v = o * CT + ct
                        b_bank = 1 if v % 2 == 0 else 4
                        dve.wait_ge(sym_out, 2 * (v + 1))
                        if v >= 2:
                            dve.wait_ge(skipped, v - 1)
                        t = tm[:, v % 2, :]
                        dve.tensor_tensor(t[:, 0:FOLD], sym[:, v % 2, 0:FOLD], g.ps[:, b_bank, :], ALU.add).then_inc(times, 1)
                        dve.tensor_copy(t[:, FOLD:FOLD + 1], sym[:, v % 2, FOLD:FOLD + 1]).then_inc(middle, 1)
                        dve.tensor_tensor(t[:, LAT - 1:FOLD:-1], sym[:, v % 2, 1:FOLD], g.ps[:, b_bank, 1:FOLD], ALU.subtract).then_inc(mirrored, 1)
                        dve.wait_ge(times, v + 1)
                        dve.wait_ge(middle, v + 1)
                        dve.wait_ge(mirrored, v + 1)
                        prev = z[:, ct, :]
                        if o:
                            dve.wait_ge(gated, ct + 1)
                        dve.scalar_tensor_tensor(out=t, in0=prev, scalar=vec(g, "skip", 4 * o + ct), in1=t, op0=ALU.mult, op1=ALU.add).then_inc(skipped, 1)
                        dve.wait_ge(skipped, v + 1)
                        dve.tensor_tensor(z[:, ct, :], t, u3[:, CT * (o + 1) + ct, :], ALU.mult).then_inc(gated, 1)
                        if o == 0:
                            dve.wait_ge(gated, v + 1)
                            if ct == 0:
                                dve.wait_ge(mid_turned, 1)
                            fold_tile(z, ct)


def build_program(nc, d):
    g = Globals()
    STAGES.clear()
    with ExitStack() as mem:
        def sb(name, shape):
            return tile(nc, mem, name, shape)

        g.ps = mem.enter_context(nc.psum_tensor("psum", [P, 8, BANK], F32))
        g.vec = sb("small_vectors", [P, NVEC])
        g.ident = sb("identity", [P, P])
        g.ones = sb("all_ones", [P, P])
        g.cond = sb("conditioning", [P, KT, 2])
        g.mod = sb("modulation", [P, 2, 6, KT, 2])
        g.eps = sb("epsilon", [P, 1])

        sc = Globals()
        def scratch(name, shape):
            return nc.dram_tensor(name, shape, F32, kind="Internal").ap()
        sc.qk_a = scratch("scratch_qk_a", [5, P, TOK])
        sc.v_a = scratch("scratch_v_a", [P, KTILES, P])
        sc.q_b = scratch("scratch_q_b", [B_HEADS, B_DK, TOK])
        sc.k_b = scratch("scratch_k_b", [B_HEADS, B_DK, TOK])
        sc.v_b = scratch("scratch_v_b", [P, KTILES, B_HEADS * B_V])

        sc.x = scratch("scratch_x", [P, KT, TOK])
        sc.u3 = scratch("scratch_hyena", [P, 12, LAT])
        sc.y = scratch("scratch_ssd", [P, 4, LAT])
        sc.h = scratch("scratch_spectra", [2, 16, P, W_HY])
        sc.last = scratch("scratch_last", [2, W_HY])

        load_constants(nc, g, d)
        layer_0(nc, g, d, sc)
        layer_1(nc, g, d, sc)


def layer_0(nc, g, d, sc):
    adaln(nc, g, d, 0)
    with ExitStack() as sc.mem:
        g.h = tile(nc, sc.mem, "h", [P, KT, TOK])
        with ExitStack() as only_x:
            g.x = tile(nc, only_x, "x", [P, KT, TOK])
            load(nc, [(g.x, d["x"])])
            norm_modulate(nc, g, 0, SCALE_A, SHIFT_A, TOK)
        project_attention(nc, g, d, sc)
    with ExitStack() as memory:
        mixed = tile(nc, memory, "mixed", [P, KT, TOK])
        attention(nc, g, sc, mixed)
        g.x = tile(nc, memory, "x", [P, KT, TOK])
        load(nc, [(g.x, d["x"])])
        out = tile(nc, memory, "out", [P, KT, TOK])
        project_out(nc, g, mixed, d["w_out0"], out, TOK)
        residual(nc, g, out, 0, GATE_A, TOK)
        g.h = mixed
        norm_modulate(nc, g, 0, SCALE_M, SHIFT_M, TOK)
        with ExitStack() as ff:
            hid = tile(nc, ff, "hid", [P, KT, TOK])
            mlp(nc, g, out, hid, d["ff_w1"][0], d["ff_w2"][0], TOK)
        residual(nc, g, out, 0, GATE_M, TOK)
        store(nc, g.x, sc.x)


def layer_1(nc, g, d, sc):
    adaln(nc, g, d, 1)
    with ExitStack() as memory:
        y = tile(nc, memory, "ssd_out", [P, 4, LAT])
        g.h = tile(nc, memory, "h", [P, KT, TOK])
        with ExitStack() as only_x:
            g.x = tile(nc, only_x, "x", [P, KT, TOK])
            load(nc, [(g.x, sc.x)])
            norm_modulate(nc, g, 1, SCALE_A, SHIFT_A, TOK)
        project_hyena(nc, g, d, sc.u3)
        xbc = tile(nc, memory, "xbc", [P, 8, TOK])
        gate = tile(nc, memory, "gate", [P, 4, LAT])
        dt, adt = tile(nc, memory, "dt", [P, KTILES, 16]), tile(nc, memory, "adt", [P, KTILES, 16])
        project_mamba(nc, g, d, xbc, gate, dt, adt)
        with ExitStack() as tokens_first:
            ssd = Globals()
            ssd.mem, ssd.y = tokens_first, y
            scan_states(nc, g, d, xbc, gate, dt, adt, ssd)
        gate_norm(nc, g, xbc, gate, y, y)
        store(nc, y, sc.y)
    spectra = Globals()
    spectra.h, spectra.last = sc.h, sc.last
    with ExitStack() as memory:
        spectra.alt_row = tile(nc, memory, "alternate_row", [1, FOLD])
        spectra.alt_col = tile(nc, memory, "alternate_column", [P, 1])
        with ExitStack() as features:
            spectra.h2 = tile(nc, features, "hy_h2", [P, LAT + 1])
            spectra.h2r = tile(nc, features, "hy_h2_flipped", [P, FOLD])
            spectra.h2b = tile(nc, features, "hy_h2_behind", [P, P])
            hyena_spectra(nc, g, d, spectra)
        u3 = tile(nc, memory, "hyena_parts", [P, 12, LAT])
        long_convs(nc, g, d, spectra, sc.u3, u3)
        g.x = tile(nc, memory, "x", [P, KT, LAT])
        out = tile(nc, memory, "out", [P, KT, LAT])
        mixed = u3[:, 0:KT, :]
        load(nc, [(mixed[:, 4:KT, :], sc.y), (g.x, sc.x[:, :, 0:LAT])])
        project_out(nc, g, mixed, d["w_out1"], out, LAT)
        residual(nc, g, out, 1, GATE_A, LAT)
        g.h = mixed
        norm_modulate(nc, g, 1, SCALE_M, SHIFT_M, LAT)
        with ExitStack() as ff:
            hid = tile(nc, ff, "hid", [P, KT, LAT])
            mlp(nc, g, out, hid, d["ff_w1"][1], d["ff_w2"][1], LAT)
        residual(nc, g, out, 1, GATE_M, LAT)
        store(nc, g.x, d["out"])


def store(nc, src, dst):
    with stage(nc, "stored") as (mem, (stored,)):
        with nc.Block() as block:
            @block.sync
            def _(sp):
                sp.dma_start(dst, src[:]).then_inc(stored, 16)
                sp.wait_ge(stored, 16)


def feature_tiles(v):
    return np.ascontiguousarray(v.reshape(-1, P).T)


def k_major(w):
    return w.reshape(-1, P, w.shape[1]).transpose(1, 0, 2)


def pieces(w, width=256):
    kk = k_major(w)
    return np.ascontiguousarray(kk.reshape(P, kk.shape[1], -1, width).transpose(2, 0, 1, 3))


def rope_tables():
    t = np.arange(LAT)
    t_row, t_col = (t // GRID_W).astype(np.float32), (t % GRID_W).astype(np.float32)
    def angles(rot):
        quarter = rot // 4
        inv = np.float32(THETA) ** (-np.arange(quarter, dtype=np.float32) / np.float32(quarter))
        return np.concatenate([t_row[None, :] * inv[:, None], t_col[None, :] * inv[:, None]]).astype(np.float32)
    a = {}
    for tag, first, rot, heads in (("a", 0, A_DIM, 2), ("b", B_NOPE, B_ROPE, 1)):
        ang, half = angles(rot), rot // 2
        cos, sin, swap = np.ones((P, TOK), np.float32), np.zeros((P, TOK), np.float32), np.zeros((P, P), np.float32)
        for h in range(heads):
            at = first + h * rot
            for part, sign in ((0, -1), (1, 1)):
                r = np.arange(at + part * half, at + (part + 1) * half)
                cos[r, :LAT] = np.cos(ang)
                sin[r, :LAT] = sign * np.sin(ang)
                swap[r + (half if part == 0 else -half), r] = 1
        a[f"cos_{tag}"], a[f"sin_{tag}"], a[f"swap_{tag}"] = cos, sin, swap
    a["by_head"] = np.kron(np.eye(2), np.ones((A_DIM, A_DIM))).astype(np.float32)
    return a


def hyena_tables():
    f32 = np.float32
    a = {}
    bands = 16
    t = np.linspace(0.0, 1.0, LAT, dtype=f32)
    w = (f32(2.0 * math.pi) * np.arange(LAT, dtype=f32) / f32(LAT)).astype(f32)
    ph = w[:, None] * np.linspace(1e-4, bands - 1, bands, dtype=f32)[None, :]
    a["positions"] = np.ascontiguousarray(np.concatenate([t[:, None], np.cos(ph), -np.sin(ph)], axis=1).T.astype(f32))
    deltas = np.abs(np.linspace(math.log(1e-2) / 1.5, math.log(1e-2) / 0.3, W_HY, dtype=f32))
    decay = np.exp(-t[:, None] * deltas[None, :]).astype(f32)
    tiles = lambda x: x.reshape(FT, P, -1).transpose(1, 0, 2)
    ahead = np.concatenate([np.zeros((1, W_HY), f32), decay[:FOLD:-1]])
    a["decay"] = np.ascontiguousarray(np.stack([tiles(decay[:FOLD]), tiles(ahead)], axis=1))
    a["decay_middle"] = np.ascontiguousarray(decay[FOLD:FOLD + 1])
    j, m = np.arange(FOLD)[:, None], np.arange(FOLD)[None, :]
    even, odd = 2 * np.pi * (m * j % LAT) / LAT, np.pi * (j * (2 * m + 1) % (2 * LAT)) / LAT
    forms = [np.cos(even), np.sin(even), np.cos(odd), np.sin(odd)]
    a["dft"] = np.ascontiguousarray(np.stack([tiles(x) for x in forms], axis=1).astype(f32))
    a["dft_back"] = np.ascontiguousarray(np.stack([tiles(x.T) for x in forms[2:]], axis=1).astype(f32))
    a["alt_row"] = ((-1.0) ** np.arange(FOLD)).astype(f32)[None, :]
    a["alt_col"] = ((-1.0) ** np.arange(P)).astype(f32)[:, None]
    s, l = np.arange(P)[:, None], np.arange(P)[None, :]
    a["triangles"] = np.ascontiguousarray(np.stack([s <= l, s >= l], axis=1).astype(f32))
    return a


def lay_out(i):
    a = {}
    tokens = np.concatenate([i["x"][0], i["ctx"][0]], axis=0)
    a["x"] = np.ascontiguousarray(tokens.T.reshape(KT, P, TOK).transpose(1, 0, 2))
    a["cond"] = np.ascontiguousarray(np.stack([i["c"][0], i["c_ctx"]], axis=1).reshape(KT, P, 2).transpose(1, 0, 2))
    a["ident"] = np.eye(P, dtype=np.float32)
    a["ones"] = np.ones((P, P), np.float32)
    a["ada_w"] = np.stack([pieces(i["ada_w"][l]) for l in range(2)])
    def quarters(w):
        return np.concatenate([pieces(w[q * D:(q + 1) * D]) for q in range(4)])
    a["ff_w1"] = np.stack([pieces(i["ff_w1"][l]) for l in range(2)])
    a["ff_w2"] = np.stack([quarters(i["ff_w2"][l]) for l in range(2)])

    w = i["at_w_in"][0]
    k_a, v_a, low, key, q_a, q_low = np.split(w, np.cumsum([128, 128, 128, 32, 512]), axis=1)
    a["w_qk"] = pieces(np.concatenate([k_a, q_a], axis=1), P)
    a["w_low"] = np.ascontiguousarray(np.stack([k_major(x) for x in (q_low[:, :P], q_low[:, P:], low)], axis=1))
    a["w_key"] = np.ascontiguousarray(k_major(key))
    a["w_v_a"] = np.ascontiguousarray(k_major(v_a))
    up = i["ml_w_kv_up"][0].reshape(P, B_HEADS, B_NOPE + B_V)
    a["w_k_up"] = np.ascontiguousarray(up[:, :, :B_NOPE].reshape(P, -1))
    a["w_v_up"] = np.ascontiguousarray(up[:, :, B_NOPE:].reshape(P, -1))
    a["w_q_up"] = np.ascontiguousarray(k_major(i["ml_w_q_up"][0]))
    a["w_out0"] = pieces(i["at_w_out"][0])
    w_hy, w_z, w_xbc, w_dt = np.split(i["lc_w_in"][0], np.cumsum([1536, 512, 1024]), axis=1)
    a["w_hy"], a["w_z"], a["w_xbc"] = pieces(w_hy, P), pieces(w_z, P), pieces(w_xbc, P)
    a["w_dt"] = np.ascontiguousarray(k_major(w_dt))
    a["w_out1"] = pieces(i["lc_w_out"][0])
    a["hy_w1"], a["hy_w2"], a["hy_w3"] = (np.ascontiguousarray(i[n][0]) for n in ("hy_w1", "hy_w2", "hy_w3"))
    a.update(hyena_tables())
    a.update(rope_tables())

    v = np.zeros((P, NVEC), np.float32)
    def put(name, cols, at=0):
        v[:cols.shape[0], VEC[name][0] + at:VEC[name][0] + at + cols.shape[1]] = cols
    put("ada_b", np.repeat(feature_tiles(i["ada_b"]), 2, axis=1))
    put("norm_g", np.repeat(feature_tiles(i["norm_g"]), 2, axis=1))
    put("gain_k", np.tile(i["ga_k_norm"][0], 2)[:, None])
    put("gain_q", np.tile(i["ga_q_norm"][0], 2)[:, None])
    put("mlq", feature_tiles(i["ml_q_norm"][0]))
    put("mlkv", feature_tiles(i["ml_kv_norm"][0]))
    put("short_w", feature_tiles(i["hy_short_w"][0]))
    put("short_b", feature_tiles(i["hy_short_b"][0]))
    put("skip", feature_tiles(i["hy_skip"][0]))
    put("conv_w", feature_tiles(i["mb_conv_w"][0]))
    put("conv_b", feature_tiles(i["mb_conv_b"][0]))
    put("d_skip", feature_tiles(np.repeat(i["mb_d_skip"][0], 64)))
    put("mb_norm", feature_tiles(i["mb_norm"][0]))
    put("dt_bias", np.tile(i["mb_dt_bias"][0].reshape(1, 16), (P, 1)))
    put("a_log", np.tile(i["mb_a_log"][0].reshape(1, 16), (P, 1)))
    put("hy_b1", i["hy_b1"][0][:, None])
    put("hy_b2", i["hy_b2"][0][:, None])
    put("freq", i["hy_freq"][0][:, None])
    a["vec"] = v
    return a


def kernel(**inputs):
    import concourse.bacc as bacc
    from concourse.bass_utils import run_bass_kernel_spmd

    nc = bacc.Bacc("TRN2", target_bir_lowering=False, num_devices=1)
    laid_out = lay_out({name: np.asarray(a) for name, a in inputs.items()})
    d, arrays = {}, {}
    for name, a in laid_out.items():
        arrays[f"in_{name}_dram"] = a
        d[name] = nc.dram_tensor(f"in_{name}_dram", a.shape, mybir.dt.from_np(a.dtype), kind="ExternalInput").ap()
    d["out"] = nc.dram_tensor("out_0_dram", (P, KT, LAT), F32, kind="ExternalOutput").ap()
    build_program(nc, d)
    r = run_bass_kernel_spmd(nc, [arrays], core_ids=[0])
    got = r.results[0]["out_0_dram"]
    return np.ascontiguousarray(got.transpose(2, 1, 0).reshape(1, LAT, D))
```

```python
from contextlib import ExitStack, contextmanager
import math

import numpy as np
import concourse.bass as bass
from concourse import mybir

F32 = mybir.dt.float32
F32R = mybir.dt.float32r
ACT = mybir.ActivationFunctionType
ALU = mybir.AluOpType
AX = mybir.AxisListType

P = 128
D = 1024
KT = D // P
LAT, CTX = 1024, 256
TOK = LAT + CTX
CHUNKS = [(0, 512), (512, 512), (1024, 256)]
STREAMS = [(0, LAT), (LAT, CTX)]
EPS = 1e-6
FF = 4 * D
GRID_W = 64
THETA = 10000.0
BANK = 512

A_DIM, A_HEADS = 64, 8
B_NOPE, B_ROPE, B_V, B_HEADS = 64, 32, 64, 8
B_DK = B_NOPE + B_ROPE
A_SCALE = A_DIM ** -0.5
B_SCALE = B_DK ** -0.5
KTILES = TOK // P
SQUARES_AT = 5
SHIFT_A, SCALE_A, GATE_A, SHIFT_M, SCALE_M, GATE_M = range(6)

VEC = {}
_at = 0
for _name, _n in (("ada_b", 2 * 96), ("norm_g", 2 * 4 * 16), ("gain_k", 1), ("gain_q", 1), ("mlq", 2), ("mlkv", 1),
                  ("short_w", 36), ("short_b", 12), ("skip", 8), ("conv_w", 24), ("conv_b", 8),
                  ("d_skip", 4), ("mb_norm", 4), ("dt_bias", 16), ("a_log", 16), ("hy_b1", 1), ("hy_b2", 1), ("freq", 1)):
    VEC[_name] = (_at, _n)
    _at += _n
NVEC = _at


STAGES = []


def tile(nc, mem, name, shape, side="left", dtype=F32):
    return mem.enter_context(nc.sbuf_tensor(name, shape, dtype, side=side, allow_name_mangling=True))


def tile_r(nc, mem, name, shape, side="left"):
    return tile(nc, mem, name, shape, side, F32R)


@contextmanager
def stage(nc, names):
    STAGES.append(names)
    sems = [nc.alloc_semaphore(f"{n}_{len(STAGES)}") for n in names.split()]
    with ExitStack() as mem:
        yield mem, sems
    nc.clear_and_free_semaphores(sems)
    nc.all_engine_barrier(sem_only=True)


def vec(g, name, i=0, n=1):
    at = VEC[name][0] + i
    return g.vec[:, at:at + n]


class Globals:
    pass


def load_constants(nc, g, d):
    with stage(nc, "loaded cond_ready gain_ready") as (mem, (loaded, cond_ready, gain_ready)):
        with nc.Block() as block:
            @block.sync
            def _(sp):
                for dst, src in ((g.vec, d["vec"]), (g.ident, d["ident"]), (g.ones, d["ones"]), (g.cond, d["cond"])):
                    sp.dma_start(dst[:], src).then_inc(loaded, 16)

            @block.scalar
            def _(act):
                act.wait_ge(loaded, 64)
                act.activation(g.cond[:], g.cond[:], ACT.Silu).then_inc(cond_ready, 1)

            @block.vector
            def _(dve):
                dve.memset(g.eps[:], EPS).then_inc(gain_ready, 1)
                dve.wait_ge(loaded, 64)
                dve.tensor_scalar(vec(g, "gain_q"), vec(g, "gain_q"), A_SCALE, None, ALU.mult).then_inc(gain_ready, 1)


def adaln(nc, g, d):
    SLOTS, PIECES, GROUPS = 4, 24, 4
    PART = BANK // P
    with stage(nc, "w_in0 w_in1 w_in2 w_in3 sel_in product read_out turned biased folded") as (mem, sems):
        w_in, (sel_in, product, read_out, turned, biased, folded) = sems[:4], sems[4:]
        w = tile(nc, mem, "ada_ring", [P, SLOTS, KT, BANK])
        rows = tile(nc, mem, "ada_rows", [P, SLOTS, BANK])
        sel = tile(nc, mem, "group_selector", [P, 2])
        src = d["ada_w"]
        WIDTH = PIECES * PART * 2
        acc = g.ps[:, SLOTS, 0:WIDTH]
        with nc.Block() as block:
            @block.sync
            def _(sp):
                sp.dma_start(sel[:], d["group_selector"]).then_inc(sel_in, 16)
                for s in range(SLOTS):
                    sp.dma_start(w[:, s], src[s]).then_inc(w_in[s], 16)
                with sp.Fori(1, PIECES // SLOTS) as i:
                    for s in range(SLOTS):
                        sp.wait_ge(product, (i - 1) * SLOTS + (s + 1))
                        sp.dma_start(w[:, s], src[bass.ds(i * SLOTS + s, 1)].rearrange("a p k n -> p (a k) n")).then_inc(w_in[s], 16)

            @block.tensor
            def _(pe):
                pe.wait_ge(sel_in, 16)
                with pe.Fori(0, PIECES // SLOTS) as i:
                    for s in range(SLOTS):
                        pe.wait_ge(w_in[s], (i + 1) * 16)
                        pe.wait_ge(read_out, i * SLOTS + (s + 1))
                        for half in range(KT // GROUPS):
                            for c in range(GROUPS):
                                mm = pe.matmul(g.ps[32 * c:32 * c + 32, s, :], g.cond[:, half * GROUPS + c, :], w[:, s, half * GROUPS + c, :],
                                               start=(half == 0), stop=(half == 1), tile_position=(0, 32 * c))
                        mm.then_inc(product, 1)
                    for s in range(SLOTS):
                        pe.wait_ge(read_out, i * SLOTS + (SLOTS + s + 1))
                        for m in range(PART):
                            mm = pe.matmul(g.ps[:, SLOTS, bass.ds(i * (2 * PART * SLOTS) + (2 * PART * s + 2 * m), 2)],
                                           rows[:, s, m * P:(m + 1) * P], sel[:], start=True, stop=True)
                        mm.then_inc(turned, 1)

            @block.scalar
            def _(act):
                act.sem_inc(read_out, SLOTS)
                with act.Fori(0, PIECES // SLOTS) as i:
                    for s in range(SLOTS):
                        act.wait_ge(product, i * SLOTS + (s + 1))
                        act.activation(rows[:, s, :], g.ps[:, s, :], ACT.Copy).then_inc(read_out, 1)

            @block.vector
            def _(dve):
                dve.wait_ge(turned, PIECES)
                flat = g.mod[:].rearrange("p l a k s -> p (l a k s)")
                dve.tensor_tensor(flat, acc, vec(g, "ada_b", 0, WIDTH), ALU.add).then_inc(biased, 1)
                dve.wait_ge(biased, 1)
                for layer in range(2):
                    for n, part in enumerate((SCALE_A, GATE_A, SCALE_M, GATE_M)):
                        gains = vec(g, "norm_g", (layer * 4 + n) * 16, 16)
                        now = g.mod[:, layer, part].rearrange("p k s -> p (k s)")
                        if part in (SCALE_A, SCALE_M):
                            dve.scalar_tensor_tensor(out=now, in0=now, scalar=1.0, in1=gains, op0=ALU.add, op1=ALU.mult).then_inc(folded, 1)
                        else:
                            dve.tensor_tensor(now, now, gains, ALU.mult).then_inc(folded, 1)


def load(nc, pairs):
    with stage(nc, "loaded") as (mem, (loaded,)):
        with nc.Block() as block:
            @block.sync
            def _(sp):
                n = 0
                for dst, src in pairs:
                    for k in range(src.shape[1]):
                        sp.dma_start(dst[:, k, :], src[:, k, :]).then_inc(loaded, 16)
                        n += 1
                sp.wait_ge(loaded, 16 * n)


def chunks_of(tokens):
    return [(a, n) for a, n in CHUNKS if a < tokens]


def norm_modulate(nc, g, x_src, layer, scale_part, shift_part, tokens):
    streams = [(a, n) for a, n in STREAMS if a < tokens]
    with stage(nc, "x_in squared square_used logged rstd scaled shifted") as (mem, (x_in, squared, square_used, logged, rstd, scaled, shifted)):
        x = tile(nc, mem, "x", [P, KT, tokens])
        sq = tile(nc, mem, "norm_sq", [P, 2, tokens])
        rs = tile(nc, mem, "norm_rs", [P, tokens])
        total = g.ps[:, 0:3, :].rearrange("p b n -> p (b n)")[:, 0:tokens]
        with nc.Block() as block:
            @block.sync
            def _(sp):
                for k in range(KT):
                    sp.dma_start(x[:, k, :], x_src[:, k, 0:tokens]).then_inc(x_in, 16)

            @block.scalar
            def _(act):
                act.preload_act_table_set("natural_log_exp_and_others")
                act.wait_ge(x_in, 16 * KT)
                for k in range(KT):
                    if k >= 2:
                        act.wait_ge(square_used, k - 1)
                    act.activation(sq[:, k % 2, :], x[:, k, 0:tokens], ACT.Square).then_inc(squared, 1)
                act.wait_ge(square_used, KT)
                act.activation(rs[:], total, ACT.Ln, bias=g.eps[:], scale=1.0 / D).then_inc(logged, 1)
                act.wait_ge(logged, 1)
                act.activation(rs[:], rs[:], ACT.Exp, scale=-0.5).then_inc(rstd, 1)
                for k in range(KT):
                    act.wait_ge(scaled, len(streams) * (k + 1))
                    for s, (a, n) in enumerate(streams):
                        act.activation(g.h[:, k, a:a + n], g.h[:, k, a:a + n], ACT.Identity,
                                       bias=g.mod[:, layer, shift_part, k, s:s + 1]).then_inc(shifted, 1)

            @block.tensor
            def _(pe):
                for k in range(KT):
                    pe.wait_ge(squared, k + 1)
                    for a, n in chunks_of(tokens):
                        mm = pe.matmul(total[:, a:a + n], g.ones[:], sq[:, k % 2, a:a + n], start=(k == 0), stop=(k == KT - 1))
                    mm.then_inc(square_used, 1)

            @block.vector
            def _(dve):
                dve.wait_ge(rstd, 1)
                for k in range(KT):
                    for s, (a, n) in enumerate(streams):
                        dve.scalar_tensor_tensor(out=g.h[:, k, a:a + n], in0=x[:, k, a:a + n],
                                                 scalar=g.mod[:, layer, scale_part, k, s:s + 1], in1=rs[:, a:a + n],
                                                 op0=ALU.mult, op1=ALU.mult).then_inc(scaled, 1)


def residual(nc, g, x_src, x_dst, out, layer, gate_part, tokens):
    with stage(nc, "x_in x_stored squared square_used logged rstd gated added") as (mem, (x_in, x_stored, squared, square_used, logged, rstd, gated, added)):
        x = tile(nc, mem, "x", [P, KT, tokens])
        sq = tile(nc, mem, "norm_sq", [P, 2, tokens])
        rs = tile(nc, mem, "norm_rs", [P, tokens])
        total = g.ps[:, 0:3, :].rearrange("p b n -> p (b n)")[:, 0:tokens]
        with nc.Block() as block:
            @block.sync
            def _(sp):
                for k in range(KT):
                    sp.dma_start(x[:, k, :], x_src[:, k, 0:tokens]).then_inc(x_in, 16)
                for k in range(KT):
                    sp.wait_ge(added, k + 1)
                    sp.dma_start(x_dst[:, k, 0:tokens], x[:, k, :]).then_inc(x_stored, 16)
                sp.wait_ge(x_stored, 16 * KT)

            @block.scalar
            def _(act):
                act.preload_act_table_set("natural_log_exp_and_others")
                for k in range(KT):
                    if k >= 2:
                        act.wait_ge(square_used, k - 1)
                    act.activation(sq[:, k % 2, :], out[:, k, 0:tokens], ACT.Square).then_inc(squared, 1)
                act.wait_ge(square_used, KT)
                act.activation(rs[:], total, ACT.Ln, bias=g.eps[:], scale=1.0 / D).then_inc(logged, 1)
                act.wait_ge(logged, 1)
                act.activation(rs[:], rs[:], ACT.Exp, scale=-0.5).then_inc(rstd, 1)

            @block.tensor
            def _(pe):
                for k in range(KT):
                    pe.wait_ge(squared, k + 1)
                    for a, n in chunks_of(tokens):
                        mm = pe.matmul(total[:, a:a + n], g.ones[:], sq[:, k % 2, a:a + n], start=(k == 0), stop=(k == KT - 1))
                    mm.then_inc(square_used, 1)

            @block.vector
            def _(dve):
                dve.wait_ge(rstd, 1)
                dve.wait_ge(x_in, 16 * KT)
                n_gated = 0
                for k in range(KT):
                    for s, (a, n) in enumerate(STREAMS):
                        if a >= tokens:
                            continue
                        dve.scalar_tensor_tensor(out=out[:, k, a:a + n], in0=out[:, k, a:a + n],
                                                 scalar=g.mod[:, layer, gate_part, k, s:s + 1], in1=rs[:, a:a + n],
                                                 op0=ALU.mult, op1=ALU.mult).then_inc(gated, 1)
                        n_gated += 1
                    dve.wait_ge(gated, n_gated)
                    dve.tensor_tensor(x[:, k, 0:tokens], x[:, k, 0:tokens], out[:, k, 0:tokens], ALU.add).then_inc(added, 1)


def residual_norm_split(nc, g, x_src, x_dst, out, gate, norm, tokens, high, low, squares_made=False):
    streams = [(a, n) for a, n in STREAMS if a < tokens]
    S = len(streams)
    spans = chunks_of(tokens)
    names = "x_in x_stored squared square_used logged rstd gated added_even added_odd scaled rounded split"
    with stage(nc, names) as (mem, sems):
        x_in, x_stored, squared, square_used, logged, rstd, gated, added_even, added_odd, scaled, rounded, split = sems
        added = (added_even, added_odd)
        x = tile(nc, mem, "x", [P, KT, tokens])
        sq = tile(nc, mem, "norm_sq", [P, 2, tokens])
        t = tile(nc, mem, "norm_scaled", [P, 2, tokens])
        rs = tile(nc, mem, "norm_rs", [P, tokens])
        totals = [g.ps[:, b:b + 3, :].rearrange("p b n -> p (b n)")[:, 0:tokens] for b in (SQUARES_AT, 0)]
        made = KT if squares_made else 0
        mod = lambda which, part, k, s: g.mod[:, which[0], part, k, s:s + 1]
        with nc.Block() as block:
            @block.sync
            def _(sp):
                for k in range(KT):
                    sp.dma_start(x[:, k, :], x_src[:, k, 0:tokens]).then_inc(x_in, 16)
                for k in range(KT):
                    sp.wait_ge(added[k % 2], k // 2 + 1)
                    sp.dma_start(x_dst[:, k, 0:tokens], x[:, k, :]).then_inc(x_stored, 16)
                sp.wait_ge(x_stored, 16 * KT)

            @block.scalar
            def _(act):
                act.preload_act_table_set("natural_log_exp_and_others")
                for i in range(2):
                    for k in range(KT):
                        q = i * KT + k - made
                        if q < 0:
                            continue
                        if i == 1:
                            act.wait_ge(added[k % 2], k // 2 + 1)
                        if q >= 2:
                            act.wait_ge(square_used, q - 1)
                        src = out[:, k, 0:tokens] if i == 0 else x[:, k, :]
                        act.activation(sq[:, q % 2, :], src, ACT.Square).then_inc(squared, 1)
                    if (i + 1) * KT > made:
                        act.wait_ge(square_used, (i + 1) * KT - made)
                    act.activation(rs[:], totals[i], ACT.Ln, bias=g.eps[:], scale=1.0 / D).then_inc(logged, 1)
                    act.wait_ge(logged, i + 1)
                    act.activation(rs[:], rs[:], ACT.Exp, scale=-0.5).then_inc(rstd, 1)
                for k in range(KT):
                    for s, (a, n) in enumerate(streams):
                        act.wait_ge(scaled, S * k + s + 1)
                        act.activation(high[:, k, a:a + n], t[:, k % 2, a:a + n], ACT.Identity, bias=mod(norm, norm[2], k, s)).then_inc(rounded, 1)

            @block.tensor
            def _(pe):
                for q in range(2 * KT - made):
                    i, k = divmod(q + made, KT)
                    pe.wait_ge(squared, q + 1)
                    for a, n in spans:
                        mm = pe.matmul(totals[i][:, a:a + n], g.ones[:], sq[:, q % 2, a:a + n], start=(k == 0), stop=(k == KT - 1))
                    mm.then_inc(square_used, 1)

            @block.gpsimd
            def _(pool):
                pool.wait_ge(x_in, 16 * KT)
                for k in range(1, KT, 2):
                    pool.wait_ge(gated, S * (k + 1))
                    pool.tensor_tensor(x[:, k, :], x[:, k, :], out[:, k, 0:tokens], ALU.add).then_inc(added_odd, 1)

            @block.vector
            def _(dve):
                dve.wait_ge(x_in, 16 * KT)
                dve.wait_ge(rstd, 1)
                for k in range(KT + 1):
                    if k < KT:
                        for s, (a, n) in enumerate(streams):
                            dve.scalar_tensor_tensor(out=out[:, k, a:a + n], in0=out[:, k, a:a + n], scalar=mod(gate, gate[1], k, s),
                                                     in1=rs[:, a:a + n], op0=ALU.mult, op1=ALU.mult).then_inc(gated, 1)
                    if k % 2:
                        v = k - 1
                        dve.wait_ge(gated, S * (v + 1))
                        dve.tensor_tensor(x[:, v, :], x[:, v, :], out[:, v, 0:tokens], ALU.add).then_inc(added_even, 1)
                dve.wait_ge(rstd, 2)
                for k in range(KT + 1):
                    if k < KT:
                        for s, (a, n) in enumerate(streams):
                            if k >= 2:
                                dve.wait_ge(split, S * (k - 2) + s + 1)
                            if k < 2:
                                dve.wait_ge(added[k % 2], k // 2 + 1)
                            else:
                                dve.wait_ge(added[k % 2], KT // 2)
                            dve.scalar_tensor_tensor(out=t[:, k % 2, a:a + n], in0=x[:, k, a:a + n], scalar=mod(norm, norm[1], k, s),
                                                     in1=rs[:, a:a + n], op0=ALU.mult, op1=ALU.mult).then_inc(scaled, 1)
                    if k >= 1:
                        v = k - 1
                        for s, (a, n) in enumerate(streams):
                            dve.wait_ge(rounded, S * v + s + 1)
                            dve.scalar_tensor_tensor(out=low[:, v, a:a + n], in0=t[:, v % 2, a:a + n], scalar=mod(norm, norm[2], v, s),
                                                     in1=high[:, v, a:a + n], op0=ALU.add, op1=ALU.subtract).then_inc(split, 1)


class WeightRing:

    def __init__(self, nc, mem, sems, product, after, shape=(KT, P)):
        self.raw_in, (self.rounded, self.split) = sems[:2], sems[2:]
        self.product, self.after = product, after
        self.raw = tile(nc, mem, "w_raw", [P, 2, *shape])
        self.high, self.low = tile_r(nc, mem, "w_high", [P, 2, *shape]), tile_r(nc, mem, "w_low", [P, 2, *shape])
        self.pieces = len(after)

    def load(self, sp, t, src):
        if t >= 2:
            sp.wait_ge(self.split, t - 1)
        sp.dma_start(self.raw[:, t % 2], src).then_inc(self.raw_in[t % 2], 16)

    def round_piece(self, act, t):
        if t >= self.pieces:
            return
        act.wait_ge(self.raw_in[t % 2], 16 * (t // 2 + 1))
        if t >= 2:
            act.wait_ge(self.product, self.after[t - 2])
        act.activation(self.high[:, t % 2], self.raw[:, t % 2], ACT.Copy).then_inc(self.rounded, 1)

    def split_piece(self, dve, t):
        if t >= self.pieces:
            return
        dve.wait_ge(self.rounded, t + 1)
        dve.tensor_tensor(self.low[:, t % 2], self.raw[:, t % 2], self.high[:, t % 2], ALU.subtract).then_inc(self.split, 1)

    def product_of(self, pe, out, t, high, low, a, n):
        w_high, w_low = self.high[:, t % 2], self.low[:, t % 2]
        for k in range(KT):
            for i, (x, y) in enumerate(((w_high, high), (w_high, low), (w_low, high))):
                mm = pe.matmul(out, x[:, k, :], y[:, k, a:a + n], start=(k == 0 and i == 0), stop=(k == KT - 1 and i == 2))
        return mm


def mlp(nc, g, out, high, low, w, tokens):
    EIGHTHS, PIECES, HT, BANKS = 8, 8, 4, 4
    spans = chunks_of(tokens)
    C = len(spans)
    UP, DOWN = HT * C, 2 * HT * C
    ALL = UP + DOWN
    names = "w_in0 w_in1 w_rounded w_split product up_free down_free rectified squared rounded hid_split cleared"
    with stage(nc, names) as (mem, sems):
        w_in, (w_rounded, w_split, product, up_free, down_free, rectified, squared, rounded, hid_split, cleared) = sems[:2], sems[2:]
        raw = tile(nc, mem, "w_raw", [P, 2, KT, P])
        w_hi, w_lo = tile_r(nc, mem, "w_high", [P, 2, KT, P]), tile_r(nc, mem, "w_low", [P, 2, KT, P])
        hid_hi, hid_lo = tile_r(nc, mem, "hid_high", [P, HT, tokens]), tile_r(nc, mem, "hid_low", [P, HT, tokens])
        relu, square = tile(nc, mem, "hid_relu", [P, 2, BANK]), tile(nc, mem, "hid_square", [P, 2, BANK])

        def products_before(e, j):
            done = (j + 1) * C if j < HT else UP + (j + 1 - HT) * 2 * C
            return e * ALL + done

        with nc.Block() as block:
            @block.sync
            def _(sp):
                def load(piece, slot):
                    sp.dma_start(raw[:, slot], w[bass.ds(piece, 1)].rearrange("a p k n -> p (a k) n")).then_inc(w_in[slot], 16)
                load(0, 0)
                load(1, 1)
                def eighth(e, last):
                    for j in range(PIECES - 2 if last else PIECES):
                        sp.wait_ge(w_split, e * PIECES + (j + 1))
                        load(e * PIECES + (j + 2), j % 2)
                with sp.Fori(0, EIGHTHS - 1) as e:
                    eighth(e, False)
                eighth(EIGHTHS - 1, True)

            @block.tensor
            def _(pe):
                with pe.Fori(0, EIGHTHS) as e:
                    for j in range(PIECES):
                        pe.wait_ge(w_split, e * PIECES + (j + 1))
                        wh, wl = w_hi[:, j % 2], w_lo[:, j % 2]
                        if j < HT:
                            for c, (a, n) in enumerate(spans):
                                u = j * C + c
                                pe.wait_ge(up_free, e * UP + (u + 1))
                                for k in range(KT):
                                    for i, (x, y) in enumerate(((wh, high), (wh, low), (wl, high))):
                                        mm = pe.matmul(g.ps[:, u % BANKS, 0:n], x[:, k, :], y[:, k, a:a + n],
                                                       start=(k == 0 and i == 0), stop=(k == KT - 1 and i == 2))
                                mm.then_inc(product, 1)
                        else:
                            for half in range(2):
                                for c, (a, n) in enumerate(spans):
                                    u = ((j - HT) * 2 + half) * C + c
                                    pe.wait_ge(down_free, e * DOWN + (u + 1))
                                    if u < C:
                                        pe.wait_ge(hid_split, e * UP + ((HT - 1) * C + c + 1))
                                    for k in range(HT):
                                        for i, (x, y) in enumerate(((wh, hid_hi), (wh, hid_lo), (wl, hid_hi))):
                                            mm = pe.matmul(g.ps[:, BANKS + u % BANKS, 0:n], x[:, k * 2 + half, :], y[:, k, a:a + n],
                                                           start=(k == 0 and i == 0), stop=(k == HT - 1 and i == 2))
                                    mm.then_inc(product, 1)

            @block.scalar
            def _(act):
                act.sem_inc(up_free, BANKS)
                def round_piece(e, j):
                    slot = (j + 1) % 2
                    act.wait_ge(w_in[slot], e * (8 * PIECES) + 16 * ((j + 1) // 2 + 1))
                    if j >= 1:
                        act.wait_ge(product, products_before(e, j - 1))
                    act.activation(w_hi[:, slot], raw[:, slot], ACT.Copy).then_inc(w_rounded, 1)
                def eighth(e, last, first=False):
                    for j in range(PIECES):
                        if j == 0 and not first:
                            act.wait_ge(product, e * ALL)
                        if not (last and j == PIECES - 1):
                            round_piece(e, j)
                        if j < HT:
                            for c, (a, n) in enumerate(spans):
                                u = j * C + c
                                act.wait_ge(product, e * ALL + (u + 1))
                                if u >= 2 or not first:
                                    act.wait_ge(hid_split, e * UP + (u - 1))
                                act.activation(relu[:, u % 2, 0:n], g.ps[:, u % BANKS, 0:n], ACT.Relu).then_inc(up_free, 1)
                                act.wait_ge(up_free, e * UP + (BANKS + u + 1))
                                act.activation(square[:, u % 2, 0:n], relu[:, u % 2, 0:n], ACT.Square).then_inc(squared, 1)
                act.wait_ge(w_in[0], 16)
                act.activation(w_hi[:, 0], raw[:, 0], ACT.Copy).then_inc(w_rounded, 1)
                eighth(0, False, True)
                with act.Fori(1, EIGHTHS - 1) as e:
                    eighth(e, False)
                eighth(EIGHTHS - 1, True)

            @block.vector
            def _(dve):
                dve.sem_inc(down_free, BANKS)
                def split_piece(e, j):
                    slot = (j + 1) % 2
                    dve.wait_ge(w_rounded, e * PIECES + (j + 2))
                    dve.tensor_tensor(w_lo[:, slot], raw[:, slot], w_hi[:, slot], ALU.subtract).then_inc(w_split, 1)
                def eighth(e, last):
                    for j in range(PIECES):
                        if not (last and j == PIECES - 1):
                            split_piece(e, j)
                        if j < HT:
                            for c, (a, n) in enumerate(spans):
                                u = j * C + c
                                dve.wait_ge(up_free, e * UP + (BANKS + u + 1))
                                dve.tensor_tensor(hid_hi[:, j, a:a + n], relu[:, u % 2, 0:n], relu[:, u % 2, 0:n], ALU.mult).then_inc(rounded, 1)
                                dve.wait_ge(rounded, e * UP + (u + 1))
                                dve.wait_ge(squared, e * UP + (u + 1))
                                dve.tensor_tensor(hid_lo[:, j, a:a + n], square[:, u % 2, 0:n], hid_hi[:, j, a:a + n], ALU.subtract).then_inc(hid_split, 1)
                        else:
                            for half in range(2):
                                m = (j - HT) * 2 + half
                                for c, (a, n) in enumerate(spans):
                                    u = m * C + c
                                    dve.wait_ge(product, e * ALL + (UP + u + 1))
                                    dve.tensor_tensor(out[:, m, a:a + n], out[:, m, a:a + n],
                                                      g.ps[:, BANKS + u % BANKS, 0:n], ALU.add).then_inc(down_free, 1)
                dve.wait_ge(w_rounded, 1)
                dve.tensor_tensor(w_lo[:, 0], raw[:, 0], w_hi[:, 0], ALU.subtract).then_inc(w_split, 1)
                dve.memset(out[:, :, 0:tokens], 0.0).then_inc(cleared, 1)
                dve.wait_ge(cleared, 1)
                with dve.Fori(0, EIGHTHS - 1) as e:
                    eighth(e, False)
                eighth(EIGHTHS - 1, True)


def project_attention(nc, g, d, sc):
    TILES = 5
    units = [(t, a, n) for t in range(TILES) for a, n in CHUNKS]
    U = len(units)
    C = len(CHUNKS)

    names = "w_in tabs_in product raw_out squared meaned logged rstd normed rotated halves roped stored0 stored1"
    with stage(nc, names) as (mem, sems):
        w_in, tabs_in, product, raw_out, squared, meaned, logged, rstd, normed, rotated, halves, roped = sems[:12]
        stored = sems[12:]
        w = tile(nc, mem, "wa", [P, TILES, KT, P])
        cos, sin = tile(nc, mem, "cos_a", [P, TOK]), tile(nc, mem, "sin_a", [P, TOK])
        by_head, swap = tile(nc, mem, "ones_by_head", [P, P]), tile(nc, mem, "swap_halves", [P, P])
        raw, sq, rs, nrm, t1, t2, res = (tile(nc, mem, f"a_{x}", [P, 2, BANK]) for x in ("raw", "sq", "rs", "nrm", "t1", "t2", "res"))
        with nc.Block() as block:
            @block.sync
            def _(sp):
                for t in range(TILES):
                    sp.dma_start(w[:, t], d["w_qk"][t]).then_inc(w_in, 16)
                for dst, src in ((cos, "cos_a"), (sin, "sin_a"), (by_head, "by_head"), (swap, "swap_a")):
                    sp.dma_start(dst[:], d[src]).then_inc(tabs_in, 16)
                for u, (t, a, n) in enumerate(units):
                    sp.wait_ge(roped, u + 1)
                    sp.dma_start(sc.qk_a[t][:, a:a + n], res[:, u % 2, 0:n]).then_inc(stored[u % 2], 16)
                sp.wait_ge(stored[0], 16 * ((U + 1) // 2))
                sp.wait_ge(stored[1], 16 * (U // 2))

            @block.tensor
            def _(pe):
                pe.wait_ge(w_in, 16 * TILES)
                pe.wait_ge(tabs_in, 64)
                for step in range(U + 2):
                    if step < U:
                        t, a, n = units[step]
                        if step >= 3:
                            pe.wait_ge(squared, step - 2)
                        for k in range(KT):
                            mm = pe.matmul(g.ps[:, step % 3, 0:n], w[:, t, k, :], g.h[:, k, a:a + n], start=(k == 0), stop=(k == KT - 1))
                        mm.then_inc(product, 1)
                    if 0 <= step - 1 < U:
                        v = step - 1
                        n = units[v][2]
                        pe.wait_ge(squared, v + 1)
                        if v >= 2:
                            pe.wait_ge(logged, v - 1)
                        pe.matmul(g.ps[:, 3 + v % 2, 0:n], by_head[:], sq[:, v % 2, 0:n], start=True, stop=True).then_inc(meaned, 1)
                    if 0 <= step - 2 < U:
                        v = step - 2
                        n = units[v][2]
                        pe.wait_ge(normed, v + 1)
                        if v >= 2:
                            pe.wait_ge(halves, 2 * (v - 1))
                        pe.matmul(g.ps[:, 5 + v % 2, 0:n], swap[:], nrm[:, v % 2, 0:n], start=True, stop=True).then_inc(rotated, 1)

            @block.scalar
            def _(act):
                act.preload_act_table_set("natural_log_exp_and_others")
                for step in range(U + 1):
                    if step < U:
                        n = units[step][2]
                        act.wait_ge(product, step + 1)
                        if step >= 2:
                            act.wait_ge(normed, step - 1)
                            act.wait_ge(meaned, step - 1)
                        act.activation(raw[:, step % 2, 0:n], g.ps[:, step % 3, 0:n], ACT.Copy).then_inc(raw_out, 1)
                        act.activation(sq[:, step % 2, 0:n], g.ps[:, step % 3, 0:n], ACT.Square).then_inc(squared, 1)
                    if step >= 1:
                        v = step - 1
                        n = units[v][2]
                        act.wait_ge(meaned, v + 1)
                        if v >= 2:
                            act.wait_ge(normed, v - 1)
                        act.activation(rs[:, v % 2, 0:n], g.ps[:, 3 + v % 2, 0:n], ACT.Ln, bias=g.eps[:], scale=1.0 / A_DIM).then_inc(logged, 1)
                        act.wait_ge(logged, v + 1)
                        act.activation(rs[:, v % 2, 0:n], rs[:, v % 2, 0:n], ACT.Exp, scale=-0.5).then_inc(rstd, 1)

            @block.vector
            def _(dve):
                dve.wait_ge(tabs_in, 64)
                for step in range(1, U + 2):
                    if step <= U:
                        v = step - 1
                        t, a, n = units[v]
                        dve.wait_ge(raw_out, v + 1)
                        dve.wait_ge(rstd, v + 1)
                        if v >= 2:
                            dve.wait_ge(rotated, v - 1)
                            dve.wait_ge(halves, 2 * (v - 1))
                        gain = vec(g, "gain_k" if t == 0 else "gain_q")
                        dve.scalar_tensor_tensor(out=nrm[:, v % 2, 0:n], in0=raw[:, v % 2, 0:n], scalar=gain,
                                                 in1=rs[:, v % 2, 0:n], op0=ALU.mult, op1=ALU.mult).then_inc(normed, 1)
                    if step >= 2:
                        v = step - 2
                        t, a, n = units[v]
                        dve.wait_ge(normed, v + 1)
                        dve.wait_ge(rotated, v + 1)
                        if v >= 2:
                            dve.wait_ge(roped, v - 1)
                            dve.wait_ge(stored[v % 2], 16 * (v // 2))
                        dve.tensor_tensor(t1[:, v % 2, 0:n], nrm[:, v % 2, 0:n], cos[:, a:a + n], ALU.mult).then_inc(halves, 1)
                        dve.tensor_tensor(t2[:, v % 2, 0:n], g.ps[:, 5 + v % 2, 0:n], sin[:, a:a + n], ALU.mult).then_inc(halves, 1)
                        dve.wait_ge(halves, 2 * (v + 1))
                        dve.tensor_tensor(res[:, v % 2, 0:n], t1[:, v % 2, 0:n], t2[:, v % 2, 0:n], ALU.add).then_inc(roped, 1)

    q_low = tile(nc, sc.mem, "q_low", [P, 2, TOK])
    kv_low = tile(nc, sc.mem, "kv_low", [P, TOK])
    groups = [((0, 1), (q_low[:, 0, :], q_low[:, 1, :]), ("mlq", 0), 256), ((2,), (kv_low[:],), ("mlkv", 0), 128)]
    gunits = [(gi, a, n) for gi in range(2) for a, n in CHUNKS]
    names = "w_in tabs_in product squared meaned logged rstd normed key_raw key_read key_rotated key_halves key_roped key_stored v_product v_out v_stored0 v_stored1"
    with stage(nc, names) as (mem, sems):
        (w_in, tabs_in, product, squared, meaned, logged, rstd, normed, key_raw, key_read, key_rotated, key_halves,
         key_roped, key_stored, v_product, v_out) = sems[:16]
        v_stored = sems[16:]
        w = tile(nc, mem, "w_low", [P, 3, KT, P])
        w_key = tile(nc, mem, "w_key", [P, KT, B_ROPE])
        w_v = tile(nc, mem, "w_v", [P, KT, P])
        cos, sin = tile(nc, mem, "cos_b", [P, TOK]), tile(nc, mem, "sin_b", [P, TOK])
        swap = tile(nc, mem, "swap_b", [P, P])
        sq = tile(nc, mem, "b_sq", [P, 3, BANK])
        raw = tile(nc, mem, "b_raw", [P, 3, BANK])
        rs = tile(nc, mem, "b_rs", [P, 2, BANK])
        key, kt1, kt2 = (tile(nc, mem, f"key_{x}", [P, TOK]) for x in ("raw", "t1", "t2"))
        vt = tile(nc, mem, "v_tile", [P, 2, P])
        tiles = [(gi, ti, a, n) for gi, a, n in gunits for ti in range(len(groups[gi][0]))]
        T = len(tiles)
        last_of = [max(i for i, x in enumerate(tiles) if (x[0], x[2]) == (gi, a)) for gi, a, n in gunits]
        rows = slice(B_NOPE, B_DK)
        with nc.Block() as block:
            @block.sync
            def _(sp):
                sp.dma_start(w[:], d["w_low"]).then_inc(w_in, 16)
                sp.dma_start(w_key[:], d["w_key"]).then_inc(w_in, 16)
                sp.dma_start(w_v[:], d["w_v_a"]).then_inc(w_in, 16)
                for dst, src in ((cos, "cos_b"), (sin, "sin_b"), (swap, "swap_b")):
                    sp.dma_start(dst[:], d[src]).then_inc(tabs_in, 16)
                sp.wait_ge(key_roped, C)
                for h in range(B_HEADS):
                    sp.dma_start(sc.k_b[h][rows, :], key[rows, :]).then_inc(key_stored, 16)
                for j in range(KTILES):
                    sp.wait_ge(v_out, j + 1)
                    sp.dma_start(sc.v_a[:, j, :], vt[:, j % 2, :]).then_inc(v_stored[j % 2], 16)
                sp.wait_ge(key_stored, 16 * B_HEADS)
                for s in range(2):
                    sp.wait_ge(v_stored[s], 16 * (KTILES // 2))

            @block.tensor
            def _(pe):
                pe.wait_ge(w_in, 48)
                pe.wait_ge(tabs_in, 48)
                for c, (a, n) in enumerate(CHUNKS):
                    for k in range(KT):
                        mm = pe.matmul(g.ps[rows, c, 0:n], w_key[:, k, :], g.h[:, k, a:a + n], start=(k == 0), stop=(k == KT - 1))
                    mm.then_inc(key_raw, 1)
                def mean(v):
                    gi, a, n = gunits[v]
                    pe.wait_ge(squared, last_of[v] + 1)
                    if v >= 2:
                        pe.wait_ge(logged, v - 1)
                    first = last_of[v] + 1 - len(groups[gi][0])
                    for i in range(first, last_of[v] + 1):
                        mm = pe.matmul(g.ps[:, 6 + v % 2, 0:n], g.ones[:], sq[:, i % 3, 0:n], start=(i == first), stop=(i == last_of[v]))
                    mm.then_inc(meaned, 1)
                due = 0
                for i, (gi, ti, a, n) in enumerate(tiles):
                    if i >= 3:
                        pe.wait_ge(squared, i - 2)
                    for k in range(KT):
                        mm = pe.matmul(g.ps[:, 3 + i % 3, 0:n], w[:, groups[gi][0][ti], k, :], g.h[:, k, a:a + n], start=(k == 0), stop=(k == KT - 1))
                    mm.then_inc(product, 1)
                    if due < len(gunits) and last_of[due] < i:
                        mean(due)
                        due += 1
                while due < len(gunits):
                    mean(due)
                    due += 1
                for c, (a, n) in enumerate(CHUNKS):
                    pe.wait_ge(key_read, c + 1)
                    pe.matmul(g.ps[rows, c, 0:n], swap[rows, rows], key[rows, a:a + n], start=True, stop=True).then_inc(key_rotated, 1)
                for j in range(KTILES):
                    if j < 3:
                        pe.wait_ge(squared, T)
                    else:
                        pe.wait_ge(v_out, j - 2)
                    for k in range(KT):
                        mm = pe.matmul(g.ps[:, 3 + j % 3, 0:P], g.h[:, k, j * P:(j + 1) * P], w_v[:, k, :], start=(k == 0), stop=(k == KT - 1))
                    mm.then_inc(v_product, 1)

            @block.scalar
            def _(act):
                act.preload_act_table_set("natural_log_exp_and_others")
                for c, (a, n) in enumerate(CHUNKS):
                    act.wait_ge(key_raw, c + 1)
                    act.activation(key[rows, a:a + n], g.ps[rows, c, 0:n], ACT.Copy).then_inc(key_read, 1)
                due = 0
                def root(v):
                    gi, a, n = gunits[v]
                    act.wait_ge(meaned, v + 1)
                    if v >= 2:
                        act.wait_ge(normed, last_of[v - 2] + 1)
                    act.activation(rs[:, v % 2, 0:n], g.ps[:, 6 + v % 2, 0:n], ACT.Ln, bias=g.eps[:], scale=1.0 / groups[gi][3]).then_inc(logged, 1)
                    act.wait_ge(logged, v + 1)
                    act.activation(rs[:, v % 2, 0:n], rs[:, v % 2, 0:n], ACT.Exp, scale=-0.5).then_inc(rstd, 1)
                for i, (gi, ti, a, n) in enumerate(tiles):
                    act.wait_ge(product, i + 1)
                    if i >= 3:
                        act.wait_ge(normed, i - 2)
                        act.wait_ge(meaned, gunits.index((tiles[i - 3][0],) + tiles[i - 3][2:]) + 1)
                    act.activation(raw[:, i % 3, 0:n], g.ps[:, 3 + i % 3, 0:n], ACT.Copy).then_inc(key_read, 1)
                    act.activation(sq[:, i % 3, 0:n], g.ps[:, 3 + i % 3, 0:n], ACT.Square).then_inc(squared, 1)
                    if last_of[due] < i:
                        root(due)
                        due += 1
                while due < len(gunits):
                    root(due)
                    due += 1
                for j in range(KTILES):
                    act.wait_ge(v_product, j + 1)
                    if j >= 2:
                        act.wait_ge(v_stored[j % 2], 16 * (j // 2))
                    act.activation(vt[:, j % 2, :], g.ps[:, 3 + j % 3, 0:P], ACT.Copy).then_inc(v_out, 1)

            @block.vector
            def _(dve):
                for v, (gi, a, n) in enumerate(gunits):
                    dve.wait_ge(rstd, v + 1)
                    size = len(groups[gi][0])
                    for ti in range(size):
                        i = last_of[v] + 1 - size + ti
                        name, at = groups[gi][2]
                        dve.wait_ge(key_read, C + i + 1)
                        dve.scalar_tensor_tensor(out=groups[gi][1][ti][:, a:a + n], in0=raw[:, i % 3, 0:n], scalar=vec(g, name, at + ti),
                                                 in1=rs[:, v % 2, 0:n], op0=ALU.mult, op1=ALU.mult).then_inc(normed, 1)
                dve.wait_ge(tabs_in, 48)
                for c, (a, n) in enumerate(CHUNKS):
                    dve.wait_ge(key_rotated, c + 1)
                    dve.tensor_tensor(kt1[rows, a:a + n], key[rows, a:a + n], cos[rows, a:a + n], ALU.mult).then_inc(key_halves, 1)
                    dve.tensor_tensor(kt2[rows, a:a + n], g.ps[rows, c, 0:n], sin[rows, a:a + n], ALU.mult).then_inc(key_halves, 1)
                    dve.wait_ge(key_halves, 2 * (c + 1))
                    dve.tensor_tensor(key[rows, a:a + n], kt1[rows, a:a + n], kt2[rows, a:a + n], ALU.add).then_inc(key_roped, 1)

    names = "w_in w_head0 w_head1 tabs_in product raw_out rotated halves roped q_stored0 q_stored1 k_product k_out k_stored0 k_stored1 v_product v_out v_stored0 v_stored1"
    units = [(h, c, a, n) for h in range(B_HEADS) for c, (a, n) in enumerate(CHUNKS)]
    U = len(units)
    with stage(nc, names) as (mem, sems):
        (w_in, w_head0, w_head1, tabs_in, product, raw_out, rotated, halves, roped, q_stored0, q_stored1, k_product, k_out,
         k_stored0, k_stored1, v_product, v_out, v_stored0, v_stored1) = sems
        q_stored, k_stored, v_stored = (q_stored0, q_stored1), (k_stored0, k_stored1), (v_stored0, v_stored1)
        wq = tile(nc, mem, "w_q_up", [P, 2, B_HEADS * B_DK])
        wk = tile(nc, mem, "w_k_up", [P, B_HEADS * B_NOPE])
        wv = tile(nc, mem, "w_v_up", [P, B_HEADS * B_V])
        cos, sin = tile(nc, mem, "cos_b", [P, TOK]), tile(nc, mem, "sin_b", [P, TOK])
        swap = tile(nc, mem, "swap_b", [P, P])
        raw, t1, t2, res, kres, vres = (tile(nc, mem, f"u_{x}", [P, 2, BANK]) for x in ("raw", "t1", "t2", "res", "k", "v"))
        top = slice(0, B_DK)
        nope = slice(0, B_NOPE)
        with nc.Block() as block:
            @block.sync
            def _(sp):
                for dst, src in ((wq, "w_q_up"), (wk, "w_k_up"), (wv, "w_v_up"), (cos, "cos_b"), (sin, "sin_b"), (swap, "swap_b")):
                    sp.dma_start(dst[:], d[src]).then_inc(tabs_in, 16)
                for j in range(KTILES):
                    sp.wait_ge(v_out, j + 1)
                    sp.dma_start(sc.v_b[:, j, :], vres[:, j % 2, :]).then_inc(v_stored[j % 2], 16)
                for u, (h, c, a, n) in enumerate(units):
                    sp.wait_ge(k_out, u + 1)
                    sp.dma_start(sc.k_b[h][nope, a:a + n], kres[nope, u % 2, 0:n]).then_inc(k_stored[u % 2], 16)
                    sp.wait_ge(roped, u + 1)
                    sp.dma_start(sc.q_b[h][:, a:a + n], res[top, u % 2, 0:n]).then_inc(q_stored[u % 2], 16)
                for s in range(2):
                    sp.wait_ge(v_stored[s], 16 * (KTILES // 2))
                    sp.wait_ge(k_stored[s], 16 * (U // 2))
                    sp.wait_ge(q_stored[s], 16 * (U // 2))

            @block.tensor
            def _(pe):
                pe.wait_ge(tabs_in, 96)
                for j in range(KTILES):
                    if j >= 2:
                        pe.wait_ge(v_out, j - 1)
                    pe.matmul(g.ps[:, 6 + j % 2, :], kv_low[:, j * P:(j + 1) * P], wv[:], start=True, stop=True).then_inc(v_product, 1)
                for step in range(U + 1):
                    if step < U:
                        h, c, a, n = units[step]
                        if step >= 2:
                            pe.wait_ge(raw_out, step - 1)
                        for k in range(2):
                            mm = pe.matmul(g.ps[top, step % 2, 0:n], wq[:, k, h * B_DK:(h + 1) * B_DK], q_low[:, k, a:a + n], start=(k == 0), stop=(k == 1))
                        mm.then_inc(product, 1)
                        if step >= 2:
                            pe.wait_ge(k_out, step - 1)
                        pe.matmul(g.ps[nope, 4 + step % 2, 0:n], wk[:, h * B_NOPE:(h + 1) * B_NOPE], kv_low[:, a:a + n], start=True, stop=True).then_inc(k_product, 1)
                    if step >= 1:
                        v = step - 1
                        n = units[v][3]
                        pe.wait_ge(raw_out, v + 1)
                        if v >= 2:
                            pe.wait_ge(halves, 2 * (v - 1))
                        pe.matmul(g.ps[top, 2 + v % 2, 0:n], swap[top, top], raw[top, v % 2, 0:n], start=True, stop=True).then_inc(rotated, 1)

            @block.scalar
            def _(act):
                for j in range(KTILES):
                    act.wait_ge(v_product, j + 1)
                    if j >= 2:
                        act.wait_ge(v_stored[j % 2], 16 * (j // 2))
                    act.activation(vres[:, j % 2, :], g.ps[:, 6 + j % 2, :], ACT.Copy).then_inc(v_out, 1)
                for u, (h, c, a, n) in enumerate(units):
                    act.wait_ge(product, u + 1)
                    if u >= 2:
                        act.wait_ge(halves, 2 * (u - 1))
                        act.wait_ge(rotated, u - 1)
                    act.activation(raw[top, u % 2, 0:n], g.ps[top, u % 2, 0:n], ACT.Copy, scale=B_SCALE).then_inc(raw_out, 1)
                    act.wait_ge(k_product, u + 1)
                    if u >= 2:
                        act.wait_ge(k_stored[u % 2], 16 * (u // 2))
                    act.activation(kres[nope, u % 2, 0:n], g.ps[nope, 4 + u % 2, 0:n], ACT.Copy).then_inc(k_out, 1)

            @block.vector
            def _(dve):
                dve.wait_ge(tabs_in, 96)
                for v, (h, c, a, n) in enumerate(units):
                    dve.wait_ge(raw_out, v + 1)
                    dve.wait_ge(rotated, v + 1)
                    if v >= 2:
                        dve.wait_ge(roped, v - 1)
                        dve.wait_ge(q_stored[v % 2], 16 * (v // 2))
                    dve.tensor_tensor(t1[top, v % 2, 0:n], raw[top, v % 2, 0:n], cos[top, a:a + n], ALU.mult).then_inc(halves, 1)
                    dve.tensor_tensor(t2[top, v % 2, 0:n], g.ps[top, 2 + v % 2, 0:n], sin[top, a:a + n], ALU.mult).then_inc(halves, 1)
                    dve.wait_ge(halves, 2 * (v + 1))
                    dve.tensor_tensor(res[top, v % 2, 0:n], t1[top, v % 2, 0:n], t2[top, v % 2, 0:n], ALU.add).then_inc(roped, 1)


def attention(nc, g, sc, out):
    PAIRS = 4
    QB = 256
    steps = [(b, h, t) for b in range(TOK // QB) for h in range(2) for t in range(2)]
    S, B = len(steps), TOK // QB
    PER_BLOCK = S // B
    ALL = [(pair, i) for pair in range(PAIRS) for i in range(S)]
    N = len(ALL)

    def keys_of(b):
        return (0, KTILES) if b < LAT // QB else (LAT // P, KTILES)

    def block_of(x):
        return steps[ALL[x][1]][0]

    def width(x):
        lo, hi = keys_of(block_of(x))
        return (hi - lo) * P

    def turns(x):
        lo, hi = keys_of(block_of(x))
        return [(i, min(i + 4, hi)) for i in range(lo, hi, 4)]

    use = {}
    for x in range(2, N + 3):
        if x > 2 and (x - 2) % PER_BLOCK == 0:
            use["mix", (x - 3) // PER_BLOCK] = len(use)
        if x - 2 < N:
            for j in range(len(turns(x - 2))):
                use["turn", x - 2, j] = len(use)

    def last_turn(x):
        return use["turn", x, len(turns(x)) - 1]

    for kind in range(2):
        rows = slice(0, (P, B_DK)[kind])
        items = (((0, 0), (0, 1), (1, 0)), ((0, 0), (0, 1), (1, 0), (1, 1)))[kind]
        I = len(items)
        COPIES = (2, 1)[kind]
        names = "raw_in0 raw_in1 v_in0 v_in1 rounded split scores maxed exped inverse probs filled emptied"
        with stage(nc, names) as (mem, sems):
            raw_in, v_in, (rounded, split, scores, maxed, exped, inverse, probs, filled, emptied) = sems[:2], sems[2:4], sems[4:]
            raw = tile(nc, mem, "qk_raw", [P, 2, TOK])
            heads = len(items) - 2
            q_hi, k_hi, k_lo = (tile_r(nc, mem, f"{x}", [P, 2, n, TOK]) for x, n in (("q_high", 2), ("k_high", heads), ("k_low", heads)))
            q_lo = q_hi if kind == 0 else tile_r(nc, mem, "q_low_part", [P, 2, 2, TOK])
            v = tile(nc, mem, "v_pair", [P, 2, KTILES, 2, B_V])
            p = tile(nc, mem, "probs", [P, 3, TOK])
            pt = tile(nc, mem, "probs_turned", [P, 2, 2, KTILES, QB])
            neg_max, total, inv = (tile(nc, mem, f"row_{x}", [P, 4]) for x in ("max", "sum", "inv"))

            def source(pair, item):
                which, h = item
                if kind == 0:
                    return sc.qk_a[1 + pair][64 * h:64 * h + 64, :] if which == 0 else sc.qk_a[0][64 * (pair // 2):64 * (pair // 2) + 64, :]
                return (sc.q_b, sc.k_b)[which][2 * pair + h]

            def split_at(x):
                pair, i = ALL[x]
                n, off = divmod(i - 5, 3)
                return (pair + 1, n) if off == 0 and 0 <= n < I and pair + 1 < PAIRS else None

            with nc.Block() as block:
                @block.sync
                def _(sp):
                    for pair in range(PAIRS):
                        for n in range(I):
                            m = pair * I + n
                            if m >= 2:
                                sp.wait_ge(split, m - 1)
                            for c in range(COPIES):
                                at = rows if kind == 1 else slice(64 * c, 64 * c + 64)
                                sp.dma_start(raw[at, m % 2, :], source(pair, items[n])).then_inc(raw_in[m % 2], 16)
                        if pair >= 2:
                            sp.wait_ge(filled, use["mix", (pair - 1) * B - 1] + 1)
                        s = pair % 2
                        if kind == 0:
                            for h in range(2):
                                sp.dma_start(v[:, s, :, h, :], sc.v_a[:, :, 64 * (pair // 2):64 * (pair // 2) + 64]).then_inc(v_in[s], 16)
                        else:
                            sp.dma_start(v[:, s], sc.v_b[:, :, 128 * pair:128 * pair + 128].rearrange("p j (h n) -> p j h n", h=2)).then_inc(v_in[s], 16)

                @block.tensor
                def _(pe):
                    def scores_of(x):
                        pair, i = ALL[x]
                        b, h, t = steps[i]
                        s, q0 = pair % 2, b * QB + t * P
                        qs = slice(q0, q0 + P)
                        lo, hi = keys_of(b)
                        parts = [(a, min(BANK, hi * P - a)) for a in range(lo * P, hi * P, BANK)]
                        if i == 0:
                            pe.wait_ge(split, I * (pair + 1))
                        if x >= 2:
                            pe.wait_ge(exped, x - 1)
                        kh = 0 if kind == 0 else h
                        passes = [(q_hi, k_hi), (q_hi, k_lo)] + ([(q_lo, k_hi)] if kind else [])
                        for j, (a, n) in enumerate(parts):
                            for m, (left, right) in enumerate(passes):
                                mm = pe.matmul(g.ps[:, 3 * (x % 2) + j, 0:n], left[rows, s, h, qs], right[rows, s, kh, a:a + n],
                                               start=(m == 0), stop=(m == len(passes) - 1))
                            if j == len(parts) - 1:
                                mm.then_inc(scores, 1)

                    def turn(x):
                        first = keys_of(block_of(x))[0]
                        for j, (lo, hi) in enumerate(turns(x)):
                            if j == 0:
                                pe.wait_ge(probs, x + 1)
                            r = use["turn", x, j]
                            if r >= 2:
                                pe.wait_ge(emptied, r - 1)
                            for kt in range(lo, hi):
                                mm = pe.transpose(g.ps[:, 6 + r % 2, (kt - lo) * P:(kt - lo + 1) * P], p[:, x % 3, (kt - first) * P:(kt - first + 1) * P], g.ident[:])
                            mm.then_inc(filled, 1)

                    def mix(y):
                        pair, b = divmod(y, B)
                        lo, hi = keys_of(b)
                        r = use["mix", y]
                        pe.wait_ge(emptied, r)
                        pe.wait_ge(v_in[pair % 2], 16 * COPIES * (pair // 2 + 1))
                        for kt in range(lo, hi):
                            for h in range(2):
                                mm = pe.matmul(g.ps[64 * h:64 * h + 64, 6 + r % 2, 0:QB], v[:, pair % 2, kt, h, :], pt[:, y % 2, h, kt, :],
                                               start=(kt == lo), stop=(kt == hi - 1))
                        mm.then_inc(filled, 1)

                    for x in range(N + 3):
                        if x < N:
                            scores_of(x)
                        if x > 2 and (x - 2) % PER_BLOCK == 0:
                            mix((x - 3) // PER_BLOCK)
                        if 2 <= x < N + 2:
                            turn(x - 2)

                @block.vector
                def _(dve):
                    def split_item(pair, n):
                        which, h = items[n]
                        m, s = pair * I + n, pair % 2
                        dve.wait_ge(rounded, m + 1)
                        if which == 1:
                            low, high, at = k_lo, k_hi, rows
                        else:
                            low, high, at = q_lo, q_hi, (slice(64, P) if kind == 0 else rows)
                        dve.tensor_tensor(low[at, s, h, :], raw[at, m % 2, :], high[at, s, h, :], ALU.subtract).then_inc(split, 1)

                    for n in range(I):
                        split_item(0, n)
                    for x in range(N + 1):
                        if x < N:
                            dve.wait_ge(scores, x + 1)
                            if x >= 4:
                                dve.wait_ge(exped, x - 3)
                            flat = g.ps[:, 3 * (x % 2):3 * (x % 2) + 3, :].rearrange("p b n -> p (b n)")[:, 0:width(x)]
                            dve.tensor_reduce(neg_max[:, x % 4:x % 4 + 1], flat, AX.X, ALU.max, negate=True).then_inc(maxed, 1)
                        if x >= 1:
                            y = x - 1
                            dve.wait_ge(exped, y + 1)
                            if y >= 4:
                                dve.wait_ge(probs, y - 3)
                            dve.reciprocal(inv[:, y % 4:y % 4 + 1], total[:, y % 4:y % 4 + 1]).then_inc(inverse, 1)
                            dve.wait_ge(inverse, y + 1)
                            dve.tensor_scalar(p[:, y % 3, 0:width(y)], p[:, y % 3, 0:width(y)], inv[:, y % 4:y % 4 + 1], None, ALU.mult).then_inc(probs, 1)
                        if x < N and split_at(x):
                            split_item(*split_at(x))

                @block.scalar
                def _(act):
                    def round_item(pair, n):
                        which, h = items[n]
                        m, s = pair * I + n, pair % 2
                        act.wait_ge(raw_in[m % 2], 16 * COPIES * (m // 2 + 1))
                        if pair >= 2:
                            act.wait_ge(scores, (pair - 1) * S)
                        act.activation((q_hi, k_hi)[which][rows, s, h, :], raw[rows, m % 2, :], ACT.Copy).then_inc(rounded, 1)

                    def turn_out(x, j):
                        pair, i = ALL[x]
                        b, h, t = steps[i]
                        lo, hi = turns(x)[j]
                        y = pair * B + b
                        r = use["turn", x, j]
                        act.wait_ge(filled, r + 1)
                        act.activation(pt[:, y % 2, h, lo:hi, t * P:(t + 1) * P],
                                       g.ps[:, 6 + r % 2, 0:(hi - lo) * P].rearrange("p (k n) -> p k n", n=P), ACT.Copy).then_inc(emptied, 1)

                    def mix_out(y):
                        pair, b = divmod(y, B)
                        r = use["mix", y]
                        act.wait_ge(filled, r + 1)
                        act.activation(out[:, kind * PAIRS + pair, b * QB:(b + 1) * QB], g.ps[:, 6 + r % 2, 0:QB], ACT.Copy).then_inc(emptied, 1)

                    for n in range(I):
                        round_item(0, n)
                    for x in range(N + 3):
                        if x > 2 and (x - 2) % PER_BLOCK == 0:
                            mix_out((x - 3) // PER_BLOCK)
                        if 2 <= x < N + 2:
                            for j in range(len(turns(x - 2))):
                                turn_out(x - 2, j)
                        if x < N:
                            act.wait_ge(maxed, x + 1)
                            if x >= 3:
                                act.wait_ge(filled, last_turn(x - 3) + 1)
                            if x >= 4:
                                act.wait_ge(inverse, x - 3)
                            flat = g.ps[:, 3 * (x % 2):3 * (x % 2) + 3, :].rearrange("p b n -> p (b n)")[:, 0:width(x)]
                            act.activation(p[:, x % 3, 0:width(x)], flat, ACT.Exp, bias=neg_max[:, x % 4:x % 4 + 1], accum_out=total[:, x % 4:x % 4 + 1]).then_inc(exped, 1)
                            if split_at(x):
                                round_item(*split_at(x))


def project_out(nc, g, src, w, out, tokens):
    PIECES, BANKS = KT, 4
    spans = chunks_of(tokens)
    C = len(spans)
    units = [(t, a, n) for t in range(PIECES) for a, n in spans]
    U = len(units)
    total = g.ps[:, SQUARES_AT:SQUARES_AT + 3, :].rearrange("p b n -> p (b n)")
    high, low = g.high, g.low
    with stage(nc, "raw_in0 raw_in1 w_rounded w_split src_rounded src_split product copied squared square_used") as (mem, sems):
        w_sems, (src_rounded, src_split, product, copied, squared, square_used) = sems[:4], sems[4:]
        ring = WeightRing(nc, mem, w_sems, product, [C * (t + 1) for t in range(PIECES)])
        sq = tile(nc, mem, "out_square", [P, 2, BANK])
        with nc.Block() as block:
            @block.sync
            def _(sp):
                for t in range(PIECES):
                    ring.load(sp, t, w[t])

            @block.tensor
            def _(pe):
                def add_squares(u):
                    t, a, n = units[u]
                    pe.wait_ge(squared, u + 1)
                    pe.matmul(total[:, a:a + n], g.ones[:], sq[:, u % 2, 0:n], start=(t == 0), stop=(t == PIECES - 1)).then_inc(square_used, 1)

                pe.wait_ge(ring.split, 1)
                for k in range(KT):
                    pe.wait_ge(src_split, k + 1)
                    for c, (a, n) in enumerate(spans):
                        for i, (x, y) in enumerate(((ring.high, high), (ring.high, low), (ring.low, high))):
                            mm = pe.matmul(g.ps[:, c, 0:n], x[:, 0, k, :], y[:, k, a:a + n], start=(k == 0 and i == 0), stop=(k == KT - 1 and i == 2))
                        if k == KT - 1:
                            mm.then_inc(product, 1)
                for u in range(C, U):
                    t, a, n = units[u]
                    if u % C == 0:
                        pe.wait_ge(ring.split, t + 1)
                    if u >= BANKS:
                        pe.wait_ge(squared, u - BANKS + 1)
                    ring.product_of(pe, g.ps[:, u % BANKS, 0:n], t, high, low, a, n).then_inc(product, 1)
                    if u == C:
                        for v in range(C):
                            add_squares(v)
                    else:
                        add_squares(u - 1)
                add_squares(U - 1)

            @block.scalar
            def _(act):
                ring.round_piece(act, 0)
                for k in range(KT):
                    act.activation(high[:, k, 0:tokens], src[:, k, 0:tokens], ACT.Copy).then_inc(src_rounded, 1)
                for u, (t, a, n) in enumerate(units):
                    if u % C == 0:
                        ring.round_piece(act, t + 1)
                    act.wait_ge(product, u + 1)
                    act.activation(out[:, t, a:a + n], g.ps[:, u % BANKS, 0:n], ACT.Copy).then_inc(copied, 1)
                    if u >= 2:
                        act.wait_ge(square_used, u - 1)
                    act.activation(sq[:, u % 2, 0:n], g.ps[:, u % BANKS, 0:n], ACT.Square).then_inc(squared, 1)

            @block.vector
            def _(dve):
                ring.split_piece(dve, 0)
                for k in range(KT):
                    dve.wait_ge(src_rounded, k + 1)
                    dve.tensor_tensor(low[:, k, 0:tokens], src[:, k, 0:tokens], high[:, k, 0:tokens], ALU.subtract).then_inc(src_split, 1)
                for t in range(1, PIECES):
                    ring.split_piece(dve, t)


def project_mamba(nc, g, d, high, low, xbc, gate, dt, adt):
    TILES, Z_TILES, BANKS = 8, 4, 4
    units = [(t, a, n) for t in range(TILES) for a, n in CHUNKS]
    zunits = [(t, a, n) for t in range(Z_TILES) for a, n in CHUNKS[:2]]
    U, C = len(units), len(CHUNKS)
    WIDE = LAT + CTX + 4
    LAT_AT, CTX_AT = 1, LAT + 3
    names = ("raw_in0 raw_in1 w_rounded w_split w_dt dt_rounded dt_split product dt_product raw_out z_out padded conv conv_read dt_out steps "
             "magnitude decayed logged a_exp tapped")
    with stage(nc, names) as (mem, sems):
        w_sems, (w_dt, dt_rounded, dt_split, product, dt_product, raw_out, z_out, padded, conv, conv_read, dt_out, steps,
               magnitude, decayed, logged, a_exp, tapped) = sems[:4], sems[4:]
        ring = WeightRing(nc, mem, w_sems, product, [C * (t + 1) for t in range(TILES)] + [U + 2 * (t + 1) for t in range(Z_TILES)])
        wdt, wdt_high, wdt_low = tile(nc, mem, "w_dt", [P, KT, 16]), tile_r(nc, mem, "w_dt_high", [P, KT, 16]), tile_r(nc, mem, "w_dt_low", [P, KT, 16])
        raw = tile(nc, mem, "xbc_raw", [P, 2, WIDE])
        acc = tile(nc, mem, "conv_acc", [P, 2, WIDE])
        T16 = [P, KTILES, 16]
        mag, ex, one_e, lg, zero, den = (tile(nc, mem, f"dt_{x}", T16) for x in ("mag", "exp", "one", "log", "zero", "den"))
        rate = tile(nc, mem, "a_rate", [P, 16])
        over_tiles = lambda ap: ap.unsqueeze(1).to_broadcast(T16)
        with nc.Block() as block:
            def silu_conv(act, t):
                act.wait_ge(conv, t + 1)
                act.activation(xbc[:, t, 0:LAT], acc[:, t % 2, LAT_AT:LAT_AT + LAT], ACT.Silu, bias=vec(g, "conv_b", t)).then_inc(conv_read, 1)
                act.activation(xbc[:, t, LAT:TOK], acc[:, t % 2, CTX_AT:CTX_AT + CTX], ACT.Silu, bias=vec(g, "conv_b", t)).then_inc(conv_read, 1)

            @block.sync
            def _(sp):
                sp.dma_start(wdt[:], d["w_dt"]).then_inc(w_dt, 16)
                for t in range(TILES + Z_TILES):
                    ring.load(sp, t, d["w_xbc"][t] if t < TILES else d["w_z"][t - TILES])

            @block.tensor
            def _(pe):
                pe.wait_ge(dt_split, 1)
                for j in range(KTILES):
                    for k in range(KT):
                        for i, (x, y) in enumerate(((high, wdt_high), (high, wdt_low), (low, wdt_high))):
                            mm = pe.matmul(g.ps[:, 7, j * 16:(j + 1) * 16], x[:, k, j * P:(j + 1) * P], y[:, k, :],
                                           start=(k == 0 and i == 0), stop=(k == KT - 1 and i == 2))
                mm.then_inc(dt_product, 1)
                for u, (t, a, n) in enumerate(units):
                    if u % C == 0:
                        pe.wait_ge(ring.split, t + 1)
                    if u >= BANKS:
                        pe.wait_ge(raw_out, u - BANKS + 1)
                    ring.product_of(pe, g.ps[:, u % BANKS, 0:n], t, high, low, a, n).then_inc(product, 1)
                for u, (t, a, n) in enumerate(zunits):
                    if u % 2 == 0:
                        pe.wait_ge(ring.split, TILES + t + 1)
                    if u >= 2:
                        pe.wait_ge(z_out, u - 1)
                    ring.product_of(pe, g.ps[:, 4 + u % 2, 0:n], TILES + t, high, low, a, n).then_inc(product, 1)

            @block.scalar
            def _(act):
                act.preload_act_table_set("natural_log_exp_and_others")
                act.wait_ge(w_dt, 16)
                act.activation(wdt_high[:], wdt[:], ACT.Copy).then_inc(dt_rounded, 1)
                ring.round_piece(act, 0)
                act.wait_ge(padded, 1)
                for u, (t, a, n) in enumerate(units):
                    if u % C == 0:
                        ring.round_piece(act, t + 1)
                    act.wait_ge(product, u + 1)
                    if t >= 2 and u % C == 0:
                        act.wait_ge(conv, t - 1)
                    at = LAT_AT + a if a < LAT else CTX_AT + a - LAT
                    act.activation(raw[:, t % 2, at:at + n], g.ps[:, u % BANKS, 0:n], ACT.Copy).then_inc(raw_out, 1)
                    if u % C == C - 1 and t >= 1:
                        silu_conv(act, t - 1)
                    if u == C - 1:
                        act.wait_ge(steps, 1)
                        act.activation(mag[:], dt[:], ACT.Abs).then_inc(magnitude, 1)
                        act.wait_ge(magnitude, 1)
                        act.activation(ex[:], mag[:], ACT.Exp, scale=-1.0).then_inc(decayed, 1)
                        act.activation(rate[:], vec(g, "a_log", 0, 16), ACT.Exp).then_inc(a_exp, 1)
                    if u == 2 * C - 1:
                        act.wait_ge(steps, 2)
                        act.activation(lg[:], one_e[:], ACT.Ln).then_inc(logged, 1)
                silu_conv(act, TILES - 1)
                for u, (t, a, n) in enumerate(zunits):
                    if u % 2 == 0:
                        ring.round_piece(act, TILES + t + 1)
                    act.wait_ge(product, U + u + 1)
                    act.activation(gate[:, t, a:a + n], g.ps[:, 4 + u % 2, 0:n], ACT.Silu).then_inc(z_out, 1)

            @block.vector
            def _(dve):
                dve.wait_ge(dt_rounded, 1)
                dve.tensor_tensor(wdt_low[:], wdt[:], wdt_high[:], ALU.subtract).then_inc(dt_split, 1)
                ring.split_piece(dve, 0)
                dve.memset(raw[:], 0.0).then_inc(padded, 1)
                dve.wait_ge(dt_product, 1)
                dps = g.ps[:, 7, 0:160].rearrange("p (j c) -> p j c", c=16)
                dve.tensor_tensor(dt[:], dps, over_tiles(vec(g, "dt_bias", 0, 16)), ALU.add).then_inc(steps, 1)
                for t in range(TILES):
                    ring.split_piece(dve, t + 1)
                    if t == 1:
                        dve.wait_ge(decayed, 1)
                        dve.tensor_scalar(one_e[:], ex[:], 1.0, None, ALU.add).then_inc(steps, 1)
                    if t == 2:
                        dve.wait_ge(steps, 2)
                        dve.tensor_scalar(zero[:], one_e[:], 1.0, None, ALU.is_equal).then_inc(steps, 1)
                        dve.wait_ge(steps, 3)
                        dve.scalar_tensor_tensor(out=den[:], in0=one_e[:], scalar=-1.0, in1=zero[:], op0=ALU.add, op1=ALU.add).then_inc(steps, 1)
                        dve.wait_ge(steps, 4)
                        dve.reciprocal(den[:], den[:]).then_inc(steps, 1)
                        dve.wait_ge(logged, 1)
                        dve.tensor_tensor(lg[:], lg[:], zero[:], ALU.add).then_inc(steps, 1)
                        dve.wait_ge(steps, 6)
                        dve.tensor_tensor(lg[:], lg[:], den[:], ALU.mult).then_inc(steps, 1)
                        dve.wait_ge(steps, 7)
                        dve.tensor_tensor(lg[:], lg[:], ex[:], ALU.mult).then_inc(steps, 1)
                        dve.wait_ge(steps, 8)
                        dve.scalar_tensor_tensor(out=dt[:], in0=dt[:], scalar=0.0, in1=lg[:], op0=ALU.max, op1=ALU.add).then_inc(steps, 1)
                        dve.wait_ge(a_exp, 1)
                        dve.tensor_scalar(rate[:], rate[:], -1.0, None, ALU.mult).then_inc(steps, 1)
                        dve.wait_ge(steps, 10)
                        dve.tensor_tensor(adt[:], dt[:], over_tiles(rate[:]), ALU.mult).then_inc(steps, 1)
                    dve.wait_ge(raw_out, C * (t + 1))
                    if t >= 2:
                        dve.wait_ge(conv_read, 2 * (t - 1))
                    out, n = acc[:, t % 2, 1:WIDE - 1], WIDE - 2
                    tap = lambda i: vec(g, "conv_w", i * TILES + t)
                    dve.tensor_scalar(out, raw[:, t % 2, 0:n], tap(0), None, ALU.mult).then_inc(tapped, 1)
                    dve.wait_ge(tapped, 2 * t + 1)
                    dve.scalar_tensor_tensor(out=out, in0=raw[:, t % 2, 1:1 + n], scalar=tap(1), in1=out, op0=ALU.mult, op1=ALU.add).then_inc(tapped, 1)
                    dve.wait_ge(tapped, 2 * t + 2)
                    dve.scalar_tensor_tensor(out=out, in0=raw[:, t % 2, 2:2 + n], scalar=tap(2), in1=out, op0=ALU.mult, op1=ALU.add).then_inc(conv, 1)
                for t in range(TILES, TILES + Z_TILES):
                    ring.split_piece(dve, t + 1)


def scan_states(nc, g, d, xbc, gate, dt, adt, out):
    CH, H, HD, G = P, 8, 64, 2
    LATC, NC = LAT // CH, TOK // CH
    fwd = list(range(LATC, NC)) + list(range(LATC))
    bwd = list(range(NC - 1, LATC - 1, -1)) + list(range(LATC - 1, -1, -1))
    units = [(dr, c) for pair in zip(fwd, bwd) for dr, c in enumerate(pair)]
    U = len(units)
    ys = [u for u, (dr, c) in enumerate(units) if c < LATC]
    Y = {u: i for i, u in enumerate(ys)}
    first_y = {}
    for u in ys:
        first_y.setdefault(units[u][1], u)

    xt = tile(nc, out.mem, "x_tokens", [P, NC, H * HD])
    bt = tile(nc, out.mem, "b_tokens", [P, NC, G * P])
    tri = tile(nc, out.mem, "triangles", [P, 2, P])
    with stage(nc, "tri_in turned read_out") as (mem, (tri_in, turned, read_out)):
        jobs = [(c, kind) for c in range(NC) for kind in range(2)]
        with nc.Block() as block:
            @block.sync
            def _(sp):
                sp.dma_start(tri[:], d["triangles"]).then_inc(tri_in, 16)
                sp.wait_ge(tri_in, 16)

            @block.tensor
            def _(pe):
                for i, (c, kind) in enumerate(jobs):
                    if i >= 4:
                        pe.wait_ge(read_out, i - 3)
                    for t in range(4 if kind == 0 else 2):
                        mm = pe.transpose(g.ps[:, i % 4, t * P:(t + 1) * P], xbc[:, 4 * kind + t, c * CH:(c + 1) * CH], g.ident[:])
                    mm.then_inc(turned, 1)

            @block.scalar
            def _(act):
                for i, (c, kind) in enumerate(jobs):
                    act.wait_ge(turned, i + 1)
                    dst = xt[:, c, :] if kind == 0 else bt[:, c, :]
                    act.activation(dst, g.ps[:, i % 4, 0:dst.shape[1]], ACT.Copy).then_inc(read_out, 1)

    names = ("spread sums acs_out act_read last_made seg_made decay_done clamped seg_exp decay_dt weighted x_dt c_scaled gram "
             "masked attended state_product kept state y_product y_out cleared")
    with stage(nc, names) as (mem, sems):
        (spread, sums, acs_out, act_read, last_made, seg_made, decay_done, clamped, seg_exp, decay_dt, weighted, x_dt,
         c_scaled, gram, masked, attended, state_product, kept, state, y_product, y_out, cleared) = sems
        HL = [P, H, CH]
        HX = [P, H, HD]
        au = tile(nc, mem, "adt_spread", [P, 2, H, CH])
        acs = tile(nc, mem, "acs_source", [P, 2, H])
        last = tile(nc, mem, "acs_left", [P, 2, H])
        dec = tile(nc, mem, "decay_source", [P, 2, H])
        whole = tile(nc, mem, "decay_chunk", [P, 2, H])
        xw = tile(nc, mem, "x_weighted", [P, 2, H, HD])
        xd = tile(nc, mem, "x_dt", [P, 2, H, HD])
        seg = tile(nc, mem, "segments", [P, 2, H, CH])
        ea = tile(nc, mem, "exp_acs", [P, 2, H, CH])
        gm = tile(nc, mem, "gram_masked", [P, 2, G, CH])
        st = tile(nc, mem, "states", [P, 2, 2, H, HD])
        tmp = tile(nc, mem, "state_kept", [P, H, HD])
        y = out.y
        acs_ps = g.ps[:, 0:2, :].rearrange("p b (h l) -> p (b h) l", l=CH)
        by_head = lambda ap, shape: ap.unsqueeze(2).to_broadcast(shape)
        ny = lambda u: sum(1 for v in ys if v < u)
        with nc.Block() as block:
            def y_read(dve, i):
                c = units[ys[i]][1]
                dve.wait_ge(y_product, i + 1)
                src = g.ps[:, 5 + i % 2, :].rearrange("p (t l) -> p t l", l=CH)
                dst = y[:, :, c * CH:(c + 1) * CH]
                if first_y[c] == ys[i]:
                    dve.tensor_copy(dst, src).then_inc(y_out, 1)
                else:
                    dve.wait_ge(y_out, Y[first_y[c]] + 1)
                    dve.tensor_tensor(dst, dst, src, ALU.add).then_inc(y_out, 1)

            @block.tensor
            def _(pe):
                def running_sums(u):
                    dr, c = units[u]
                    pe.wait_ge(spread, u + 1)
                    if u >= 1:
                        pe.wait_ge(act_read, u)
                        pe.wait_ge(last_made, u)
                        if ny(u):
                            pe.wait_ge(seg_made, ny(u))
                    for b in range(2):
                        pe.matmul(g.ps[:, b, :], g.ones[:], au[:, u % 2, 4 * b:4 * b + 4, :].rearrange("p h l -> p (h l)"), start=True, stop=True)
                    pe.matmul(g.ps[:, 2, 0:H], tri[:, dr, :], adt[:, c, 8 * dr:8 * dr + 8], start=True, stop=True).then_inc(sums, 1)

                running_sums(0)
                for u, (dr, c) in enumerate(units):
                    tok = slice(c * CH, (c + 1) * CH)
                    if u in Y:
                        i = Y[u]
                        if i >= 1:
                            pe.wait_ge(masked, i)
                        for grp in range(G):
                            mm = pe.matmul(g.ps[:, 4, grp * CH:(grp + 1) * CH], xbc[:, 4 + grp, tok], xbc[:, 6 + grp, tok], start=True, stop=True)
                        mm.then_inc(gram, 1)
                    pe.wait_ge(weighted, u + 1)
                    if u >= 1:
                        pe.wait_ge(state, u)
                    for grp in range(G):
                        mm = pe.matmul(g.ps[:, 3, grp * 256:(grp + 1) * 256], bt[:, c, grp * P:(grp + 1) * P],
                                       xw[:, u % 2, 4 * grp:4 * grp + 4, :].rearrange("p h x -> p (h x)"), start=True, stop=True)
                    mm.then_inc(state_product, 1)
                    if u + 1 < U:
                        running_sums(u + 1)
                    if u in Y:
                        i = Y[u]
                        pe.wait_ge(attended, i + 1)
                        pe.wait_ge(c_scaled, i + 1)
                        pe.wait_ge(x_dt, i + 1)
                        if i >= 2:
                            pe.wait_ge(y_out, i - 1)
                        for h in range(H):
                            dst = g.ps[64 * (h % 2):64 * (h % 2) + 64, 5 + i % 2, (h // 2) * CH:(h // 2 + 1) * CH]
                            pe.matmul(dst, xd[:, i % 2, h, :], seg[:, i % 2, h, :], start=True, stop=False)
                            mm = pe.matmul(dst, st[:, dr, (u // 2) % 2, h, :], ea[:, i % 2, h, :], start=False, stop=True)
                        mm.then_inc(y_product, 1)

            @block.scalar
            def _(act):
                for u, (dr, c) in enumerate(units):
                    end = CH - 1 if dr == 0 else 0
                    act.wait_ge(sums, u + 1)
                    if u >= 2:
                        act.wait_ge(last_made, u - 1)
                        if ny(u - 1):
                            act.wait_ge(seg_made, ny(u - 1))
                        act.wait_ge(kept, u - 1)
                    act.activation(acs[:, u % 2, :], g.ps[:, 2, 0:H], ACT.Copy).then_inc(acs_out, 1)
                    done = act.activation(whole[:, u % 2, :], acs_ps[:, :, end], ACT.Exp)
                    if u in Y:
                        i = Y[u]
                        if i >= 2:
                            act.wait_ge(y_product, i - 1)
                        done = act.activation(ea[:, i % 2], acs_ps, ACT.Exp)
                    done.then_inc(act_read, 1)
                    act.wait_ge(last_made, u + 1)
                    if u >= 2:
                        act.wait_ge(weighted, u - 1)
                    act.activation(dec[:, u % 2, :], last[:, u % 2, :], ACT.Exp).then_inc(decay_done, 1)
                    if u in Y:
                        act.wait_ge(clamped, i + 1)
                        act.activation(seg[:, i % 2], seg[:, i % 2], ACT.Exp).then_inc(seg_exp, 1)

            @block.vector
            def _(dve):
                def spread_adt(u):
                    dr, c = units[u]
                    if u >= 2:
                        dve.wait_ge(sums, u - 1)
                    dve.tensor_tensor(au[:, u % 2], tri[:, dr, :].unsqueeze(1).to_broadcast(HL),
                                      by_head(adt[:, c, 8 * dr:8 * dr + 8], HL), ALU.mult).then_inc(spread, 1)

                spread_adt(0)
                dve.memset(st[:], 0.0).then_inc(cleared, 1)
                dve.wait_ge(cleared, 1)
                for u, (dr, c) in enumerate(units):
                    end = CH - 1 if dr == 0 else 0
                    tok = slice(c * CH, (c + 1) * CH)
                    if u + 1 < U:
                        spread_adt(u + 1)
                    dve.wait_ge(acs_out, u + 1)
                    dve.wait_ge(act_read, u + 1)
                    if u >= 2:
                        dve.wait_ge(decay_done, u - 1)
                    dve.tensor_tensor(last[:, u % 2, :], acs_ps[:, :, end], acs[:, u % 2, :], ALU.subtract).then_inc(last_made, 1)
                    if u in Y:
                        i = Y[u]
                        if i >= 2:
                            dve.wait_ge(y_product, i - 1)
                        dve.tensor_tensor(seg[:, i % 2], acs_ps, by_head(acs[:, u % 2, :], HL), ALU.subtract).then_inc(seg_made, 1)
                        dve.wait_ge(seg_made, i + 1)
                        dve.tensor_scalar(seg[:, i % 2], seg[:, i % 2], 0.0, None, ALU.min).then_inc(clamped, 1)
                    dve.wait_ge(decay_done, u + 1)
                    dve.tensor_tensor(dec[:, u % 2, :], dec[:, u % 2, :], dt[:, c, 8 * dr:8 * dr + 8], ALU.mult).then_inc(decay_dt, 1)
                    dve.wait_ge(decay_dt, u + 1)
                    if u >= 2:
                        dve.wait_ge(state_product, u - 1)
                    xh = xt[:, c, :].rearrange("p (h x) -> p h x", x=HD)
                    dve.tensor_tensor(xw[:, u % 2], xh, by_head(dec[:, u % 2, :], HX), ALU.mult).then_inc(weighted, 1)
                    if u in Y:
                        dve.tensor_tensor(xd[:, i % 2], xh, by_head(dt[:, c, 8 * dr:8 * dr + 8], HX), ALU.mult).then_inc(x_dt, 1)
                        dve.wait_ge(act_read, u + 1)
                        grouped = [P, G, H // G, CH]
                        ea4 = ea[:, i % 2].rearrange("p (g e) l -> p g e l", g=G)
                        dve.tensor_tensor(ea4, ea4, by_head(xbc[:, 6:8, tok], grouped), ALU.mult).then_inc(c_scaled, 1)
                        dve.wait_ge(gram, i + 1)
                        g2 = g.ps[:, 4, 0:G * CH].rearrange("p (g l) -> p g l", g=G)
                        dve.tensor_tensor(gm[:, i % 2], g2, tri[:, dr, :].unsqueeze(1).to_broadcast([P, G, CH]), ALU.mult).then_inc(masked, 1)
                        dve.wait_ge(masked, i + 1)
                        dve.wait_ge(seg_exp, i + 1)
                        s4 = seg[:, i % 2].rearrange("p (g e) l -> p g e l", g=G)
                        dve.tensor_tensor(s4, s4, by_head(gm[:, i % 2], grouped), ALU.mult).then_inc(attended, 1)
                    dve.wait_ge(act_read, u + 1)
                    if u >= 2:
                        dve.wait_ge(state, u - 1)
                    old, new = st[:, dr, (u // 2) % 2], st[:, dr, (u // 2 + 1) % 2]
                    dve.tensor_tensor(tmp[:], old, by_head(whole[:, u % 2, :], HX), ALU.mult).then_inc(kept, 1)
                    dve.wait_ge(kept, u + 1)
                    dve.wait_ge(state_product, u + 1)
                    if u - 2 in Y:
                        dve.wait_ge(y_product, Y[u - 2] + 1)
                    dve.tensor_tensor(new, tmp[:], g.ps[:, 3, :].rearrange("p (h x) -> p h x", x=HD), ALU.add).then_inc(state, 1)
                    if u in Y and i >= 1:
                        y_read(dve, i - 1)
                y_read(dve, len(ys) - 1)


def gate_norm(nc, g, xbc, gate, y, out):
    T = 4
    with stage(nc, "skipped gated squared square_used logged rstd normed") as (mem, (skipped, gated, squared, square_used, logged, rstd, normed)):
        sq = tile(nc, mem, "norm_sq", [P, 2, LAT])
        rs = tile(nc, mem, "norm_rs", [P, LAT])
        total = g.ps[:, 0:2, :].rearrange("p b n -> p (b n)")
        with nc.Block() as block:
            @block.vector
            def _(dve):
                for t in range(T):
                    dve.scalar_tensor_tensor(out=y[:, t, :], in0=xbc[:, t, 0:LAT], scalar=vec(g, "d_skip", t), in1=y[:, t, :], op0=ALU.mult, op1=ALU.add).then_inc(skipped, 1)
                    dve.wait_ge(skipped, t + 1)
                    dve.tensor_tensor(y[:, t, :], y[:, t, :], gate[:, t, :], ALU.mult).then_inc(gated, 1)
                dve.wait_ge(rstd, 1)
                for t in range(T):
                    dve.scalar_tensor_tensor(out=out[:, t, 0:LAT], in0=y[:, t, :], scalar=vec(g, "mb_norm", t), in1=rs[:], op0=ALU.mult, op1=ALU.mult).then_inc(normed, 1)

            @block.scalar
            def _(act):
                act.preload_act_table_set("natural_log_exp_and_others")
                for t in range(T):
                    act.wait_ge(gated, t + 1)
                    if t >= 2:
                        act.wait_ge(square_used, t - 1)
                    act.activation(sq[:, t % 2, :], y[:, t, :], ACT.Square).then_inc(squared, 1)
                act.wait_ge(square_used, T)
                act.activation(rs[:], total, ACT.Ln, bias=g.eps[:], scale=1.0 / (T * P)).then_inc(logged, 1)
                act.wait_ge(logged, 1)
                act.activation(rs[:], rs[:], ACT.Exp, scale=-0.5).then_inc(rstd, 1)

            @block.tensor
            def _(pe):
                for t in range(T):
                    pe.wait_ge(squared, t + 1)
                    for a, n in CHUNKS[:2]:
                        mm = pe.matmul(total[:, a:a + n], g.ones[:], sq[:, t % 2, a:a + n], start=(t == 0), stop=(t == T - 1))
                    mm.then_inc(square_used, 1)


FOLD = LAT // 2
FT = FOLD // P
W_HY = 512
PARTS = [("cos_even", "sum", True), ("sin_even", "diff", False), ("cos_odd", "diff", False), ("sin_odd", "sum", True)]
PI2_A, PI2_B = 6.28125, 0.0019350051879882812
PI2_C = 2 * math.pi - PI2_A - PI2_B
ROUND = 1.5 * 2 ** 23
BELOW_PI = 3.1415925


def hyena_spectra(nc, g, d, spectra):
    ORD = 2
    HID = 64
    with stage(nc, "loaded product biased reduced sines flipped zeroed") as (mem, (loaded, product, biased, reduced, sines, flipped, zeroed)):
        w1, w2 = tile(nc, mem, "hy_w1", [P, HID]), tile(nc, mem, "hy_w2", [P, HID])
        zt = tile(nc, mem, "positions", [P, LAT])
        h1 = tile(nc, mem, "hy_h1", [P, LAT])
        ang, turns = tile(nc, mem, "angles", [P, LAT]), tile(nc, mem, "turns", [P, LAT])
        h2, h2r, h2b = spectra.h2, spectra.h2r, spectra.h2b
        rows = slice(0, HID)
        with nc.Block() as block:
            @block.sync
            def _(sp):
                sp.dma_start(w1[0:33, :], d["hy_w1"]).then_inc(loaded, 16)
                sp.dma_start(w2[rows, :], d["hy_w2"]).then_inc(loaded, 16)
                sp.dma_start(zt[0:33, :], d["positions"]).then_inc(loaded, 16)

            @block.tensor
            def _(pe):
                pe.wait_ge(loaded, 48)
                for layer in range(2):
                    for c in range(2):
                        if layer:
                            pe.wait_ge(sines, 1)
                        w, src, kk = ((w1, zt, 33), (w2, h1, HID))[layer]
                        mm = pe.matmul(g.ps[rows, 2 * layer + c, :], w[0:kk, :], src[0:kk, c * BANK:(c + 1) * BANK], start=True, stop=True)
                    mm.then_inc(product, 1)

            @block.vector
            def _(dve):
                dve.memset(h2[rows, LAT:LAT + 1], 0.0).then_inc(zeroed, 1)
                n = 0
                for layer in range(2):
                    dve.wait_ge(product, layer + 1)
                    flat = g.ps[rows, 2 * layer:2 * layer + 2, :].rearrange("p b n -> p (b n)")
                    a, k = ang[rows, :], turns[rows, :]
                    b = vec(g, ("hy_b1", "hy_b2")[layer])[rows, :]
                    dve.tensor_scalar(a, flat, b, vec(g, "freq")[rows, :], ALU.add, ALU.mult).then_inc(biased, 1)
                    dve.wait_ge(biased, layer + 1)
                    dve.tensor_scalar(k, a, 1 / (2 * math.pi), ROUND, ALU.mult, ALU.add).then_inc(reduced, 1)
                    dve.wait_ge(reduced, n + 1)
                    dve.tensor_scalar(k, k, -ROUND, None, ALU.add).then_inc(reduced, 1)
                    dve.wait_ge(reduced, n + 2)
                    for j, part in enumerate((PI2_A, PI2_B, PI2_C)):
                        dve.scalar_tensor_tensor(out=a, in0=k, scalar=-part, in1=a, op0=ALU.mult, op1=ALU.add).then_inc(reduced, 1)
                        dve.wait_ge(reduced, n + 3 + j)
                    dve.tensor_scalar(a, a, BELOW_PI, -BELOW_PI, ALU.min, ALU.max).then_inc(reduced, 1)
                    n += 6
                dve.wait_ge(sines, 2)
                dve.wait_ge(zeroed, 1)
                dve.tensor_copy(h2r[rows, :], h2[rows, LAT:LAT - FOLD:-1]).then_inc(flipped, 1)
                dve.tensor_copy(h2b[rows, :], h2[rows, 0:P]).then_inc(flipped, 1)
                dve.wait_ge(flipped, 2)
                dve.memset(h2b[rows, 0:1], 0.0).then_inc(flipped, 1)

            @block.scalar
            def _(act):
                for layer in range(2):
                    act.wait_ge(reduced, 6 * (layer + 1))
                    act.activation((h1, h2)[layer][rows, 0:LAT], ang[rows, :], ACT.Sin).then_inc(sines, 1)

    names = "loaded taps row_taps weighed row_weighed paired row_paired folded product read_out first_halved halved stored0 stored1 stored2"
    with stage(nc, names) as (mem, sems):
        loaded, taps, row_taps, weighed, row_weighed, paired, row_paired, folded, product, read_out, first_halved, halved = sems[:12]
        stored = sems[12:]
        w3 = tile(nc, mem, "hy_w3", [P, ORD * 2 * W_HY])
        dec = tile(nc, mem, "decay", [P, 2, FT, W_HY])
        dec_row = tile(nc, mem, "decay_middle", [1, W_HY])
        tabs = tile(nc, mem, "dft", [P, 4, FT, FOLD])
        alt_row, alt_col = spectra.alt_row, spectra.alt_col
        four = tile(nc, mem, "taps_weighed", [P, 4, W_HY])
        two = tile(nc, mem, "taps_paired", [P, 4, W_HY])
        pm = tile(nc, mem, "taps_folded", [P, 4, ORD, FT, W_HY])
        mid = tile(nc, mem, "taps_middle", [1, 2, W_HY])
        mid_sum = tile(nc, mem, "taps_middle_paired", [1, ORD, 2, W_HY])
        sp_out = tile(nc, mem, "spectrum_out", [P, 3, W_HY])
        SRC = {"cos_even": 0, "cos_odd": 1, "sin_odd": 2, "sin_even": 3}
        units = [(o, i, q) for o in range(ORD) for i in range(FT) for q in range(4)]
        per_order = 4 * FT + 1
        rows = slice(0, 64)
        with nc.Block() as block:
            @block.sync
            def _(sp):
                for dst, src in ((w3[rows, :], d["hy_w3"]), (dec[:], d["decay"]), (dec_row[:], d["decay_middle"]), (tabs[:], d["dft"]),
                                 (alt_row[:], d["alt_row"]), (alt_col[:], d["alt_col"])):
                    sp.dma_start(dst, src).then_inc(loaded, 16)
                for o in range(ORD):
                    for n in range(per_order):
                        e = o * per_order + n
                        sp.wait_ge(halved, o + 1) if n == 0 else sp.wait_ge(read_out, e + 1)
                        if n < 4 * FT:
                            i, q = divmod(n, 4)
                            parity, kind = q // 2, q % 2
                            sp.dma_start(spectra.h[o, parity * 8 + kind * 4 + i], sp_out[:, e % 3, :]).then_inc(stored[e % 3], 16)
                        else:
                            sp.dma_start(spectra.last[o:o + 1], sp_out[0:1, e % 3, :]).then_inc(stored[e % 3], 16)
                E = ORD * per_order
                for s in range(3):
                    sp.wait_ge(stored[s], 16 * len(range(s, E, 3)))

            @block.tensor
            def _(pe):
                pe.wait_ge(loaded, 96)

                def tap_products(o, jt):
                    q = o * FT + jt
                    if q:
                        pe.wait_ge(weighed, 4 * q)
                    f, b = w3[rows, (2 * o) * W_HY:(2 * o + 1) * W_HY], w3[rows, (2 * o + 1) * W_HY:(2 * o + 2) * W_HY]
                    js = slice(jt * P, (jt + 1) * P)
                    pe.matmul(g.ps[:, 0, :], h2[rows, js], f, start=True, stop=True)
                    pe.matmul(g.ps[:, 1, :], h2b[rows, :] if jt == 0 else h2[rows, js], b, start=True, stop=True)
                    pe.matmul(g.ps[:, 2, :], h2r[rows, js], f, start=True, stop=True)
                    pe.matmul(g.ps[:, 3, :], h2r[rows, js], b, start=True, stop=True).then_inc(taps, 1)

                def middle_products(o):
                    for n in range(2):
                        if 2 * o + n:
                            pe.wait_ge(row_weighed, 2 * o + n)
                        pe.matmul(g.ps[0:1, 4, :], h2[rows, FOLD:FOLD + 1], w3[rows, (2 * o + n) * W_HY:(2 * o + n + 1) * W_HY],
                                  start=True, stop=True).then_inc(row_taps, 1)

                def spectrum(o, n):
                    e = o * per_order + n
                    if e >= 3:
                        pe.wait_ge(read_out, e - 2)
                    if n == 0:
                        pe.wait_ge(folded, 4 * FT * (o + 1))
                        pe.wait_ge(row_paired, 2 * (o + 1))
                    bank = 5 + e % 3
                    if n < 4 * FT:
                        i, q = divmod(n, 4)
                        part, fold, middle = PARTS[q]
                        for jt in range(FT):
                            mm = pe.matmul(g.ps[:, bank, :], tabs[:, q, jt, i * P:(i + 1) * P], pm[:, SRC[part], o, jt, :], start=(jt == 0), stop=(jt == FT - 1 and not middle))
                        if middle:
                            mm = pe.matmul(g.ps[:, bank, :], alt_row[:, 0:P], mid_sum[:, o, 0 if part == "cos_even" else 1, :], start=False, stop=True)
                    else:
                        for jt in range(FT):
                            pe.matmul(g.ps[0:1, bank, :], alt_col[:], pm[:, 0, o, jt, :], start=(jt == 0), stop=False)
                        mm = pe.matmul(g.ps[0:1, bank, :], alt_row[:, 0:1], mid_sum[:, o, 0, :], start=False, stop=True)
                    mm.then_inc(product, 1)

                for jt in range(FT):
                    tap_products(0, jt)
                middle_products(0)
                for n in range(per_order):
                    if n % 4 == 0 and n // 4 < FT:
                        tap_products(1, n // 4)
                    spectrum(0, n)
                middle_products(1)
                for n in range(per_order):
                    spectrum(1, n)

            @block.scalar
            def _(act):
                for e in range(ORD * per_order):
                    o, n = divmod(e, per_order)
                    act.wait_ge(product, e + 1)
                    if e >= 3:
                        act.wait_ge(stored[e % 3], 16 * (e // 3))
                    if n < 4 * FT:
                        act.activation(sp_out[:, e % 3, :], g.ps[:, 5 + e % 3, :], ACT.Copy, scale=1.0 / LAT).then_inc(read_out, 1)
                        if n == 0:
                            act.wait_ge(read_out, e + 1)
                            act.activation(sp_out[0:1, e % 3, :], sp_out[0:1, e % 3, :], ACT.Copy, scale=0.5).then_inc(halved, 1)
                    else:
                        act.activation(sp_out[0:1, e % 3, :], g.ps[0:1, 5 + e % 3, :], ACT.Copy, scale=0.5 / LAT).then_inc(read_out, 1)

            @block.vector
            def _(dve):
                dve.wait_ge(loaded, 96)
                for o in range(ORD):
                    for jt in range(FT):
                        q = o * FT + jt
                        dve.wait_ge(taps, q + 1)
                        if q:
                            dve.wait_ge(paired, 4 * q)
                            dve.wait_ge(folded, 4 * q)
                        for n in range(4):
                            dve.tensor_tensor(four[:, n, :], g.ps[:, n, :], dec[:, n // 2, jt, :], ALU.mult).then_inc(weighed, 1)
                        dve.wait_ge(weighed, 4 * (q + 1))
                        for n, (x, op) in enumerate(((0, ALU.add), (2, ALU.add), (0, ALU.subtract), (2, ALU.subtract))):
                            dve.tensor_tensor(two[:, n, :], four[:, x, :], four[:, x + 1, :], op).then_inc(paired, 1)
                        dve.wait_ge(paired, 4 * (q + 1))
                        for n, (x, op) in enumerate(((0, ALU.add), (0, ALU.subtract), (2, ALU.add), (2, ALU.subtract))):
                            dve.tensor_tensor(pm[:, n, o, jt, :], two[:, x, :], two[:, x + 1, :], op).then_inc(folded, 1)
                    for n in range(2):
                        dve.wait_ge(row_taps, 2 * o + n + 1)
                        if o and n == 0:
                            dve.wait_ge(row_paired, 2 * o)
                        dve.tensor_tensor(mid[:, n, :], g.ps[0:1, 4, :], dec_row[:], ALU.mult).then_inc(row_weighed, 1)
                    dve.wait_ge(row_weighed, 2 * (o + 1))
                    dve.tensor_tensor(mid_sum[:, o, 0, :], mid[:, 0, :], mid[:, 1, :], ALU.add).then_inc(row_paired, 1)
                    dve.tensor_tensor(mid_sum[:, o, 1, :], mid[:, 0, :], mid[:, 1, :], ALU.subtract).then_inc(row_paired, 1)


def project_hyena(nc, g, d, high, low, u3):
    TILES, BANKS = 12, 8
    units = [(t, a, n) for t in range(TILES) for a, n in CHUNKS[:2]]
    C = 2
    with stage(nc, "raw_in0 raw_in1 w_rounded w_split product raw_out padded steps conv stored0 stored1") as (mem, sems):
        w_sems, (product, raw_out, padded, steps, conv), stored = sems[:4], sems[4:9], sems[9:]
        ring = WeightRing(nc, mem, w_sems, product, [C * (t + 1) for t in range(TILES)])
        raw = tile(nc, mem, "hy_raw", [P, 2, LAT + 2])
        res = tile(nc, mem, "hy_conv", [P, 2, LAT])
        with nc.Block() as block:
            @block.sync
            def _(sp):
                for t in range(TILES + 3):
                    if t < TILES:
                        ring.load(sp, t, d["w_hy"][t])
                    if t >= 3:
                        v = t - 3
                        sp.wait_ge(conv, v + 1)
                        sp.dma_start(u3[:, v, :], res[:, v % 2, :]).then_inc(stored[v % 2], 16)
                for s in range(2):
                    sp.wait_ge(stored[s], 16 * (TILES // 2))

            @block.tensor
            def _(pe):
                for u, (t, a, n) in enumerate(units):
                    if u % C == 0:
                        pe.wait_ge(ring.split, t + 1)
                    if u >= BANKS:
                        pe.wait_ge(raw_out, u - BANKS + 1)
                    ring.product_of(pe, g.ps[:, u % BANKS, 0:n], t, high, low, a, n).then_inc(product, 1)

            @block.scalar
            def _(act):
                ring.round_piece(act, 0)
                act.wait_ge(padded, 1)
                for u, (t, a, n) in enumerate(units):
                    if u % C == 0:
                        ring.round_piece(act, t + 1)
                    act.wait_ge(product, u + 1)
                    if t >= 2 and u % C == 0:
                        act.wait_ge(conv, t - 1)
                    act.activation(raw[:, t % 2, 1 + a:1 + a + n], g.ps[:, u % BANKS, 0:n], ACT.Copy).then_inc(raw_out, 1)

            @block.vector
            def _(dve):
                dve.memset(raw[:], 0.0).then_inc(padded, 1)
                ring.split_piece(dve, 0)
                for t in range(TILES):
                    ring.split_piece(dve, t + 1)
                    dve.wait_ge(raw_out, C * (t + 1))
                    if t >= 2:
                        dve.wait_ge(stored[t % 2], 16 * (t // 2))
                    tap = lambda i: vec(g, "short_w", i * TILES + t)
                    dve.tensor_scalar(res[:, t % 2, :], raw[:, t % 2, 0:LAT], tap(0), vec(g, "short_b", t), ALU.mult, ALU.add).then_inc(steps, 1)
                    dve.wait_ge(steps, 2 * t + 1)
                    dve.scalar_tensor_tensor(out=res[:, t % 2, :], in0=raw[:, t % 2, 1:1 + LAT], scalar=tap(1), in1=res[:, t % 2, :], op0=ALU.mult, op1=ALU.add).then_inc(steps, 1)
                    dve.wait_ge(steps, 2 * t + 2)
                    dve.scalar_tensor_tensor(out=res[:, t % 2, :], in0=raw[:, t % 2, 2:2 + LAT], scalar=tap(2), in1=res[:, t % 2, :], op0=ALU.mult, op1=ALU.add).then_inc(conv, 1)


def long_convs(nc, g, d, spectra, u3_src, u3):
    ORD, CT = 2, W_HY // P
    names = ("tabs_in u3_in0 u3_in1 u3_in2 h_in0 h_in1 h_in2 last_in folded first_copied turned turned_out mid_turned mid_out product mult combined last_made "
             "inverse sym_out times mirrored middle skipped gated")
    with stage(nc, names) as (mem, sems):
        (tabs_in, u3_in0, u3_in1, u3_in2, h_in0, h_in1, h_in2, last_in, folded, first_copied, turned, turned_out, mid_turned, mid_out, product, mult, combined, last_made,
         inverse, sym_out, times, mirrored, middle, skipped, gated) = sems
        u3_in, h_in = (u3_in0, u3_in1, u3_in2), (h_in0, h_in1, h_in2)
        tabs = tile(nc, mem, "dft", [P, 4, FT, FOLD])
        back = tile(nc, mem, "dft_back", [P, 2, FT, FOLD])
        alt_row, alt_col = spectra.alt_row, spectra.alt_col
        fold = tile(nc, mem, "folded", [P, 2, CT, FOLD])
        tim = tile(nc, mem, "folded_turned", [P, 2, FT, W_HY])
        mid = tile(nc, mem, "middle_time", [1, W_HY])
        h = tile(nc, mem, "filter_ring", [P, 3, 2, W_HY])
        hl = tile(nc, mem, "filter_last", [1, W_HY])
        yv = tile(nc, mem, "output_spectrum", [P, 4, FT, W_HY])
        yl = tile(nc, mem, "output_last", [1, W_HY])
        pr = tile(nc, mem, "products", [P, 4, W_HY])
        sym = tile(nc, mem, "symmetric", [P, 2, FOLD + 1])
        tm = tile(nc, mem, "convolved", [P, 2, LAT])
        z = u3
        with nc.Block() as block:
            @block.sync
            def _(sp):
                sp.dma_start(u3[:, 0:CT, :], u3_src[:, 0:CT, :]).then_inc(u3_in[0], 16)
                for dst, src in ((tabs, "dft"), (back, "dft_back")):
                    sp.dma_start(dst[:], d[src]).then_inc(tabs_in, 16)
                for o in range(ORD):
                    if o:
                        sp.wait_ge(last_made, 1)
                    sp.dma_start(hl[:], spectra.last[o:o + 1]).then_inc(last_in, 16)
                    filters = spectra.h[o].rearrange("(q k i) p n -> q i p k n", q=2, k=2)
                    for n in range(2 * FT):
                        w = o * 2 * FT + n
                        if w >= 3:
                            sp.wait_ge(mult, 4 * (w - 2))
                        sp.dma_start(h[:, w % 3], filters[n // FT, n % FT]).then_inc(h_in[w % 3], 16)
                        if w in (3, 4):
                            sp.dma_start(u3[:, CT * (w - 2):CT * (w - 1), :], u3_src[:, CT * (w - 2):CT * (w - 1), :]).then_inc(u3_in[w - 2], 16)

            @block.tensor
            def _(pe):
                pe.wait_ge(tabs_in, 32)
                n_turn = 0
                for o in range(ORD):
                    for s in range(2):
                        for jt in range(FT):
                            pe.wait_ge(folded, 2 * CT * (o + 1))
                            if n_turn >= 2:
                                pe.wait_ge(turned_out, n_turn - 1)
                            for ct in range(CT):
                                mm = pe.transpose(g.ps[:, n_turn % 2, ct * P:(ct + 1) * P], fold[:, s, ct, jt * P:(jt + 1) * P], g.ident[:])
                            mm.then_inc(turned, 1)
                            n_turn += 1
                    for ct in range(CT):
                        src = z[:, ct, FOLD:FOLD + 1]
                        mm = pe.transpose(g.ps[0:1, 2, ct * P:(ct + 1) * P], src, g.ident[:])
                    mm.then_inc(mid_turned, 1)
                    pe.wait_ge(turned_out, 2 * FT * (o + 1))
                    pe.wait_ge(mid_out, o + 1)
                    n = 0
                    for parity in range(2):
                        for i in range(FT):
                            w = o * 2 * FT + n
                            for kind in range(2):
                                q = 2 * parity + kind
                                part, src, middle_counts = PARTS[q]
                                bank = 3 + 2 * (n % 2) + kind
                                if n >= 2 and kind == 0:
                                    pe.wait_ge(mult, 4 * (w - 1))
                                for jt in range(FT):
                                    mm = pe.matmul(g.ps[:, bank, :], tabs[:, q, jt, i * P:(i + 1) * P], tim[:, 0 if src == "sum" else 1, jt, :],
                                                   start=(jt == 0), stop=(jt == FT - 1 and not middle_counts))
                                if middle_counts:
                                    mm = pe.matmul(g.ps[:, bank, :], alt_row[:, 0:P], mid[:], start=False, stop=True)
                            mm.then_inc(product, 1)
                            n += 1
                    for jt in range(FT):
                        pe.matmul(g.ps[0:1, 7, :], alt_col[:], tim[:, 0, jt, :], start=(jt == 0), stop=False)
                    pe.matmul(g.ps[0:1, 7, :], alt_row[:, 0:1], mid[:], start=False, stop=True).then_inc(product, 1)
                    pe.wait_ge(combined, 4 * FT * (o + 1))
                    pe.wait_ge(last_made, o + 1)
                    for ct in range(CT):
                        v = o * CT + ct
                        cs = slice(ct * P, (ct + 1) * P)
                        a_bank, b_bank, c_bank = (0, 1, 2) if v % 2 == 0 else (3, 4, 5)
                        if ct >= 2:
                            pe.wait_ge(mirrored, v - 1)
                            pe.wait_ge(sym_out, 2 * (v - 1))
                        for bank, (p0, t0), (p1, t1) in ((a_bank, (0, tabs[:, 0]), (3, back[:, 1])), (b_bank, (2, back[:, 0]), (1, tabs[:, 1]))):
                            for pp, tab in ((p0, t0), (p1, t1)):
                                for i in range(FT):
                                    mm = pe.matmul(g.ps[:, bank, :], yv[:, pp, i, cs], tab[:, i, :], start=(pp == p0 and i == 0),
                                                   stop=(bank == b_bank and pp == p1 and i == FT - 1))
                            if bank == a_bank:
                                pe.matmul(g.ps[:, bank, :], yl[:, cs], alt_row[:], start=False, stop=True)
                        for pp in (0, 3):
                            for i in range(FT):
                                pe.matmul(g.ps[:, c_bank, 0:1], yv[:, pp, i, cs], alt_col[:], start=(pp == 0 and i == 0), stop=False)
                        pe.matmul(g.ps[:, c_bank, 0:1], yl[:, cs], alt_row[:, 0:1], start=False, stop=True).then_inc(inverse, 1)

            @block.scalar
            def _(act):
                n_turn = 0
                for o in range(ORD):
                    for s in range(2):
                        for jt in range(FT):
                            act.wait_ge(turned, n_turn + 1)
                            if o and n_turn == 2 * FT:
                                act.wait_ge(product, 2 * FT + 1)
                            act.activation(tim[:, s, jt, :], g.ps[:, n_turn % 2, :], ACT.Copy).then_inc(turned_out, 1)
                            n_turn += 1
                    act.wait_ge(mid_turned, o + 1)
                    act.activation(mid[:], g.ps[0:1, 2, :], ACT.Copy).then_inc(mid_out, 1)
                    for ct in range(CT):
                        v = o * CT + ct
                        act.wait_ge(inverse, v + 1)
                        if v >= 2:
                            act.wait_ge(mirrored, v - 1)
                            act.wait_ge(middle, v - 1)
                        a_bank, c_bank = (0, 2) if v % 2 == 0 else (3, 5)
                        act.activation(sym[:, v % 2, 0:FOLD], g.ps[:, a_bank, :], ACT.Copy).then_inc(sym_out, 1)
                        act.activation(sym[:, v % 2, FOLD:FOLD + 1], g.ps[:, c_bank, 0:1], ACT.Copy).then_inc(sym_out, 1)

            @block.vector
            def _(dve):
                def fold_tile(src, ct):
                    x = src[:, ct, :]
                    head, tail = x[:, 1:FOLD], x[:, LAT - 1:FOLD:-1]
                    dve.tensor_tensor(fold[:, 0, ct, 1:FOLD], head, tail, ALU.add).then_inc(first_copied, 1)
                    dve.tensor_tensor(fold[:, 1, ct, 1:FOLD], head, tail, ALU.subtract).then_inc(first_copied, 1)
                    dve.tensor_copy(fold[:, 0, ct, 0:1], x[:, 0:1]).then_inc(folded, 1)
                    dve.tensor_copy(fold[:, 1, ct, 0:1], x[:, 0:1]).then_inc(folded, 1)

                dve.wait_ge(u3_in[0], 16)
                for ct in range(CT):
                    fold_tile(z, ct)
                for o in range(ORD):
                    n = 0
                    for parity in range(2):
                        for i in range(FT):
                            w = o * 2 * FT + n
                            dve.wait_ge(product, o * (2 * FT + 1) + n + 1)
                            dve.wait_ge(h_in[w % 3], 16 * (w // 3 + 1))
                            if w:
                                dve.wait_ge(combined, 2 * w)
                            if o and n == 0:
                                dve.wait_ge(inverse, CT * o)
                            c_ps, s_ps = g.ps[:, 3 + 2 * (n % 2), :], g.ps[:, 4 + 2 * (n % 2), :]
                            ch, sh = h[:, w % 3, 0, :], h[:, w % 3, 1, :]
                            for m, (x, y_) in enumerate(((c_ps, ch), (s_ps, sh), (c_ps, sh), (s_ps, ch))):
                                dve.tensor_tensor(pr[:, m, :], x, y_, ALU.mult).then_inc(mult, 1)
                            dve.wait_ge(mult, 4 * (w + 1))
                            dve.tensor_tensor(yv[:, 2 * parity, i, :], pr[:, 0, :], pr[:, 1, :], ALU.subtract).then_inc(combined, 1)
                            dve.tensor_tensor(yv[:, 2 * parity + 1, i, :], pr[:, 2, :], pr[:, 3, :], ALU.add).then_inc(combined, 1)
                            n += 1
                    dve.wait_ge(product, (o + 1) * (2 * FT + 1))
                    dve.wait_ge(last_in, 16 * (o + 1))
                    if o:
                        dve.wait_ge(inverse, CT * o)
                    dve.tensor_tensor(yl[:], g.ps[0:1, 7, :], hl[:], ALU.mult).then_inc(last_made, 1)
                    dve.wait_ge(u3_in[o + 1], 16)
                    for ct in range(CT):
                        v = o * CT + ct
                        b_bank = 1 if v % 2 == 0 else 4
                        dve.wait_ge(sym_out, 2 * (v + 1))
                        if v >= 2:
                            dve.wait_ge(skipped, v - 1)
                        t = tm[:, v % 2, :]
                        dve.tensor_tensor(t[:, 0:FOLD], sym[:, v % 2, 0:FOLD], g.ps[:, b_bank, :], ALU.add).then_inc(times, 1)
                        dve.tensor_copy(t[:, FOLD:FOLD + 1], sym[:, v % 2, FOLD:FOLD + 1]).then_inc(middle, 1)
                        dve.tensor_tensor(t[:, LAT - 1:FOLD:-1], sym[:, v % 2, 1:FOLD], g.ps[:, b_bank, 1:FOLD], ALU.subtract).then_inc(mirrored, 1)
                        dve.wait_ge(times, v + 1)
                        dve.wait_ge(middle, v + 1)
                        dve.wait_ge(mirrored, v + 1)
                        prev = z[:, ct, :]
                        if o:
                            dve.wait_ge(gated, ct + 1)
                        dve.scalar_tensor_tensor(out=t, in0=prev, scalar=vec(g, "skip", 4 * o + ct), in1=t, op0=ALU.mult, op1=ALU.add).then_inc(skipped, 1)
                        dve.wait_ge(skipped, v + 1)
                        dve.tensor_tensor(z[:, ct, :], t, u3[:, CT * (o + 1) + ct, :], ALU.mult).then_inc(gated, 1)
                        if o == 0:
                            dve.wait_ge(gated, v + 1)
                            if ct == 0:
                                dve.wait_ge(mid_turned, 1)
                            fold_tile(z, ct)


def build_program(nc, d):
    g = Globals()
    STAGES.clear()
    with ExitStack() as mem:
        def sb(name, shape):
            return tile(nc, mem, name, shape)

        g.ps = mem.enter_context(nc.psum_tensor("psum", [P, 8, BANK], F32))
        g.vec = sb("small_vectors", [P, NVEC])
        g.ident = sb("identity", [P, P])
        g.ones = sb("all_ones", [P, P])
        g.cond = sb("conditioning", [P, KT, 32])
        g.mod = sb("modulation", [P, 2, 6, KT, 2])
        g.eps = sb("epsilon", [P, 1])

        sc = Globals()
        def scratch(name, shape):
            return nc.dram_tensor(name, shape, F32, kind="Internal").ap()
        sc.qk_a = scratch("scratch_qk_a", [5, P, TOK])
        sc.v_a = scratch("scratch_v_a", [P, KTILES, P])
        sc.q_b = scratch("scratch_q_b", [B_HEADS, B_DK, TOK])
        sc.k_b = scratch("scratch_k_b", [B_HEADS, B_DK, TOK])
        sc.v_b = scratch("scratch_v_b", [P, KTILES, B_HEADS * B_V])

        sc.x = scratch("scratch_x", [P, KT, TOK])
        sc.u3 = scratch("scratch_hyena", [P, 12, LAT])
        sc.y = scratch("scratch_ssd", [P, 4, LAT])
        sc.h = scratch("scratch_spectra", [2, 16, P, W_HY])
        sc.last = scratch("scratch_last", [2, W_HY])

        load_constants(nc, g, d)
        adaln(nc, g, d)
        layer_0(nc, g, d, sc)
        layer_1(nc, g, d, sc)


def layer_0(nc, g, d, sc):
    with ExitStack() as sc.mem:
        g.h = tile(nc, sc.mem, "h", [P, KT, TOK])
        norm_modulate(nc, g, d["x"], 0, SCALE_A, SHIFT_A, TOK)
        project_attention(nc, g, d, sc)
    with ExitStack() as attended:
        mixed = tile(nc, attended, "mixed", [P, KT, TOK], "right")
        attention(nc, g, sc, mixed)
        allocate_parts(nc, g, TOK)
        out = tile(nc, g.out_memory, "out", [P, KT, TOK])
        project_out(nc, g, mixed, d["w_out0"], out, TOK)
    residual_norm_split(nc, g, d["x"], sc.x, out, (0, GATE_A), (0, SCALE_M, SHIFT_M), TOK, g.high, g.low, True)
    mlp(nc, g, out, g.high, g.low, d["ff_w"][0], TOK)
    residual_norm_split(nc, g, sc.x, sc.x, out, (0, GATE_M), (1, SCALE_A, SHIFT_A), TOK, g.high, g.low)
    g.out_memory.close()


def allocate_parts(nc, g, tokens, side="left"):
    g.parts_memory, g.out_memory = ExitStack(), ExitStack()
    g.high, g.low = tile_r(nc, g.parts_memory, "h_high", [P, KT, tokens], side), tile_r(nc, g.parts_memory, "h_low", [P, KT, tokens], side)


def layer_1(nc, g, d, sc):
    with ExitStack() as memory:
        project_hyena(nc, g, d, g.high, g.low, sc.u3)
        y = tile(nc, memory, "ssd_out", [P, 4, LAT], "right")
        xbc = tile(nc, memory, "xbc", [P, 8, TOK], "right")
        gate = tile(nc, memory, "gate", [P, 4, LAT], "right")
        dt, adt = tile(nc, memory, "dt", [P, KTILES, 16], "right"), tile(nc, memory, "adt", [P, KTILES, 16], "right")
        project_mamba(nc, g, d, g.high, g.low, xbc, gate, dt, adt)
        g.parts_memory.close()
        with ExitStack() as tokens_first:
            ssd = Globals()
            ssd.mem, ssd.y = tokens_first, y
            scan_states(nc, g, d, xbc, gate, dt, adt, ssd)
        gate_norm(nc, g, xbc, gate, y, y)
        store(nc, y, sc.y)
    spectra = Globals()
    spectra.h, spectra.last = sc.h, sc.last
    with ExitStack() as memory:
        spectra.alt_row = tile(nc, memory, "alternate_row", [1, FOLD])
        spectra.alt_col = tile(nc, memory, "alternate_column", [P, 1])
        with ExitStack() as features:
            spectra.h2 = tile(nc, features, "hy_h2", [P, LAT + 1])
            spectra.h2r = tile(nc, features, "hy_h2_flipped", [P, FOLD])
            spectra.h2b = tile(nc, features, "hy_h2_behind", [P, P])
            hyena_spectra(nc, g, d, spectra)
        memory_left = ExitStack()
        u3 = tile(nc, memory_left, "hyena_parts", [P, 12, LAT])
        long_convs(nc, g, d, spectra, sc.u3, u3)
        mixed = u3[:, 0:KT, :]
        load(nc, [(mixed[:, 4:KT, :], sc.y)])
        out = tile(nc, memory, "out", [P, KT, LAT], "right")
        allocate_parts(nc, g, LAT, "right")
        project_out(nc, g, mixed, d["w_out1"], out, LAT)
        memory_left.close()
        residual_norm_split(nc, g, sc.x, sc.x, out, (1, GATE_A), (1, SCALE_M, SHIFT_M), LAT, g.high, g.low, True)
        mlp(nc, g, out, g.high, g.low, d["ff_w"][1], LAT)
        g.parts_memory.close()
        residual(nc, g, sc.x, d["out"], out, 1, GATE_M, LAT)


def store(nc, src, dst):
    with stage(nc, "stored") as (mem, (stored,)):
        with nc.Block() as block:
            @block.sync
            def _(sp):
                sp.dma_start(dst, src[:]).then_inc(stored, 16)
                sp.wait_ge(stored, 16)


def feature_tiles(v):
    return np.ascontiguousarray(v.reshape(-1, P).T)


def k_major(w):
    return w.reshape(-1, P, w.shape[1]).transpose(1, 0, 2)


def pieces(w, width=256):
    kk = k_major(w)
    return np.ascontiguousarray(kk.reshape(P, kk.shape[1], -1, width).transpose(2, 0, 1, 3))


def rope_tables():
    t = np.arange(LAT)
    t_row, t_col = (t // GRID_W).astype(np.float32), (t % GRID_W).astype(np.float32)
    def angles(rot):
        quarter = rot // 4
        inv = np.float32(THETA) ** (-np.arange(quarter, dtype=np.float32) / np.float32(quarter))
        return np.concatenate([t_row[None, :] * inv[:, None], t_col[None, :] * inv[:, None]]).astype(np.float32)
    a = {}
    for tag, first, rot, heads in (("a", 0, A_DIM, 2), ("b", B_NOPE, B_ROPE, 1)):
        ang, half = angles(rot), rot // 2
        cos, sin, swap = np.ones((P, TOK), np.float32), np.zeros((P, TOK), np.float32), np.zeros((P, P), np.float32)
        for h in range(heads):
            at = first + h * rot
            for part, sign in ((0, -1), (1, 1)):
                r = np.arange(at + part * half, at + (part + 1) * half)
                cos[r, :LAT] = np.cos(ang)
                sin[r, :LAT] = sign * np.sin(ang)
                swap[r + (half if part == 0 else -half), r] = 1
        a[f"cos_{tag}"], a[f"sin_{tag}"], a[f"swap_{tag}"] = cos, sin, swap
    a["by_head"] = np.kron(np.eye(2), np.ones((A_DIM, A_DIM))).astype(np.float32)
    return a


def hyena_tables():
    f32 = np.float32
    a = {}
    bands = 16
    t = np.linspace(0.0, 1.0, LAT, dtype=f32)
    w = (f32(2.0 * math.pi) * np.arange(LAT, dtype=f32) / f32(LAT)).astype(f32)
    ph = w[:, None] * np.linspace(1e-4, bands - 1, bands, dtype=f32)[None, :]
    a["positions"] = np.ascontiguousarray(np.concatenate([t[:, None], np.cos(ph), -np.sin(ph)], axis=1).T.astype(f32))
    deltas = np.abs(np.linspace(math.log(1e-2) / 1.5, math.log(1e-2) / 0.3, W_HY, dtype=f32))
    decay = np.exp(-t[:, None] * deltas[None, :]).astype(f32)
    tiles = lambda x: x.reshape(FT, P, -1).transpose(1, 0, 2)
    ahead = np.concatenate([np.zeros((1, W_HY), f32), decay[:FOLD:-1]])
    a["decay"] = np.ascontiguousarray(np.stack([tiles(decay[:FOLD]), tiles(ahead)], axis=1))
    a["decay_middle"] = np.ascontiguousarray(decay[FOLD:FOLD + 1])
    j, m = np.arange(FOLD)[:, None], np.arange(FOLD)[None, :]
    even, odd = 2 * np.pi * (m * j % LAT) / LAT, np.pi * (j * (2 * m + 1) % (2 * LAT)) / LAT
    forms = [np.cos(even), np.sin(even), np.cos(odd), np.sin(odd)]
    a["dft"] = np.ascontiguousarray(np.stack([tiles(x) for x in forms], axis=1).astype(f32))
    a["dft_back"] = np.ascontiguousarray(np.stack([tiles(x.T) for x in forms[2:]], axis=1).astype(f32))
    a["alt_row"] = ((-1.0) ** np.arange(FOLD)).astype(f32)[None, :]
    a["alt_col"] = ((-1.0) ** np.arange(P)).astype(f32)[:, None]
    s, l = np.arange(P)[:, None], np.arange(P)[None, :]
    a["triangles"] = np.ascontiguousarray(np.stack([s <= l, s >= l], axis=1).astype(f32))
    return a


def lay_out(i):
    a = {}
    tokens = np.concatenate([i["x"][0], i["ctx"][0]], axis=0)
    a["x"] = np.ascontiguousarray(tokens.T.reshape(KT, P, TOK).transpose(1, 0, 2))
    a["cond"] = np.zeros((P, KT, 32), np.float32)
    a["cond"][:, :, 0:2] = np.stack([i["c"][0], i["c_ctx"]], axis=1).reshape(KT, P, 2).transpose(1, 0, 2)
    a["group_selector"] = np.tile(np.eye(32, 2, dtype=np.float32), (4, 1))
    a["ident"] = np.eye(P, dtype=np.float32)
    a["ones"] = np.ones((P, P), np.float32)
    a["ada_w"] = np.concatenate([pieces(i["ada_w"][l], BANK) for l in range(2)])
    def eighths(w1, w2):
        up = pieces(w1, P).reshape(8, 4, P, KT, P)
        down = [pieces(w2[e * 512:(e + 1) * 512]).reshape(4, P, KT, P) for e in range(8)]
        return np.concatenate([up, np.stack(down)], axis=1).reshape(64, P, KT, P)
    a["ff_w"] = np.stack([eighths(i["ff_w1"][l], i["ff_w2"][l]) for l in range(2)])

    w = i["at_w_in"][0]
    k_a, v_a, low, key, q_a, q_low = np.split(w, np.cumsum([128, 128, 128, 32, 512]), axis=1)
    a["w_qk"] = pieces(np.concatenate([k_a, q_a], axis=1), P)
    a["w_low"] = np.ascontiguousarray(np.stack([k_major(x) for x in (q_low[:, :P], q_low[:, P:], low)], axis=1))
    a["w_key"] = np.ascontiguousarray(k_major(key))
    a["w_v_a"] = np.ascontiguousarray(k_major(v_a))
    up = i["ml_w_kv_up"][0].reshape(P, B_HEADS, B_NOPE + B_V)
    a["w_k_up"] = np.ascontiguousarray(up[:, :, :B_NOPE].reshape(P, -1))
    a["w_v_up"] = np.ascontiguousarray(up[:, :, B_NOPE:].reshape(P, -1))
    a["w_q_up"] = np.ascontiguousarray(k_major(i["ml_w_q_up"][0]))
    a["w_out0"] = pieces(i["at_w_out"][0], P)
    w_hy, w_z, w_xbc, w_dt = np.split(i["lc_w_in"][0], np.cumsum([1536, 512, 1024]), axis=1)
    a["w_hy"], a["w_z"], a["w_xbc"] = pieces(w_hy, P), pieces(w_z, P), pieces(w_xbc, P)
    a["w_dt"] = np.ascontiguousarray(k_major(w_dt))
    a["w_out1"] = pieces(i["lc_w_out"][0], P)
    a["hy_w1"], a["hy_w2"], a["hy_w3"] = (np.ascontiguousarray(i[n][0]) for n in ("hy_w1", "hy_w2", "hy_w3"))
    a.update(hyena_tables())
    a.update(rope_tables())

    v = np.zeros((P, NVEC), np.float32)
    def put(name, cols, at=0):
        v[:cols.shape[0], VEC[name][0] + at:VEC[name][0] + at + cols.shape[1]] = cols
    put("ada_b", np.repeat(feature_tiles(i["ada_b"]), 2, axis=1))
    put("norm_g", np.repeat(feature_tiles(i["norm_g"]), 2, axis=1))
    put("gain_k", np.tile(i["ga_k_norm"][0], 2)[:, None])
    put("gain_q", np.tile(i["ga_q_norm"][0], 2)[:, None])
    put("mlq", feature_tiles(i["ml_q_norm"][0]))
    put("mlkv", feature_tiles(i["ml_kv_norm"][0]))
    put("short_w", feature_tiles(i["hy_short_w"][0]))
    put("short_b", feature_tiles(i["hy_short_b"][0]))
    put("skip", feature_tiles(i["hy_skip"][0]))
    put("conv_w", feature_tiles(i["mb_conv_w"][0]))
    put("conv_b", feature_tiles(i["mb_conv_b"][0]))
    put("d_skip", feature_tiles(np.repeat(i["mb_d_skip"][0], 64)))
    put("mb_norm", feature_tiles(i["mb_norm"][0]))
    put("dt_bias", np.tile(i["mb_dt_bias"][0].reshape(1, 16), (P, 1)))
    put("a_log", np.tile(i["mb_a_log"][0].reshape(1, 16), (P, 1)))
    put("hy_b1", i["hy_b1"][0][:, None])
    put("hy_b2", i["hy_b2"][0][:, None])
    put("freq", i["hy_freq"][0][:, None])
    a["vec"] = v
    return a


def kernel(**inputs):
    import concourse.bacc as bacc
    from concourse.bass_utils import run_bass_kernel_spmd

    nc = bacc.Bacc("TRN2", target_bir_lowering=False, num_devices=1)
    laid_out = lay_out({name: np.asarray(a) for name, a in inputs.items()})
    d, arrays = {}, {}
    for name, a in laid_out.items():
        arrays[f"in_{name}_dram"] = a
        d[name] = nc.dram_tensor(f"in_{name}_dram", a.shape, mybir.dt.from_np(a.dtype), kind="ExternalInput").ap()
    d["out"] = nc.dram_tensor("out_0_dram", (P, KT, LAT), F32, kind="ExternalOutput").ap()
    build_program(nc, d)
    r = run_bass_kernel_spmd(nc, [arrays], core_ids=[0])
    got = r.results[0]["out_0_dram"]
    return np.ascontiguousarray(got.transpose(2, 1, 0).reshape(1, LAT, D))
```

```python
from contextlib import ExitStack, contextmanager
import math

import numpy as np
import concourse.bass as bass
from concourse import mybir

F32 = mybir.dt.float32
F32R = mybir.dt.float32r
ACT = mybir.ActivationFunctionType
ALU = mybir.AluOpType
AX = mybir.AxisListType

P = 128
D = 1024
KT = D // P
LAT, CTX = 1024, 256
TOK = LAT + CTX
CHUNKS = [(0, 512), (512, 512), (1024, 256)]
STREAMS = [(0, LAT), (LAT, CTX)]
EPS = 1e-6
FF = 4 * D
GRID_W = 64
THETA = 10000.0
BANK = 512

A_DIM, A_HEADS = 64, 8
B_NOPE, B_ROPE, B_V, B_HEADS = 64, 32, 64, 8
B_DK = B_NOPE + B_ROPE
A_SCALE = A_DIM ** -0.5
B_SCALE = B_DK ** -0.5
KTILES = TOK // P
SQUARES_AT = 5
SHIFT_A, SCALE_A, GATE_A, SHIFT_M, SCALE_M, GATE_M = range(6)

VEC = {}
_at = 0
for _name, _n in (("ada_b", 2 * 96), ("norm_g", 2 * 4 * 16), ("gain_k", 1), ("gain_q", 1), ("mlq", 2), ("mlkv", 1),
                  ("short_w", 36), ("short_b", 12), ("skip", 8), ("conv_w", 24), ("conv_b", 8),
                  ("d_skip", 4), ("mb_norm", 4), ("dt_bias", 16), ("a_log", 16), ("hy_b1", 1), ("hy_b2", 1), ("freq", 1)):
    VEC[_name] = (_at, _n)
    _at += _n
NVEC = _at


STAGES = []


def tile(nc, mem, name, shape, side="left", dtype=F32):
    return mem.enter_context(nc.sbuf_tensor(name, shape, dtype, side=side, allow_name_mangling=True))


def tile_r(nc, mem, name, shape, side="left"):
    return tile(nc, mem, name, shape, side, F32R)


@contextmanager
def stage(nc, names):
    STAGES.append(names)
    sems = [nc.alloc_semaphore(f"{n}_{len(STAGES)}") for n in names.split()]
    with ExitStack() as mem:
        yield mem, sems
    nc.clear_and_free_semaphores(sems)
    nc.all_engine_barrier(sem_only=True)


def vec(g, name, i=0, n=1):
    at = VEC[name][0] + i
    return g.vec[:, at:at + n]


class Globals:
    pass


def load_constants(nc, g, d):
    with stage(nc, "loaded cond_ready gain_ready") as (mem, (loaded, cond_ready, gain_ready)):
        with nc.Block() as block:
            @block.sync
            def _(sp):
                for dst, src in ((g.vec, d["vec"]), (g.ident, d["ident"]), (g.ones, d["ones"]), (g.cond, d["cond"])):
                    sp.dma_start(dst[:], src).then_inc(loaded, 16)

            @block.scalar
            def _(act):
                act.wait_ge(loaded, 64)
                act.activation(g.cond[:], g.cond[:], ACT.Silu).then_inc(cond_ready, 1)

            @block.vector
            def _(dve):
                dve.memset(g.eps[:], EPS).then_inc(gain_ready, 1)
                dve.wait_ge(loaded, 64)
                dve.tensor_scalar(vec(g, "gain_q"), vec(g, "gain_q"), A_SCALE, None, ALU.mult).then_inc(gain_ready, 1)


ADA_PIECES = 6 * D // BANK


def fold_gains(g, dve, layer, folded):
    for n, part in enumerate((SCALE_A, GATE_A, SCALE_M, GATE_M)):
        gains = vec(g, "norm_g", (layer * 4 + n) * 16, 16)
        now = g.mod[:, layer, part].rearrange("p k s -> p (k s)")
        if part in (SCALE_A, SCALE_M):
            dve.scalar_tensor_tensor(out=now, in0=now, scalar=1.0, in1=gains, op0=ALU.add, op1=ALU.mult).then_inc(folded, 1)
        else:
            dve.tensor_tensor(now, now, gains, ALU.mult).then_inc(folded, 1)


def adaln_0(nc, g, d):
    SLOTS, PIECES, GROUPS = 4, ADA_PIECES, 4
    PART = BANK // P
    with stage(nc, "w_in0 w_in1 w_in2 w_in3 sel_in product read_out turned biased folded") as (mem, sems):
        w_in, (sel_in, product, read_out, turned, biased, folded) = sems[:4], sems[4:]
        w = tile(nc, mem, "ada_ring", [P, SLOTS, KT, BANK])
        rows = tile(nc, mem, "ada_rows", [P, SLOTS, BANK])
        sel = tile(nc, mem, "group_selector", [P, 2])
        src = d["ada_w"]
        WIDTH = PIECES * PART * 2
        acc = g.ps[:, SLOTS, 0:WIDTH]
        with nc.Block() as block:
            @block.sync
            def _(sp):
                sp.dma_start(sel[:], d["group_selector"]).then_inc(sel_in, 16)
                for s in range(SLOTS):
                    sp.dma_start(w[:, s], src[s]).then_inc(w_in[s], 16)
                with sp.Fori(1, PIECES // SLOTS) as i:
                    for s in range(SLOTS):
                        sp.wait_ge(product, (i - 1) * SLOTS + (s + 1))
                        sp.dma_start(w[:, s], src[bass.ds(i * SLOTS + s, 1)].rearrange("a p k n -> p (a k) n")).then_inc(w_in[s], 16)

            @block.tensor
            def _(pe):
                pe.wait_ge(sel_in, 16)
                with pe.Fori(0, PIECES // SLOTS) as i:
                    for s in range(SLOTS):
                        pe.wait_ge(w_in[s], (i + 1) * 16)
                        pe.wait_ge(read_out, i * SLOTS + (s + 1))
                        for half in range(KT // GROUPS):
                            for c in range(GROUPS):
                                mm = pe.matmul(g.ps[32 * c:32 * c + 32, s, :], g.cond[:, half * GROUPS + c, :], w[:, s, half * GROUPS + c, :],
                                               start=(half == 0), stop=(half == 1), tile_position=(0, 32 * c))
                        mm.then_inc(product, 1)
                    for s in range(SLOTS):
                        pe.wait_ge(read_out, i * SLOTS + (SLOTS + s + 1))
                        for m in range(PART):
                            mm = pe.matmul(g.ps[:, SLOTS, bass.ds(i * (2 * PART * SLOTS) + (2 * PART * s + 2 * m), 2)],
                                           rows[:, s, m * P:(m + 1) * P], sel[:], start=True, stop=True)
                        mm.then_inc(turned, 1)

            @block.scalar
            def _(act):
                act.sem_inc(read_out, SLOTS)
                with act.Fori(0, PIECES // SLOTS) as i:
                    for s in range(SLOTS):
                        act.wait_ge(product, i * SLOTS + (s + 1))
                        act.activation(rows[:, s, :], g.ps[:, s, :], ACT.Copy).then_inc(read_out, 1)

            @block.vector
            def _(dve):
                dve.wait_ge(turned, PIECES)
                flat = g.mod[:, 0].rearrange("p a k s -> p (a k s)")
                dve.tensor_tensor(flat, acc, vec(g, "ada_b", 0, WIDTH), ALU.add).then_inc(biased, 1)
                dve.wait_ge(biased, 1)
                fold_gains(g, dve, 0, folded)


class Adaln1:
    SLOTS = 3

    def __init__(self, nc, g, d, mem, sems):
        self.g, self.w_in = g, sems[:3]
        self.sel_in, self.made, self.copied, self.turned, self.biased, self.folded = sems[3:]
        self.w = tile(nc, mem, "ada_ring", [P, self.SLOTS, KT, BANK])
        self.rows = tile(nc, mem, "ada_rows", [P, BANK])
        self.sel = tile(nc, mem, "group_selector", [P, 2])
        self.src, self.sel_src = d["ada_w"], d["group_selector"]
        self.bank = g.ps[:, 7, :]

    def load(self, sp, i):
        if i >= ADA_PIECES:
            return
        if i == 0:
            sp.dma_start(self.sel[:], self.sel_src).then_inc(self.sel_in, 16)
        if i >= self.SLOTS:
            sp.wait_ge(self.made, i - self.SLOTS + 1)
        sp.dma_start(self.w[:, i % self.SLOTS], self.src[ADA_PIECES + i]).then_inc(self.w_in[i % self.SLOTS], 16)

    def multiply(self, pe, i):
        if i >= ADA_PIECES:
            return
        s = i % self.SLOTS
        pe.wait_ge(self.w_in[s], 16 * (i // self.SLOTS + 1))
        if i >= 1:
            pe.wait_ge(self.biased, i)
        for half in range(2):
            for c in range(4):
                mm = pe.matmul(self.g.ps[32 * c:32 * c + 32, 7, :], self.g.cond[:, half * 4 + c, :], self.w[:, s, half * 4 + c, :],
                               start=(half == 0), stop=(half == 1), tile_position=(0, 32 * c))
        mm.then_inc(self.made, 1)

    def copy(self, act, i):
        if not 0 <= i < ADA_PIECES:
            return
        act.wait_ge(self.made, i + 1)
        if i >= 1:
            act.wait_ge(self.turned, i)
        act.activation(self.rows[:], self.bank, ACT.Copy).then_inc(self.copied, 1)

    def turn(self, pe, i):
        if not 0 <= i < ADA_PIECES:
            return
        if i == 0:
            pe.wait_ge(self.sel_in, 16)
        pe.wait_ge(self.copied, i + 1)
        for m in range(BANK // P):
            mm = pe.matmul(self.bank[:, 2 * m:2 * m + 2], self.rows[:, m * P:(m + 1) * P], self.sel[:], start=True, stop=True)
        mm.then_inc(self.turned, 1)

    def bias(self, dve, i):
        if not 0 <= i < ADA_PIECES:
            return
        flat = self.g.mod[:, 1].rearrange("p a k s -> p (a k s)")
        dve.wait_ge(self.turned, i + 1)
        dve.tensor_tensor(flat[:, 8 * i:8 * i + 8], self.bank[:, 0:8], vec(self.g, "ada_b", 8 * (ADA_PIECES + i), 8), ALU.add).then_inc(self.biased, 1)
        if i == ADA_PIECES - 1:
            dve.wait_ge(self.biased, ADA_PIECES)
            fold_gains(self.g, dve, 1, self.folded)


def load(nc, pairs):
    with stage(nc, "loaded") as (mem, (loaded,)):
        with nc.Block() as block:
            @block.sync
            def _(sp):
                n = 0
                for dst, src in pairs:
                    for k in range(src.shape[1]):
                        sp.dma_start(dst[:, k, :], src[:, k, :]).then_inc(loaded, 16)
                        n += 1
                sp.wait_ge(loaded, 16 * n)


def chunks_of(tokens):
    return [(a, n) for a, n in CHUNKS if a < tokens]


def residual_norm(nc, g, x_src, x_dst, out, gate, norm, tokens, squares_made=False):
    spans = chunks_of(tokens)
    C = len(spans)
    RING = 4
    stream = [0 if a < LAT else 1 for a, n in spans]
    names = ("x_in0 x_in1 x_in2 x_stored squared_1 used_1 logged_1 rstd_1 gated added_even added_odd squared_2 used_2 logged_2 rstd_2 "
             "scaled rounded split")
    with stage(nc, names) as (mem, sems):
        x_in = sems[:C]
        (x_stored, squared_1, used_1, logged_1, rstd_1, gated, added_even, added_odd, squared_2, used_2, logged_2, rstd_2,
         scaled, rounded, split) = sems[3:]
        added = (added_even, added_odd)
        x = tile(nc, mem, "x", [P, KT, tokens])
        sq_1, sq_2, t = (tile(nc, mem, f"norm_{name}", [P, RING, BANK]) for name in ("square_out", "square_x", "scaled"))
        rs_1, rs_2 = tile(nc, mem, "rstd_out", [P, tokens]), tile(nc, mem, "rstd_x", [P, tokens])
        mod = lambda which, part, k, c: g.mod[:, which[0], part, k, stream[c]:stream[c] + 1]

        def in_turn(first, second, third):
            for c in range(C + 2):
                if c < C:
                    first(c)
                if norm and 0 <= c - 1 < C:
                    second(c - 1)
                if norm and 0 <= c - 2 < C:
                    third(c - 2)

        with nc.Block() as block:
            @block.sync
            def _(sp):
                for c, (a, n) in enumerate(spans):
                    sp.dma_start(x[:, :, a:a + n], x_src[:, :, a:a + n]).then_inc(x_in[c], 16)
                if gate:
                    for c, (a, n) in enumerate(spans):
                        for half in range(2):
                            sp.wait_ge(added[half], (c + 1) * KT // 2)
                        sp.dma_start(x_dst[:, :, a:a + n], x[:, :, a:a + n]).then_inc(x_stored, 16)
                    sp.wait_ge(x_stored, 16 * C)

            @block.scalar
            def _(act):
                act.preload_act_table_set("natural_log_exp_and_others")

                def root(c, used, bank, rs, logged, rstd, needed):
                    a, n = spans[c]
                    if needed:
                        act.wait_ge(used, (c + 1) * KT)
                    act.activation(rs[:, a:a + n], g.ps[:, bank + c, 0:n], ACT.Ln, bias=g.eps[:], scale=1.0 / D).then_inc(logged, 1)
                    act.wait_ge(logged, c + 1)
                    act.activation(rs[:, a:a + n], rs[:, a:a + n], ACT.Exp, scale=-0.5).then_inc(rstd, 1)

                def of_out(c):
                    a, n = spans[c]
                    if gate and not squares_made:
                        for k in range(KT):
                            q = c * KT + k
                            if q >= RING:
                                act.wait_ge(used_1, q - RING + 1)
                            act.activation(sq_1[:, q % RING, 0:n], out[:, k, a:a + n], ACT.Square).then_inc(squared_1, 1)
                    if gate:
                        root(c, used_1, SQUARES_AT, rs_1, logged_1, rstd_1, not squares_made)

                def of_x(c):
                    a, n = spans[c]
                    for k in range(KT):
                        q = c * KT + k
                        if gate:
                            act.wait_ge(added[k % 2], q // 2 + 1)
                        else:
                            act.wait_ge(x_in[c], 16)
                        if q >= RING:
                            act.wait_ge(used_2, q - RING + 1)
                        act.activation(sq_2[:, q % RING, 0:n], x[:, k, a:a + n], ACT.Square).then_inc(squared_2, 1)
                    root(c, used_2, 0, rs_2, logged_2, rstd_2, True)

                def shift(c):
                    a, n = spans[c]
                    for k in range(KT):
                        q = c * KT + k
                        act.wait_ge(scaled, q + 1)
                        act.activation(g.high[:, k, a:a + n], t[:, q % RING, 0:n], ACT.Identity, bias=mod(norm, norm[2], k, c)).then_inc(rounded, 1)

                in_turn(of_out, of_x, shift)

            @block.tensor
            def _(pe):
                def add_squares(c, squared, used, sq, bank):
                    a, n = spans[c]
                    for k in range(KT):
                        q = c * KT + k
                        pe.wait_ge(squared, q + 1)
                        pe.matmul(g.ps[:, bank + c, 0:n], g.ones[:], sq[:, q % RING, 0:n], start=(k == 0), stop=(k == KT - 1)).then_inc(used, 1)

                def of_out(c):
                    if gate and not squares_made:
                        add_squares(c, squared_1, used_1, sq_1, SQUARES_AT)

                in_turn(of_out, lambda c: add_squares(c, squared_2, used_2, sq_2, 0), lambda c: None)

            @block.gpsimd
            def _(pool):
                for c, (a, n) in enumerate(spans if gate else []):
                    pool.wait_ge(x_in[c], 16)
                    for k in range(1, KT, 2):
                        pool.wait_ge(gated, c * KT + k + 1)
                        pool.tensor_tensor(x[:, k, a:a + n], x[:, k, a:a + n], out[:, k, a:a + n], ALU.add).then_inc(added_odd, 1)

            @block.vector
            def _(dve):
                def add(c):
                    if not gate:
                        return
                    a, n = spans[c]
                    dve.wait_ge(x_in[c], 16)
                    dve.wait_ge(rstd_1, c + 1)
                    for k in range(KT):
                        q = c * KT + k
                        dve.scalar_tensor_tensor(out=out[:, k, a:a + n], in0=out[:, k, a:a + n], scalar=mod(gate, gate[1], k, c),
                                                 in1=rs_1[:, a:a + n], op0=ALU.mult, op1=ALU.mult).then_inc(gated, 1)
                        if k % 2:
                            dve.wait_ge(gated, q)
                            dve.tensor_tensor(x[:, k - 1, a:a + n], x[:, k - 1, a:a + n], out[:, k - 1, a:a + n], ALU.add).then_inc(added_even, 1)

                def split_norm(c):
                    a, n = spans[c]
                    dve.wait_ge(rstd_2, c + 1)
                    LAG = 2
                    for k in range(KT + LAG):
                        q = c * KT + k
                        if k < KT:
                            if q >= RING:
                                dve.wait_ge(split, q - RING + 1)
                            dve.scalar_tensor_tensor(out=t[:, q % RING, 0:n], in0=x[:, k, a:a + n], scalar=mod(norm, norm[1], k, c),
                                                     in1=rs_2[:, a:a + n], op0=ALU.mult, op1=ALU.mult).then_inc(scaled, 1)
                        if k >= LAG:
                            v = k - LAG
                            dve.wait_ge(rounded, q - LAG + 1)
                            dve.scalar_tensor_tensor(out=g.low[:, v, a:a + n], in0=t[:, (q - LAG) % RING, 0:n], scalar=mod(norm, norm[2], v, c),
                                                     in1=g.high[:, v, a:a + n], op0=ALU.add, op1=ALU.subtract).then_inc(split, 1)

                in_turn(add, lambda c: None, split_norm)


class WeightRing:

    def __init__(self, nc, mem, sems, product, after, shape=(KT, P)):
        self.raw_in, (self.rounded, self.split) = sems[:2], sems[2:]
        self.product, self.after = product, after
        self.raw = tile(nc, mem, "w_raw", [P, 2, *shape])
        self.high, self.low = tile_r(nc, mem, "w_high", [P, 2, *shape]), tile_r(nc, mem, "w_low", [P, 2, *shape])
        self.pieces = len(after)

    def load(self, sp, t, src):
        if t >= 2:
            sp.wait_ge(self.split, t - 1)
        sp.dma_start(self.raw[:, t % 2], src).then_inc(self.raw_in[t % 2], 16)

    def round_piece(self, act, t):
        if t >= self.pieces:
            return
        act.wait_ge(self.raw_in[t % 2], 16 * (t // 2 + 1))
        if t >= 2:
            act.wait_ge(self.product, self.after[t - 2])
        act.activation(self.high[:, t % 2], self.raw[:, t % 2], ACT.Copy).then_inc(self.rounded, 1)

    def split_piece(self, dve, t):
        if t >= self.pieces:
            return
        dve.wait_ge(self.rounded, t + 1)
        dve.tensor_tensor(self.low[:, t % 2], self.raw[:, t % 2], self.high[:, t % 2], ALU.subtract).then_inc(self.split, 1)

    def product_of(self, pe, out, t, high, low, a, n):
        w_high, w_low = self.high[:, t % 2], self.low[:, t % 2]
        for k in range(KT):
            for i, (x, y) in enumerate(((w_high, high), (w_high, low), (w_low, high))):
                mm = pe.matmul(out, x[:, k, :], y[:, k, a:a + n], start=(k == 0 and i == 0), stop=(k == KT - 1 and i == 2))
        return mm


def mlp(nc, g, out, high, low, w, tokens):
    EIGHTHS, PIECES, HT, BANKS = 8, 8, 4, 4
    spans = chunks_of(tokens)
    C = len(spans)
    UP, DOWN = HT * C, 2 * HT * C
    ALL = UP + DOWN
    names = "w_in0 w_in1 w_rounded w_split product up_free down_free rectified squared rounded hid_split cleared"
    with stage(nc, names) as (mem, sems):
        w_in, (w_rounded, w_split, product, up_free, down_free, rectified, squared, rounded, hid_split, cleared) = sems[:2], sems[2:]
        raw = tile(nc, mem, "w_raw", [P, 2, KT, P])
        w_hi, w_lo = tile_r(nc, mem, "w_high", [P, 2, KT, P]), tile_r(nc, mem, "w_low", [P, 2, KT, P])
        hid_hi, hid_lo = tile_r(nc, mem, "hid_high", [P, HT, tokens]), tile_r(nc, mem, "hid_low", [P, HT, tokens])
        relu, square = tile(nc, mem, "hid_relu", [P, 2, BANK]), tile(nc, mem, "hid_square", [P, 2, BANK])

        def products_before(e, j):
            done = (j + 1) * C if j < HT else UP + (j + 1 - HT) * 2 * C
            return e * ALL + done

        with nc.Block() as block:
            @block.sync
            def _(sp):
                def load(piece, slot):
                    sp.dma_start(raw[:, slot], w[bass.ds(piece, 1)].rearrange("a p k n -> p (a k) n")).then_inc(w_in[slot], 16)
                load(0, 0)
                load(1, 1)
                def eighth(e, last):
                    for j in range(PIECES - 2 if last else PIECES):
                        sp.wait_ge(w_split, e * PIECES + (j + 1))
                        load(e * PIECES + (j + 2), j % 2)
                with sp.Fori(0, EIGHTHS - 1) as e:
                    eighth(e, False)
                eighth(EIGHTHS - 1, True)

            @block.tensor
            def _(pe):
                with pe.Fori(0, EIGHTHS) as e:
                    for j in range(PIECES):
                        pe.wait_ge(w_split, e * PIECES + (j + 1))
                        wh, wl = w_hi[:, j % 2], w_lo[:, j % 2]
                        if j < HT:
                            for c, (a, n) in enumerate(spans):
                                u = j * C + c
                                pe.wait_ge(up_free, e * UP + (u + 1))
                                for k in range(KT):
                                    for i, (x, y) in enumerate(((wh, high), (wh, low), (wl, high))):
                                        mm = pe.matmul(g.ps[:, u % BANKS, 0:n], x[:, k, :], y[:, k, a:a + n],
                                                       start=(k == 0 and i == 0), stop=(k == KT - 1 and i == 2))
                                mm.then_inc(product, 1)
                        else:
                            for half in range(2):
                                for c, (a, n) in enumerate(spans):
                                    u = ((j - HT) * 2 + half) * C + c
                                    pe.wait_ge(down_free, e * DOWN + (u + 1))
                                    if u < C:
                                        pe.wait_ge(hid_split, e * UP + ((HT - 1) * C + c + 1))
                                    for k in range(HT):
                                        for i, (x, y) in enumerate(((wh, hid_hi), (wh, hid_lo), (wl, hid_hi))):
                                            mm = pe.matmul(g.ps[:, BANKS + u % BANKS, 0:n], x[:, k * 2 + half, :], y[:, k, a:a + n],
                                                           start=(k == 0 and i == 0), stop=(k == HT - 1 and i == 2))
                                    mm.then_inc(product, 1)

            @block.scalar
            def _(act):
                act.sem_inc(up_free, BANKS)
                def round_piece(e, j):
                    slot = (j + 1) % 2
                    act.wait_ge(w_in[slot], e * (8 * PIECES) + 16 * ((j + 1) // 2 + 1))
                    if j >= 1:
                        act.wait_ge(product, products_before(e, j - 1))
                    act.activation(w_hi[:, slot], raw[:, slot], ACT.Copy).then_inc(w_rounded, 1)
                def eighth(e, last, first=False):
                    for j in range(PIECES):
                        if j == 0 and not first:
                            act.wait_ge(product, e * ALL)
                        if not (last and j == PIECES - 1):
                            round_piece(e, j)
                        if j < HT:
                            for c, (a, n) in enumerate(spans):
                                u = j * C + c
                                act.wait_ge(product, e * ALL + (u + 1))
                                if u >= 2 or not first:
                                    act.wait_ge(hid_split, e * UP + (u - 1))
                                act.activation(relu[:, u % 2, 0:n], g.ps[:, u % BANKS, 0:n], ACT.Relu).then_inc(up_free, 1)
                                act.wait_ge(up_free, e * UP + (BANKS + u + 1))
                                act.activation(square[:, u % 2, 0:n], relu[:, u % 2, 0:n], ACT.Square).then_inc(squared, 1)
                act.wait_ge(w_in[0], 16)
                act.activation(w_hi[:, 0], raw[:, 0], ACT.Copy).then_inc(w_rounded, 1)
                eighth(0, False, True)
                with act.Fori(1, EIGHTHS - 1) as e:
                    eighth(e, False)
                eighth(EIGHTHS - 1, True)

            @block.vector
            def _(dve):
                dve.sem_inc(down_free, BANKS)
                def split_piece(e, j):
                    slot = (j + 1) % 2
                    dve.wait_ge(w_rounded, e * PIECES + (j + 2))
                    dve.tensor_tensor(w_lo[:, slot], raw[:, slot], w_hi[:, slot], ALU.subtract).then_inc(w_split, 1)
                def eighth(e, last):
                    for j in range(PIECES):
                        if not (last and j == PIECES - 1):
                            split_piece(e, j)
                        if j < HT:
                            for c, (a, n) in enumerate(spans):
                                u = j * C + c
                                dve.wait_ge(up_free, e * UP + (BANKS + u + 1))
                                dve.tensor_tensor(hid_hi[:, j, a:a + n], relu[:, u % 2, 0:n], relu[:, u % 2, 0:n], ALU.mult).then_inc(rounded, 1)
                                dve.wait_ge(rounded, e * UP + (u + 1))
                                dve.wait_ge(squared, e * UP + (u + 1))
                                dve.tensor_tensor(hid_lo[:, j, a:a + n], square[:, u % 2, 0:n], hid_hi[:, j, a:a + n], ALU.subtract).then_inc(hid_split, 1)
                        else:
                            for half in range(2):
                                m = (j - HT) * 2 + half
                                for c, (a, n) in enumerate(spans):
                                    u = m * C + c
                                    dve.wait_ge(product, e * ALL + (UP + u + 1))
                                    dve.tensor_tensor(out[:, m, a:a + n], out[:, m, a:a + n],
                                                      g.ps[:, BANKS + u % BANKS, 0:n], ALU.add).then_inc(down_free, 1)
                dve.wait_ge(w_rounded, 1)
                dve.tensor_tensor(w_lo[:, 0], raw[:, 0], w_hi[:, 0], ALU.subtract).then_inc(w_split, 1)
                dve.memset(out[:, :, 0:tokens], 0.0).then_inc(cleared, 1)
                dve.wait_ge(cleared, 1)
                with dve.Fori(0, EIGHTHS - 1) as e:
                    eighth(e, False)
                eighth(EIGHTHS - 1, True)


def project_attention(nc, g, d, sc):
    TILES = 5
    units = [(t, a, n) for t in range(TILES) for a, n in CHUNKS]
    U = len(units)
    C = len(CHUNKS)

    names = "raw_in0 raw_in1 w_rounded w_split tabs_in product raw_out squared meaned logged rstd normed rotated halves roped stored0 stored1"
    names += " ada_in0 ada_in1 ada_in2 sel_in made copied turned biased folded"
    with stage(nc, names) as (mem, sems):
        tabs_in, product, raw_out, squared, meaned, logged, rstd, normed, rotated, halves, roped = sems[4:15]
        stored = sems[15:17]
        ada = Adaln1(nc, g, d, mem, sems[17:])
        ring = WeightRing(nc, mem, sems[:4], product, [C * (t + 1) for t in range(TILES)])
        cos, sin = tile(nc, mem, "cos_a", [P, TOK]), tile(nc, mem, "sin_a", [P, TOK])
        by_head, swap = tile(nc, mem, "ones_by_head", [P, P]), tile(nc, mem, "swap_halves", [P, P])
        raw, sq, rs, nrm, t1, t2, res = (tile(nc, mem, f"a_{x}", [P, 2, BANK]) for x in ("raw", "sq", "rs", "nrm", "t1", "t2", "res"))
        with nc.Block() as block:
            @block.sync
            def _(sp):
                for t in range(2):
                    ring.load(sp, t, d["w_qk"][t])
                for dst, src in ((cos, "cos_a"), (sin, "sin_a"), (by_head, "by_head"), (swap, "swap_a")):
                    sp.dma_start(dst[:], d[src]).then_inc(tabs_in, 16)
                for i in range(ada.SLOTS):
                    ada.load(sp, i)
                for u, (t, a, n) in enumerate(units):
                    ada.load(sp, u + ada.SLOTS)
                    if u % C == 0 and t + 2 < TILES:
                        ring.load(sp, t + 2, d["w_qk"][t + 2])
                    sp.wait_ge(roped, u + 1)
                    sp.dma_start(sc.qk_a[t][:, a:a + n], res[:, u % 2, 0:n]).then_inc(stored[u % 2], 16)
                sp.wait_ge(stored[0], 16 * ((U + 1) // 2))
                sp.wait_ge(stored[1], 16 * (U // 2))

            @block.tensor
            def _(pe):
                pe.wait_ge(tabs_in, 64)
                for step in range(U + 2):
                    if step < U:
                        t, a, n = units[step]
                        if step >= 3:
                            pe.wait_ge(squared, step - 2)
                        if step % C == 0:
                            pe.wait_ge(ring.split, t + 1)
                        ring.product_of(pe, g.ps[:, step % 3, 0:n], t, g.high, g.low, a, n).then_inc(product, 1)
                    ada.turn(pe, step - 1)
                    ada.multiply(pe, step)
                    if 0 <= step - 1 < U:
                        v = step - 1
                        n = units[v][2]
                        pe.wait_ge(squared, v + 1)
                        if v >= 2:
                            pe.wait_ge(logged, v - 1)
                        pe.matmul(g.ps[:, 3 + v % 2, 0:n], by_head[:], sq[:, v % 2, 0:n], start=True, stop=True).then_inc(meaned, 1)
                    if 0 <= step - 2 < U:
                        v = step - 2
                        n = units[v][2]
                        pe.wait_ge(normed, v + 1)
                        if v >= 2:
                            pe.wait_ge(halves, 2 * (v - 1))
                        pe.matmul(g.ps[:, 5 + v % 2, 0:n], swap[:], nrm[:, v % 2, 0:n], start=True, stop=True).then_inc(rotated, 1)

            @block.scalar
            def _(act):
                act.preload_act_table_set("natural_log_exp_and_others")
                ring.round_piece(act, 0)
                for step in range(U + 1):
                    ada.copy(act, step - 1)
                    if step < U and step % C == 1:
                        ring.round_piece(act, step // C + 1)
                    if step < U:
                        n = units[step][2]
                        act.wait_ge(product, step + 1)
                        if step >= 2:
                            act.wait_ge(normed, step - 1)
                            act.wait_ge(meaned, step - 1)
                        act.activation(raw[:, step % 2, 0:n], g.ps[:, step % 3, 0:n], ACT.Copy).then_inc(raw_out, 1)
                        act.activation(sq[:, step % 2, 0:n], g.ps[:, step % 3, 0:n], ACT.Square).then_inc(squared, 1)
                    if step >= 1:
                        v = step - 1
                        n = units[v][2]
                        act.wait_ge(meaned, v + 1)
                        if v >= 2:
                            act.wait_ge(normed, v - 1)
                        act.activation(rs[:, v % 2, 0:n], g.ps[:, 3 + v % 2, 0:n], ACT.Ln, bias=g.eps[:], scale=1.0 / A_DIM).then_inc(logged, 1)
                        act.wait_ge(logged, v + 1)
                        act.activation(rs[:, v % 2, 0:n], rs[:, v % 2, 0:n], ACT.Exp, scale=-0.5).then_inc(rstd, 1)

            @block.vector
            def _(dve):
                ring.split_piece(dve, 0)
                dve.wait_ge(tabs_in, 64)
                for step in range(1, U + 2):
                    ada.bias(dve, step - 1)
                    if step < U and step % C == 1:
                        ring.split_piece(dve, step // C + 1)
                    if step <= U:
                        v = step - 1
                        t, a, n = units[v]
                        dve.wait_ge(raw_out, v + 1)
                        dve.wait_ge(rstd, v + 1)
                        if v >= 2:
                            dve.wait_ge(rotated, v - 1)
                            dve.wait_ge(halves, 2 * (v - 1))
                        gain = vec(g, "gain_k" if t == 0 else "gain_q")
                        dve.scalar_tensor_tensor(out=nrm[:, v % 2, 0:n], in0=raw[:, v % 2, 0:n], scalar=gain,
                                                 in1=rs[:, v % 2, 0:n], op0=ALU.mult, op1=ALU.mult).then_inc(normed, 1)
                    if step >= 2:
                        v = step - 2
                        t, a, n = units[v]
                        dve.wait_ge(normed, v + 1)
                        dve.wait_ge(rotated, v + 1)
                        if v >= 2:
                            dve.wait_ge(roped, v - 1)
                            dve.wait_ge(stored[v % 2], 16 * (v // 2))
                        dve.tensor_tensor(t1[:, v % 2, 0:n], nrm[:, v % 2, 0:n], cos[:, a:a + n], ALU.mult).then_inc(halves, 1)
                        dve.tensor_tensor(t2[:, v % 2, 0:n], g.ps[:, 5 + v % 2, 0:n], sin[:, a:a + n], ALU.mult).then_inc(halves, 1)
                        dve.wait_ge(halves, 2 * (v + 1))
                        dve.tensor_tensor(res[:, v % 2, 0:n], t1[:, v % 2, 0:n], t2[:, v % 2, 0:n], ALU.add).then_inc(roped, 1)

    q_low = tile(nc, sc.mem, "q_low", [P, 2, TOK])
    kv_low = tile(nc, sc.mem, "kv_low", [P, TOK])
    groups = [((0, 1), (q_low[:, 0, :], q_low[:, 1, :]), ("mlq", 0), 256), ((2,), (kv_low[:],), ("mlkv", 0), 128)]
    gunits = [(gi, a, n) for gi in range(2) for a, n in CHUNKS]
    names = "raw_in0 raw_in1 w_rounded w_split w_in key_w_rounded key_w_split v_row tabs_in product squared meaned logged rstd normed key_raw key_read key_rotated key_halves key_roped key_stored v_product v_out v_stored0 v_stored1"
    with stage(nc, names) as (mem, sems):
        (w_in, key_w_rounded, key_w_split, v_row, tabs_in, product, squared, meaned, logged, rstd, normed, key_raw, key_read,
         key_rotated, key_halves, key_roped, key_stored, v_product, v_out) = sems[4:23]
        v_stored = sems[23:]
        ring = WeightRing(nc, mem, sems[:4], product, [2 * C - 1, 2 * C, 3 * C, 4 * C])
        w_key = tile(nc, mem, "w_key", [P, KT, B_ROPE])
        w_key_high, w_key_low = tile_r(nc, mem, "w_key_high", [P, KT, B_ROPE]), tile_r(nc, mem, "w_key_low", [P, KT, B_ROPE])
        v_rows = tile(nc, mem, "v_rows", [P, TOK])
        cos, sin = tile(nc, mem, "cos_b", [P, TOK]), tile(nc, mem, "sin_b", [P, TOK])
        swap = tile(nc, mem, "swap_b", [P, P])
        sq = tile(nc, mem, "b_sq", [P, 3, BANK])
        raw = tile(nc, mem, "b_raw", [P, 3, BANK])
        rs = tile(nc, mem, "b_rs", [P, 2, BANK])
        key, kt1, kt2 = (tile(nc, mem, f"key_{x}", [P, TOK]) for x in ("raw", "t1", "t2"))
        vt = tile(nc, mem, "v_tile", [P, 2, P])
        tiles = [(gi, ti, a, n) for gi, a, n in gunits for ti in range(len(groups[gi][0]))]
        T = len(tiles)
        last_of = [max(i for i, x in enumerate(tiles) if (x[0], x[2]) == (gi, a)) for gi, a, n in gunits]
        rows = slice(B_NOPE, B_DK)
        with nc.Block() as block:
            @block.sync
            def _(sp):
                sp.dma_start(w_key[:], d["w_key"]).then_inc(w_in, 16)
                for dst, src in ((cos, "cos_b"), (sin, "sin_b"), (swap, "swap_b")):
                    sp.dma_start(dst[:], d[src]).then_inc(tabs_in, 16)
                for t in range(4):
                    ring.load(sp, t, d["w_low"][:, t])
                sp.wait_ge(key_roped, C)
                for h in range(B_HEADS):
                    sp.dma_start(sc.k_b[h][rows, :], key[rows, :]).then_inc(key_stored, 16)
                for j in range(KTILES):
                    sp.wait_ge(v_out, j + 1)
                    sp.dma_start(sc.v_a[:, j, :], vt[:, j % 2, :]).then_inc(v_stored[j % 2], 16)
                sp.wait_ge(key_stored, 16 * B_HEADS)
                for s in range(2):
                    sp.wait_ge(v_stored[s], 16 * (KTILES // 2))

            @block.tensor
            def _(pe):
                pe.wait_ge(key_w_split, 1)
                for c, (a, n) in enumerate(CHUNKS):
                    for k in range(KT):
                        for i, (x, y) in enumerate(((w_key_high, g.high), (w_key_high, g.low), (w_key_low, g.high))):
                            mm = pe.matmul(g.ps[0:B_ROPE, c, 0:n], x[:, k, :], y[:, k, a:a + n], start=(k == 0 and i == 0), stop=(k == KT - 1 and i == 2))
                    mm.then_inc(key_raw, 1)
                def mean(v):
                    gi, a, n = gunits[v]
                    pe.wait_ge(squared, last_of[v] + 1)
                    if v >= 2:
                        pe.wait_ge(logged, v - 1)
                    first = last_of[v] + 1 - len(groups[gi][0])
                    for i in range(first, last_of[v] + 1):
                        mm = pe.matmul(g.ps[:, 6 + v % 2, 0:n], g.ones[:], sq[:, i % 3, 0:n], start=(i == first), stop=(i == last_of[v]))
                    mm.then_inc(meaned, 1)
                due = 0
                for i, (gi, ti, a, n) in enumerate(tiles):
                    if i >= 3:
                        pe.wait_ge(squared, i - 2)
                    piece = groups[gi][0][ti]
                    pe.wait_ge(ring.split, piece + 1)
                    ring.product_of(pe, g.ps[:, 3 + i % 3, 0:n], piece, g.high, g.low, a, n).then_inc(product, 1)
                    if due < len(gunits) and last_of[due] < i:
                        mean(due)
                        due += 1
                while due < len(gunits):
                    mean(due)
                    due += 1
                pe.wait_ge(ring.split, 4)
                for c, (a, n) in enumerate(CHUNKS):
                    pe.wait_ge(squared, T + c - 2)
                    ring.product_of(pe, g.ps[:, 3 + (T + c) % 3, 0:n], 3, g.high, g.low, a, n).then_inc(product, 1)
                pe.wait_ge(tabs_in, 48)
                for c, (a, n) in enumerate(CHUNKS):
                    pe.wait_ge(key_read, c + 1)
                    pe.matmul(g.ps[rows, c, 0:n], swap[rows, rows], key[rows, a:a + n], start=True, stop=True).then_inc(key_rotated, 1)
                for j in range(KTILES):
                    if j < 3:
                        pe.wait_ge(v_row, C)
                    else:
                        pe.wait_ge(v_out, j - 2)
                    pe.transpose(g.ps[:, 3 + j % 3, 0:P], v_rows[:, j * P:(j + 1) * P], g.ident[:]).then_inc(v_product, 1)

            @block.scalar
            def _(act):
                act.preload_act_table_set("natural_log_exp_and_others")
                act.wait_ge(w_in, 16)
                act.activation(w_key_high[:], w_key[:], ACT.Copy).then_inc(key_w_rounded, 1)
                ring.round_piece(act, 0)
                ring.round_piece(act, 1)
                for c, (a, n) in enumerate(CHUNKS):
                    act.wait_ge(key_raw, c + 1)
                    act.activation(key[rows, a:a + n], g.ps[0:B_ROPE, c, 0:n], ACT.Copy).then_inc(key_read, 1)
                due = 0
                def root(v):
                    gi, a, n = gunits[v]
                    act.wait_ge(meaned, v + 1)
                    if v >= 2:
                        act.wait_ge(normed, last_of[v - 2] + 1)
                    act.activation(rs[:, v % 2, 0:n], g.ps[:, 6 + v % 2, 0:n], ACT.Ln, bias=g.eps[:], scale=1.0 / groups[gi][3]).then_inc(logged, 1)
                    act.wait_ge(logged, v + 1)
                    act.activation(rs[:, v % 2, 0:n], rs[:, v % 2, 0:n], ACT.Exp, scale=-0.5).then_inc(rstd, 1)
                for i, (gi, ti, a, n) in enumerate(tiles):
                    if i in (2 * C - 1, 2 * C):
                        ring.round_piece(act, 2 + i - (2 * C - 1))
                    act.wait_ge(product, i + 1)
                    if i >= 3:
                        act.wait_ge(normed, i - 2)
                        act.wait_ge(meaned, gunits.index((tiles[i - 3][0],) + tiles[i - 3][2:]) + 1)
                    act.activation(raw[:, i % 3, 0:n], g.ps[:, 3 + i % 3, 0:n], ACT.Copy).then_inc(key_read, 1)
                    act.activation(sq[:, i % 3, 0:n], g.ps[:, 3 + i % 3, 0:n], ACT.Square).then_inc(squared, 1)
                    if last_of[due] < i:
                        root(due)
                        due += 1
                while due < len(gunits):
                    root(due)
                    due += 1
                for c, (a, n) in enumerate(CHUNKS):
                    act.wait_ge(product, T + c + 1)
                    act.activation(v_rows[:, a:a + n], g.ps[:, 3 + (T + c) % 3, 0:n], ACT.Copy).then_inc(v_row, 1)
                for j in range(KTILES):
                    act.wait_ge(v_product, j + 1)
                    if j >= 2:
                        act.wait_ge(v_stored[j % 2], 16 * (j // 2))
                    act.activation(vt[:, j % 2, :], g.ps[:, 3 + j % 3, 0:P], ACT.Copy).then_inc(v_out, 1)

            @block.vector
            def _(dve):
                dve.wait_ge(key_w_rounded, 1)
                dve.tensor_tensor(w_key_low[:], w_key[:], w_key_high[:], ALU.subtract).then_inc(key_w_split, 1)
                ring.split_piece(dve, 0)
                ring.split_piece(dve, 1)
                for v, (gi, a, n) in enumerate(gunits):
                    if v in (2, 3):
                        ring.split_piece(dve, v)
                    dve.wait_ge(rstd, v + 1)
                    size = len(groups[gi][0])
                    for ti in range(size):
                        i = last_of[v] + 1 - size + ti
                        name, at = groups[gi][2]
                        dve.wait_ge(key_read, C + i + 1)
                        dve.scalar_tensor_tensor(out=groups[gi][1][ti][:, a:a + n], in0=raw[:, i % 3, 0:n], scalar=vec(g, name, at + ti),
                                                 in1=rs[:, v % 2, 0:n], op0=ALU.mult, op1=ALU.mult).then_inc(normed, 1)
                dve.wait_ge(tabs_in, 48)
                for c, (a, n) in enumerate(CHUNKS):
                    dve.wait_ge(key_rotated, c + 1)
                    dve.tensor_tensor(kt1[rows, a:a + n], key[rows, a:a + n], cos[rows, a:a + n], ALU.mult).then_inc(key_halves, 1)
                    dve.tensor_tensor(kt2[rows, a:a + n], g.ps[rows, c, 0:n], sin[rows, a:a + n], ALU.mult).then_inc(key_halves, 1)
                    dve.wait_ge(key_halves, 2 * (c + 1))
                    dve.tensor_tensor(key[rows, a:a + n], kt1[rows, a:a + n], kt2[rows, a:a + n], ALU.add).then_inc(key_roped, 1)

    names = "w_in tabs_in product raw_out rotated halves roped q_stored0 q_stored1 k_product k_out k_stored0 k_stored1 v_product v_out v_stored0 v_stored1"
    units = [(h, c, a, n) for h in range(B_HEADS) for c, (a, n) in enumerate(CHUNKS)]
    U = len(units)
    with stage(nc, names) as (mem, sems):
        (w_in, tabs_in, product, raw_out, rotated, halves, roped, q_stored0, q_stored1, k_product, k_out,
         k_stored0, k_stored1, v_product, v_out, v_stored0, v_stored1) = sems
        q_stored, k_stored, v_stored = (q_stored0, q_stored1), (k_stored0, k_stored1), (v_stored0, v_stored1)
        wq = tile(nc, mem, "w_q_up", [P, 2, B_HEADS * B_DK])
        wk = tile(nc, mem, "w_k_up", [P, B_HEADS * B_NOPE])
        wv = tile(nc, mem, "w_v_up", [P, B_HEADS * B_V])
        cos, sin = tile(nc, mem, "cos_b", [P, TOK]), tile(nc, mem, "sin_b", [P, TOK])
        swap = tile(nc, mem, "swap_b", [P, P])
        raw, t1, t2, res, kres, vres = (tile(nc, mem, f"u_{x}", [P, 2, BANK]) for x in ("raw", "t1", "t2", "res", "k", "v"))
        top = slice(0, B_DK)
        nope = slice(0, B_NOPE)
        with nc.Block() as block:
            @block.sync
            def _(sp):
                for dst, src in ((wv, "w_v_up"), (wk, "w_k_up"), (wq, "w_q_up")):
                    sp.dma_start(dst[:], d[src]).then_inc(w_in, 16)
                for dst, src in ((swap, "swap_b"), (cos, "cos_b"), (sin, "sin_b")):
                    sp.dma_start(dst[:], d[src]).then_inc(tabs_in, 16)
                for j in range(KTILES):
                    sp.wait_ge(v_out, j + 1)
                    sp.dma_start(sc.v_b[:, j, :], vres[:, j % 2, :]).then_inc(v_stored[j % 2], 16)
                for u, (h, c, a, n) in enumerate(units):
                    sp.wait_ge(k_out, u + 1)
                    sp.dma_start(sc.k_b[h][nope, a:a + n], kres[nope, u % 2, 0:n]).then_inc(k_stored[u % 2], 16)
                    sp.wait_ge(roped, u + 1)
                    sp.dma_start(sc.q_b[h][:, a:a + n], res[top, u % 2, 0:n]).then_inc(q_stored[u % 2], 16)
                for s in range(2):
                    sp.wait_ge(v_stored[s], 16 * (KTILES // 2))
                    sp.wait_ge(k_stored[s], 16 * (U // 2))
                    sp.wait_ge(q_stored[s], 16 * (U // 2))

            @block.tensor
            def _(pe):
                pe.wait_ge(w_in, 48)
                for j in range(KTILES):
                    if j >= 2:
                        pe.wait_ge(v_out, j - 1)
                    pe.matmul(g.ps[:, 6 + j % 2, :], kv_low[:, j * P:(j + 1) * P], wv[:], start=True, stop=True).then_inc(v_product, 1)
                for step in range(U + 1):
                    if step < U:
                        h, c, a, n = units[step]
                        if step >= 2:
                            pe.wait_ge(raw_out, step - 1)
                        for k in range(2):
                            mm = pe.matmul(g.ps[top, step % 2, 0:n], wq[:, k, h * B_DK:(h + 1) * B_DK], q_low[:, k, a:a + n], start=(k == 0), stop=(k == 1))
                        mm.then_inc(product, 1)
                        if step >= 2:
                            pe.wait_ge(k_out, step - 1)
                        pe.matmul(g.ps[nope, 4 + step % 2, 0:n], wk[:, h * B_NOPE:(h + 1) * B_NOPE], kv_low[:, a:a + n], start=True, stop=True).then_inc(k_product, 1)
                    if step == 1:
                        pe.wait_ge(tabs_in, 48)
                    if step >= 1:
                        v = step - 1
                        n = units[v][3]
                        pe.wait_ge(raw_out, v + 1)
                        if v >= 2:
                            pe.wait_ge(halves, 2 * (v - 1))
                        pe.matmul(g.ps[top, 2 + v % 2, 0:n], swap[top, top], raw[top, v % 2, 0:n], start=True, stop=True).then_inc(rotated, 1)

            @block.scalar
            def _(act):
                for j in range(KTILES):
                    act.wait_ge(v_product, j + 1)
                    if j >= 2:
                        act.wait_ge(v_stored[j % 2], 16 * (j // 2))
                    act.activation(vres[:, j % 2, :], g.ps[:, 6 + j % 2, :], ACT.Copy).then_inc(v_out, 1)
                for u, (h, c, a, n) in enumerate(units):
                    act.wait_ge(product, u + 1)
                    if u >= 2:
                        act.wait_ge(halves, 2 * (u - 1))
                        act.wait_ge(rotated, u - 1)
                    act.activation(raw[top, u % 2, 0:n], g.ps[top, u % 2, 0:n], ACT.Copy, scale=B_SCALE).then_inc(raw_out, 1)
                    act.wait_ge(k_product, u + 1)
                    if u >= 2:
                        act.wait_ge(k_stored[u % 2], 16 * (u // 2))
                    act.activation(kres[nope, u % 2, 0:n], g.ps[nope, 4 + u % 2, 0:n], ACT.Copy).then_inc(k_out, 1)

            @block.vector
            def _(dve):
                dve.wait_ge(tabs_in, 48)
                for v, (h, c, a, n) in enumerate(units):
                    dve.wait_ge(raw_out, v + 1)
                    dve.wait_ge(rotated, v + 1)
                    if v >= 2:
                        dve.wait_ge(roped, v - 1)
                        dve.wait_ge(q_stored[v % 2], 16 * (v // 2))
                    dve.tensor_tensor(t1[top, v % 2, 0:n], raw[top, v % 2, 0:n], cos[top, a:a + n], ALU.mult).then_inc(halves, 1)
                    dve.tensor_tensor(t2[top, v % 2, 0:n], g.ps[top, 2 + v % 2, 0:n], sin[top, a:a + n], ALU.mult).then_inc(halves, 1)
                    dve.wait_ge(halves, 2 * (v + 1))
                    dve.tensor_tensor(res[top, v % 2, 0:n], t1[top, v % 2, 0:n], t2[top, v % 2, 0:n], ALU.add).then_inc(roped, 1)


def attention(nc, g, sc, out):
    PAIRS = 4
    QB = 256
    steps = [(b, h, t) for b in range(TOK // QB) for h in range(2) for t in range(2)]
    S, B = len(steps), TOK // QB
    PER_BLOCK = S // B
    ALL = [(pair, i) for pair in range(PAIRS) for i in range(S)]
    N = len(ALL)

    def keys_of(b):
        return (0, KTILES) if b < LAT // QB else (LAT // P, KTILES)

    def block_of(x):
        return steps[ALL[x][1]][0]

    def width(x):
        lo, hi = keys_of(block_of(x))
        return (hi - lo) * P

    def turns(x):
        lo, hi = keys_of(block_of(x))
        return [(i, min(i + 4, hi)) for i in range(lo, hi, 4)]

    use = {}
    for x in range(2, N + 3):
        if x > 2 and (x - 2) % PER_BLOCK == 0:
            use["mix", (x - 3) // PER_BLOCK] = len(use)
        if x - 2 < N:
            for j in range(len(turns(x - 2))):
                use["turn", x - 2, j] = len(use)

    def last_turn(x):
        return use["turn", x, len(turns(x)) - 1]

    for kind in range(2):
        rows = slice(0, (P, B_DK)[kind])
        items = (((0, 0), (0, 1), (1, 0)), ((0, 0), (0, 1), (1, 0), (1, 1)))[kind]
        I = len(items)
        COPIES = (2, 1)[kind]
        names = "raw_in0 raw_in1 v_in0 v_in1 rounded split scores maxed exped inverse probs filled emptied"
        with stage(nc, names) as (mem, sems):
            raw_in, v_in, (rounded, split, scores, maxed, exped, inverse, probs, filled, emptied) = sems[:2], sems[2:4], sems[4:]
            raw = tile(nc, mem, "qk_raw", [P, 2, TOK])
            heads = len(items) - 2
            q_hi, k_hi, k_lo = (tile_r(nc, mem, f"{x}", [P, 2, n, TOK]) for x, n in (("q_high", 2), ("k_high", heads), ("k_low", heads)))
            q_lo = q_hi if kind == 0 else tile_r(nc, mem, "q_low_part", [P, 2, 2, TOK])
            v = tile(nc, mem, "v_pair", [P, 2, KTILES, 2, B_V])
            p = tile(nc, mem, "probs", [P, 3, TOK])
            pt = tile(nc, mem, "probs_turned", [P, 2, 2, KTILES, QB])
            neg_max, total, inv = (tile(nc, mem, f"row_{x}", [P, 4]) for x in ("max", "sum", "inv"))

            def source(pair, item):
                which, h = item
                if kind == 0:
                    return sc.qk_a[1 + pair][64 * h:64 * h + 64, :] if which == 0 else sc.qk_a[0][64 * (pair // 2):64 * (pair // 2) + 64, :]
                return (sc.q_b, sc.k_b)[which][2 * pair + h]

            def split_at(x):
                pair, i = ALL[x]
                n, off = divmod(i - 5, 3)
                return (pair + 1, n) if off == 0 and 0 <= n < I and pair + 1 < PAIRS else None

            with nc.Block() as block:
                @block.sync
                def _(sp):
                    for pair in range(PAIRS):
                        for n in range(I):
                            m = pair * I + n
                            if m >= 2:
                                sp.wait_ge(split, m - 1)
                            for c in range(COPIES):
                                at = rows if kind == 1 else slice(64 * c, 64 * c + 64)
                                sp.dma_start(raw[at, m % 2, :], source(pair, items[n])).then_inc(raw_in[m % 2], 16)
                        if pair >= 2:
                            sp.wait_ge(filled, use["mix", (pair - 1) * B - 1] + 1)
                        s = pair % 2
                        if kind == 0:
                            for h in range(2):
                                sp.dma_start(v[:, s, :, h, :], sc.v_a[:, :, 64 * (pair // 2):64 * (pair // 2) + 64]).then_inc(v_in[s], 16)
                        else:
                            sp.dma_start(v[:, s], sc.v_b[:, :, 128 * pair:128 * pair + 128].rearrange("p j (h n) -> p j h n", h=2)).then_inc(v_in[s], 16)

                @block.tensor
                def _(pe):
                    def scores_of(x):
                        pair, i = ALL[x]
                        b, h, t = steps[i]
                        s, q0 = pair % 2, b * QB + t * P
                        qs = slice(q0, q0 + P)
                        lo, hi = keys_of(b)
                        parts = [(a, min(BANK, hi * P - a)) for a in range(lo * P, hi * P, BANK)]
                        if i == 0:
                            pe.wait_ge(split, I * (pair + 1))
                        if x >= 2:
                            pe.wait_ge(exped, x - 1)
                        kh = 0 if kind == 0 else h
                        passes = [(q_hi, k_hi), (q_hi, k_lo)] + ([(q_lo, k_hi)] if kind else [])
                        for j, (a, n) in enumerate(parts):
                            for m, (left, right) in enumerate(passes):
                                mm = pe.matmul(g.ps[:, 3 * (x % 2) + j, 0:n], left[rows, s, h, qs], right[rows, s, kh, a:a + n],
                                               start=(m == 0), stop=(m == len(passes) - 1))
                            if j == len(parts) - 1:
                                mm.then_inc(scores, 1)

                    def turn(x):
                        first = keys_of(block_of(x))[0]
                        for j, (lo, hi) in enumerate(turns(x)):
                            if j == 0:
                                pe.wait_ge(probs, x + 1)
                            r = use["turn", x, j]
                            if r >= 2:
                                pe.wait_ge(emptied, r - 1)
                            for kt in range(lo, hi):
                                mm = pe.transpose(g.ps[:, 6 + r % 2, (kt - lo) * P:(kt - lo + 1) * P], p[:, x % 3, (kt - first) * P:(kt - first + 1) * P], g.ident[:])
                            mm.then_inc(filled, 1)

                    def mix(y):
                        pair, b = divmod(y, B)
                        lo, hi = keys_of(b)
                        r = use["mix", y]
                        pe.wait_ge(emptied, r)
                        pe.wait_ge(v_in[pair % 2], 16 * COPIES * (pair // 2 + 1))
                        for kt in range(lo, hi):
                            for h in range(2):
                                mm = pe.matmul(g.ps[64 * h:64 * h + 64, 6 + r % 2, 0:QB], v[:, pair % 2, kt, h, :], pt[:, y % 2, h, kt, :],
                                               start=(kt == lo), stop=(kt == hi - 1))
                        mm.then_inc(filled, 1)

                    for x in range(N + 3):
                        if x < N:
                            scores_of(x)
                        if x > 2 and (x - 2) % PER_BLOCK == 0:
                            mix((x - 3) // PER_BLOCK)
                        if 2 <= x < N + 2:
                            turn(x - 2)

                @block.vector
                def _(dve):
                    def split_item(pair, n):
                        which, h = items[n]
                        m, s = pair * I + n, pair % 2
                        dve.wait_ge(rounded, m + 1)
                        if which == 1:
                            low, high, at = k_lo, k_hi, rows
                        else:
                            low, high, at = q_lo, q_hi, (slice(64, P) if kind == 0 else rows)
                        dve.tensor_tensor(low[at, s, h, :], raw[at, m % 2, :], high[at, s, h, :], ALU.subtract).then_inc(split, 1)

                    for n in range(I):
                        split_item(0, n)
                    for x in range(N + 1):
                        if x < N:
                            dve.wait_ge(scores, x + 1)
                            if x >= 4:
                                dve.wait_ge(exped, x - 3)
                            flat = g.ps[:, 3 * (x % 2):3 * (x % 2) + 3, :].rearrange("p b n -> p (b n)")[:, 0:width(x)]
                            dve.tensor_reduce(neg_max[:, x % 4:x % 4 + 1], flat, AX.X, ALU.max, negate=True).then_inc(maxed, 1)
                        if x >= 1:
                            y = x - 1
                            dve.wait_ge(exped, y + 1)
                            if y >= 4:
                                dve.wait_ge(probs, y - 3)
                            dve.reciprocal(inv[:, y % 4:y % 4 + 1], total[:, y % 4:y % 4 + 1]).then_inc(inverse, 1)
                            dve.wait_ge(inverse, y + 1)
                            dve.tensor_scalar(p[:, y % 3, 0:width(y)], p[:, y % 3, 0:width(y)], inv[:, y % 4:y % 4 + 1], None, ALU.mult).then_inc(probs, 1)
                        if x < N and split_at(x):
                            split_item(*split_at(x))

                @block.scalar
                def _(act):
                    def round_item(pair, n):
                        which, h = items[n]
                        m, s = pair * I + n, pair % 2
                        act.wait_ge(raw_in[m % 2], 16 * COPIES * (m // 2 + 1))
                        if pair >= 2:
                            act.wait_ge(scores, (pair - 1) * S)
                        act.activation((q_hi, k_hi)[which][rows, s, h, :], raw[rows, m % 2, :], ACT.Copy).then_inc(rounded, 1)

                    def turn_out(x, j):
                        pair, i = ALL[x]
                        b, h, t = steps[i]
                        lo, hi = turns(x)[j]
                        y = pair * B + b
                        r = use["turn", x, j]
                        act.wait_ge(filled, r + 1)
                        act.activation(pt[:, y % 2, h, lo:hi, t * P:(t + 1) * P],
                                       g.ps[:, 6 + r % 2, 0:(hi - lo) * P].rearrange("p (k n) -> p k n", n=P), ACT.Copy).then_inc(emptied, 1)

                    def mix_out(y):
                        pair, b = divmod(y, B)
                        r = use["mix", y]
                        act.wait_ge(filled, r + 1)
                        act.activation(out[:, kind * PAIRS + pair, b * QB:(b + 1) * QB], g.ps[:, 6 + r % 2, 0:QB], ACT.Copy).then_inc(emptied, 1)

                    for n in range(I):
                        round_item(0, n)
                    for x in range(N + 3):
                        if x > 2 and (x - 2) % PER_BLOCK == 0:
                            mix_out((x - 3) // PER_BLOCK)
                        if 2 <= x < N + 2:
                            for j in range(len(turns(x - 2))):
                                turn_out(x - 2, j)
                        if x < N:
                            act.wait_ge(maxed, x + 1)
                            if x >= 3:
                                act.wait_ge(filled, last_turn(x - 3) + 1)
                            if x >= 4:
                                act.wait_ge(inverse, x - 3)
                            flat = g.ps[:, 3 * (x % 2):3 * (x % 2) + 3, :].rearrange("p b n -> p (b n)")[:, 0:width(x)]
                            act.activation(p[:, x % 3, 0:width(x)], flat, ACT.Exp, bias=neg_max[:, x % 4:x % 4 + 1], accum_out=total[:, x % 4:x % 4 + 1]).then_inc(exped, 1)
                            if split_at(x):
                                round_item(*split_at(x))


def project_out(nc, g, src, w, out, tokens):
    PIECES, BANKS = KT, 4
    spans = chunks_of(tokens)
    C = len(spans)
    units = [(t, a, n) for t in range(PIECES) for a, n in spans]
    U = len(units)
    total = g.ps[:, SQUARES_AT:SQUARES_AT + 3, :].rearrange("p b n -> p (b n)")
    high, low = g.high, g.low
    with stage(nc, "raw_in0 raw_in1 w_rounded w_split src_rounded src_split product copied squared square_used") as (mem, sems):
        w_sems, (src_rounded, src_split, product, copied, squared, square_used) = sems[:4], sems[4:]
        ring = WeightRing(nc, mem, w_sems, product, [C * (t + 1) for t in range(PIECES)])
        sq = tile(nc, mem, "out_square", [P, 2, BANK])
        with nc.Block() as block:
            @block.sync
            def _(sp):
                for t in range(PIECES):
                    ring.load(sp, t, w[t])

            @block.tensor
            def _(pe):
                def add_squares(u):
                    t, a, n = units[u]
                    pe.wait_ge(squared, u + 1)
                    pe.matmul(total[:, a:a + n], g.ones[:], sq[:, u % 2, 0:n], start=(t == 0), stop=(t == PIECES - 1)).then_inc(square_used, 1)

                pe.wait_ge(ring.split, 1)
                for k in range(KT):
                    pe.wait_ge(src_split, k + 1)
                    for c, (a, n) in enumerate(spans):
                        for i, (x, y) in enumerate(((ring.high, high), (ring.high, low), (ring.low, high))):
                            mm = pe.matmul(g.ps[:, c, 0:n], x[:, 0, k, :], y[:, k, a:a + n], start=(k == 0 and i == 0), stop=(k == KT - 1 and i == 2))
                        if k == KT - 1:
                            mm.then_inc(product, 1)
                for u in range(C, U):
                    t, a, n = units[u]
                    if u % C == 0:
                        pe.wait_ge(ring.split, t + 1)
                    if u >= BANKS:
                        pe.wait_ge(squared, u - BANKS + 1)
                    ring.product_of(pe, g.ps[:, u % BANKS, 0:n], t, high, low, a, n).then_inc(product, 1)
                    if u == C:
                        for v in range(C):
                            add_squares(v)
                    else:
                        add_squares(u - 1)
                add_squares(U - 1)

            @block.scalar
            def _(act):
                ring.round_piece(act, 0)
                for k in range(KT):
                    act.activation(high[:, k, 0:tokens], src[:, k, 0:tokens], ACT.Copy).then_inc(src_rounded, 1)
                for u, (t, a, n) in enumerate(units):
                    if u % C == 0:
                        ring.round_piece(act, t + 1)
                    act.wait_ge(product, u + 1)
                    act.activation(out[:, t, a:a + n], g.ps[:, u % BANKS, 0:n], ACT.Copy).then_inc(copied, 1)
                    if u >= 2:
                        act.wait_ge(square_used, u - 1)
                    act.activation(sq[:, u % 2, 0:n], g.ps[:, u % BANKS, 0:n], ACT.Square).then_inc(squared, 1)

            @block.vector
            def _(dve):
                ring.split_piece(dve, 0)
                for k in range(KT):
                    dve.wait_ge(src_rounded, k + 1)
                    dve.tensor_tensor(low[:, k, 0:tokens], src[:, k, 0:tokens], high[:, k, 0:tokens], ALU.subtract).then_inc(src_split, 1)
                for t in range(1, PIECES):
                    ring.split_piece(dve, t)


def project_mamba(nc, g, d, high, low, xbc, gate, dt, adt):
    TILES, Z_TILES, BANKS = 8, 4, 4
    units = [(t, a, n) for t in range(TILES) for a, n in CHUNKS]
    zunits = [(t, a, n) for t in range(Z_TILES) for a, n in CHUNKS[:2]]
    U, C = len(units), len(CHUNKS)
    WIDE = LAT + CTX + 4
    LAT_AT, CTX_AT = 1, LAT + 3
    names = ("raw_in0 raw_in1 w_rounded w_split w_dt dt_rounded dt_split dt_rows dt_copied product dt_product raw_out z_out padded conv conv_read dt_out steps "
             "magnitude decayed logged a_exp tapped")
    with stage(nc, names) as (mem, sems):
        w_sems, (w_dt, dt_rounded, dt_split, dt_rows, dt_copied, product, dt_product, raw_out, z_out, padded, conv, conv_read, dt_out, steps,
               magnitude, decayed, logged, a_exp, tapped) = sems[:4], sems[4:]
        ring = WeightRing(nc, mem, w_sems, product, [C * (t + 1) for t in range(TILES)] + [U + 2 * (t + 1) for t in range(Z_TILES)])
        wdt, wdt_high, wdt_low = tile(nc, mem, "w_dt", [P, KT, 16]), tile_r(nc, mem, "w_dt_high", [P, KT, 16]), tile_r(nc, mem, "w_dt_low", [P, KT, 16])
        dt_row = gate[0:16, 0:2, :].rearrange("p t n -> p (t n)")[:, 0:TOK]
        raw = tile(nc, mem, "xbc_raw", [P, 2, WIDE])
        acc = tile(nc, mem, "conv_acc", [P, 2, WIDE])
        T16 = [P, KTILES, 16]
        mag, ex, one_e, lg, zero, den = (tile(nc, mem, f"dt_{x}", T16) for x in ("mag", "exp", "one", "log", "zero", "den"))
        rate = tile(nc, mem, "a_rate", [P, 16])
        over_tiles = lambda ap: ap.unsqueeze(1).to_broadcast(T16)
        with nc.Block() as block:
            def silu_conv(act, t):
                act.wait_ge(conv, t + 1)
                act.activation(xbc[:, t, 0:LAT], acc[:, t % 2, LAT_AT:LAT_AT + LAT], ACT.Silu, bias=vec(g, "conv_b", t)).then_inc(conv_read, 1)
                act.activation(xbc[:, t, LAT:TOK], acc[:, t % 2, CTX_AT:CTX_AT + CTX], ACT.Silu, bias=vec(g, "conv_b", t)).then_inc(conv_read, 1)

            @block.sync
            def _(sp):
                sp.dma_start(wdt[:], d["w_dt"]).then_inc(w_dt, 16)
                for t in range(TILES + Z_TILES):
                    ring.load(sp, t, d["w_xbc"][t] if t < TILES else d["w_z"][t - TILES])

            @block.tensor
            def _(pe):
                pe.wait_ge(dt_split, 1)
                for c, (a, n) in enumerate(CHUNKS):
                    for k in range(KT):
                        for i, (x, y) in enumerate(((wdt_high, high), (wdt_high, low), (wdt_low, high))):
                            mm = pe.matmul(g.ps[0:16, 4 + c, 0:n], x[:, k, :], y[:, k, a:a + n], start=(k == 0 and i == 0), stop=(k == KT - 1 and i == 2))
                    mm.then_inc(dt_rows, 1)
                for u, (t, a, n) in enumerate(units):
                    if u % C == 0:
                        pe.wait_ge(ring.split, t + 1)
                    if u >= BANKS:
                        pe.wait_ge(raw_out, u - BANKS + 1)
                    ring.product_of(pe, g.ps[:, u % BANKS, 0:n], t, high, low, a, n).then_inc(product, 1)
                    if u == C - 1:
                        pe.wait_ge(dt_copied, C)
                        for j in range(KTILES):
                            mm = pe.transpose(g.ps[:, 7, j * 16:(j + 1) * 16], dt_row[:, j * P:(j + 1) * P], g.ident[0:16, 0:16])
                        mm.then_inc(dt_product, 1)
                for u, (t, a, n) in enumerate(zunits):
                    if u % 2 == 0:
                        pe.wait_ge(ring.split, TILES + t + 1)
                    if u >= 2:
                        pe.wait_ge(z_out, u - 1)
                    ring.product_of(pe, g.ps[:, 4 + u % 2, 0:n], TILES + t, high, low, a, n).then_inc(product, 1)

            @block.scalar
            def _(act):
                act.preload_act_table_set("natural_log_exp_and_others")
                act.wait_ge(w_dt, 16)
                act.activation(wdt_high[:], wdt[:], ACT.Copy).then_inc(dt_rounded, 1)
                ring.round_piece(act, 0)
                for c, (a, n) in enumerate(CHUNKS):
                    act.wait_ge(dt_rows, c + 1)
                    act.activation(dt_row[:, a:a + n], g.ps[0:16, 4 + c, 0:n], ACT.Copy).then_inc(dt_copied, 1)
                act.wait_ge(padded, 1)
                for u, (t, a, n) in enumerate(units):
                    if u % C == 0:
                        ring.round_piece(act, t + 1)
                    act.wait_ge(product, u + 1)
                    if t >= 2 and u % C == 0:
                        act.wait_ge(conv, t - 1)
                    at = LAT_AT + a if a < LAT else CTX_AT + a - LAT
                    act.activation(raw[:, t % 2, at:at + n], g.ps[:, u % BANKS, 0:n], ACT.Copy).then_inc(raw_out, 1)
                    if u % C == C - 1 and t >= 1:
                        silu_conv(act, t - 1)
                    if u == 2 * C - 1:
                        act.wait_ge(steps, 1)
                        act.activation(mag[:], dt[:], ACT.Abs).then_inc(magnitude, 1)
                        act.wait_ge(magnitude, 1)
                        act.activation(ex[:], mag[:], ACT.Exp, scale=-1.0).then_inc(decayed, 1)
                        act.activation(rate[:], vec(g, "a_log", 0, 16), ACT.Exp).then_inc(a_exp, 1)
                    if u == 3 * C - 1:
                        act.wait_ge(steps, 2)
                        act.activation(lg[:], one_e[:], ACT.Ln).then_inc(logged, 1)
                silu_conv(act, TILES - 1)
                for u, (t, a, n) in enumerate(zunits):
                    if u % 2 == 0:
                        ring.round_piece(act, TILES + t + 1)
                    act.wait_ge(product, U + u + 1)
                    act.activation(gate[:, t, a:a + n], g.ps[:, 4 + u % 2, 0:n], ACT.Silu).then_inc(z_out, 1)

            @block.vector
            def _(dve):
                dve.wait_ge(dt_rounded, 1)
                dve.tensor_tensor(wdt_low[:], wdt[:], wdt_high[:], ALU.subtract).then_inc(dt_split, 1)
                ring.split_piece(dve, 0)
                dve.memset(raw[:], 0.0).then_inc(padded, 1)
                for t in range(TILES):
                    ring.split_piece(dve, t + 1)
                    if t == 1:
                        dve.wait_ge(dt_product, 1)
                        dps = g.ps[:, 7, 0:160].rearrange("p (j c) -> p j c", c=16)
                        dve.tensor_tensor(dt[:], dps, over_tiles(vec(g, "dt_bias", 0, 16)), ALU.add).then_inc(steps, 1)
                    if t == 2:
                        dve.wait_ge(decayed, 1)
                        dve.tensor_scalar(one_e[:], ex[:], 1.0, None, ALU.add).then_inc(steps, 1)
                    if t == 3:
                        dve.wait_ge(steps, 2)
                        dve.tensor_scalar(zero[:], one_e[:], 1.0, None, ALU.is_equal).then_inc(steps, 1)
                        dve.wait_ge(steps, 3)
                        dve.scalar_tensor_tensor(out=den[:], in0=one_e[:], scalar=-1.0, in1=zero[:], op0=ALU.add, op1=ALU.add).then_inc(steps, 1)
                        dve.wait_ge(steps, 4)
                        dve.reciprocal(den[:], den[:]).then_inc(steps, 1)
                        dve.wait_ge(logged, 1)
                        dve.tensor_tensor(lg[:], lg[:], zero[:], ALU.add).then_inc(steps, 1)
                        dve.wait_ge(steps, 6)
                        dve.tensor_tensor(lg[:], lg[:], den[:], ALU.mult).then_inc(steps, 1)
                        dve.wait_ge(steps, 7)
                        dve.tensor_tensor(lg[:], lg[:], ex[:], ALU.mult).then_inc(steps, 1)
                        dve.wait_ge(steps, 8)
                        dve.scalar_tensor_tensor(out=dt[:], in0=dt[:], scalar=0.0, in1=lg[:], op0=ALU.max, op1=ALU.add).then_inc(steps, 1)
                        dve.wait_ge(a_exp, 1)
                        dve.tensor_scalar(rate[:], rate[:], -1.0, None, ALU.mult).then_inc(steps, 1)
                        dve.wait_ge(steps, 10)
                        dve.tensor_tensor(adt[:], dt[:], over_tiles(rate[:]), ALU.mult).then_inc(steps, 1)
                    dve.wait_ge(raw_out, C * (t + 1))
                    if t >= 2:
                        dve.wait_ge(conv_read, 2 * (t - 1))
                    out, n = acc[:, t % 2, 1:WIDE - 1], WIDE - 2
                    tap = lambda i: vec(g, "conv_w", i * TILES + t)
                    dve.tensor_scalar(out, raw[:, t % 2, 0:n], tap(0), None, ALU.mult).then_inc(tapped, 1)
                    dve.wait_ge(tapped, 2 * t + 1)
                    dve.scalar_tensor_tensor(out=out, in0=raw[:, t % 2, 1:1 + n], scalar=tap(1), in1=out, op0=ALU.mult, op1=ALU.add).then_inc(tapped, 1)
                    dve.wait_ge(tapped, 2 * t + 2)
                    dve.scalar_tensor_tensor(out=out, in0=raw[:, t % 2, 2:2 + n], scalar=tap(2), in1=out, op0=ALU.mult, op1=ALU.add).then_inc(conv, 1)
                for t in range(TILES, TILES + Z_TILES):
                    ring.split_piece(dve, t + 1)


def scan_states(nc, g, d, xbc, gate, dt, adt, out):
    CH, H, HD, G = P, 8, 64, 2
    LATC, NC = LAT // CH, TOK // CH
    fwd = list(range(LATC, NC)) + list(range(LATC))
    bwd = list(range(NC - 1, LATC - 1, -1)) + list(range(LATC - 1, -1, -1))
    units = [(dr, c) for pair in zip(fwd, bwd) for dr, c in enumerate(pair)]
    U = len(units)
    ys = [u for u, (dr, c) in enumerate(units) if c < LATC]
    Y = {u: i for i, u in enumerate(ys)}
    first_y = {}
    for u in ys:
        first_y.setdefault(units[u][1], u)

    xt = tile(nc, out.mem, "x_tokens", [P, NC, H * HD])
    bt = tile(nc, out.mem, "b_tokens", [P, NC, G * P])
    tri = tile(nc, out.mem, "triangles", [P, 2, P])
    with stage(nc, "tri_in turned read_out") as (mem, (tri_in, turned, read_out)):
        jobs = [(c, kind) for c in range(NC) for kind in range(2)]
        with nc.Block() as block:
            @block.sync
            def _(sp):
                sp.dma_start(tri[:], d["triangles"]).then_inc(tri_in, 16)
                sp.wait_ge(tri_in, 16)

            @block.tensor
            def _(pe):
                for i, (c, kind) in enumerate(jobs):
                    if i >= 4:
                        pe.wait_ge(read_out, i - 3)
                    for t in range(4 if kind == 0 else 2):
                        mm = pe.transpose(g.ps[:, i % 4, t * P:(t + 1) * P], xbc[:, 4 * kind + t, c * CH:(c + 1) * CH], g.ident[:])
                    mm.then_inc(turned, 1)

            @block.scalar
            def _(act):
                for i, (c, kind) in enumerate(jobs):
                    act.wait_ge(turned, i + 1)
                    dst = xt[:, c, :] if kind == 0 else bt[:, c, :]
                    act.activation(dst, g.ps[:, i % 4, 0:dst.shape[1]], ACT.Copy).then_inc(read_out, 1)

    names = ("spread sums acs_out act_read last_made seg_made decay_done clamped seg_exp decay_dt weighted x_dt c_scaled gram "
             "masked attended state_product kept state y_product y_out cleared")
    with stage(nc, names) as (mem, sems):
        (spread, sums, acs_out, act_read, last_made, seg_made, decay_done, clamped, seg_exp, decay_dt, weighted, x_dt,
         c_scaled, gram, masked, attended, state_product, kept, state, y_product, y_out, cleared) = sems
        HL = [P, H, CH]
        HX = [P, H, HD]
        au = tile(nc, mem, "adt_spread", [P, 2, H, CH])
        acs = tile(nc, mem, "acs_source", [P, 2, H])
        last = tile(nc, mem, "acs_left", [P, 2, H])
        dec = tile(nc, mem, "decay_source", [P, 2, H])
        whole = tile(nc, mem, "decay_chunk", [P, 2, H])
        xw = tile(nc, mem, "x_weighted", [P, 2, H, HD])
        xd = tile(nc, mem, "x_dt", [P, 2, H, HD])
        seg = tile(nc, mem, "segments", [P, 2, H, CH])
        ea = tile(nc, mem, "exp_acs", [P, 2, H, CH])
        gm = tile(nc, mem, "gram_masked", [P, 2, G, CH])
        st = tile(nc, mem, "states", [P, 2, 2, H, HD])
        tmp = tile(nc, mem, "state_kept", [P, H, HD])
        y = out.y
        acs_ps = g.ps[:, 0:2, :].rearrange("p b (h l) -> p (b h) l", l=CH)
        by_head = lambda ap, shape: ap.unsqueeze(2).to_broadcast(shape)
        ny = lambda u: sum(1 for v in ys if v < u)
        with nc.Block() as block:
            def y_read(dve, i):
                c = units[ys[i]][1]
                dve.wait_ge(y_product, i + 1)
                src = g.ps[:, 5 + i % 2, :].rearrange("p (t l) -> p t l", l=CH)
                dst = y[:, :, c * CH:(c + 1) * CH]
                if first_y[c] == ys[i]:
                    dve.tensor_copy(dst, src).then_inc(y_out, 1)
                else:
                    dve.wait_ge(y_out, Y[first_y[c]] + 1)
                    dve.tensor_tensor(dst, dst, src, ALU.add).then_inc(y_out, 1)

            @block.tensor
            def _(pe):
                def running_sums(u):
                    dr, c = units[u]
                    pe.wait_ge(spread, u + 1)
                    if u >= 1:
                        pe.wait_ge(act_read, u)
                        pe.wait_ge(last_made, u)
                        if ny(u):
                            pe.wait_ge(seg_made, ny(u))
                    for b in range(2):
                        pe.matmul(g.ps[:, b, :], g.ones[:], au[:, u % 2, 4 * b:4 * b + 4, :].rearrange("p h l -> p (h l)"), start=True, stop=True)
                    pe.matmul(g.ps[:, 2, 0:H], tri[:, dr, :], adt[:, c, 8 * dr:8 * dr + 8], start=True, stop=True).then_inc(sums, 1)

                running_sums(0)
                for u, (dr, c) in enumerate(units):
                    tok = slice(c * CH, (c + 1) * CH)
                    if u in Y:
                        i = Y[u]
                        if i >= 1:
                            pe.wait_ge(masked, i)
                        for grp in range(G):
                            mm = pe.matmul(g.ps[:, 4, grp * CH:(grp + 1) * CH], xbc[:, 4 + grp, tok], xbc[:, 6 + grp, tok], start=True, stop=True)
                        mm.then_inc(gram, 1)
                    pe.wait_ge(weighted, u + 1)
                    if u >= 1:
                        pe.wait_ge(state, u)
                    for grp in range(G):
                        mm = pe.matmul(g.ps[:, 3, grp * 256:(grp + 1) * 256], bt[:, c, grp * P:(grp + 1) * P],
                                       xw[:, u % 2, 4 * grp:4 * grp + 4, :].rearrange("p h x -> p (h x)"), start=True, stop=True)
                    mm.then_inc(state_product, 1)
                    if u + 1 < U:
                        running_sums(u + 1)
                    if u in Y:
                        i = Y[u]
                        pe.wait_ge(attended, i + 1)
                        pe.wait_ge(c_scaled, i + 1)
                        pe.wait_ge(x_dt, i + 1)
                        if i >= 2:
                            pe.wait_ge(y_out, i - 1)
                        for h in range(H):
                            dst = g.ps[64 * (h % 2):64 * (h % 2) + 64, 5 + i % 2, (h // 2) * CH:(h // 2 + 1) * CH]
                            pe.matmul(dst, xd[:, i % 2, h, :], seg[:, i % 2, h, :], start=True, stop=False)
                            mm = pe.matmul(dst, st[:, dr, (u // 2) % 2, h, :], ea[:, i % 2, h, :], start=False, stop=True)
                        mm.then_inc(y_product, 1)

            @block.scalar
            def _(act):
                for u, (dr, c) in enumerate(units):
                    end = CH - 1 if dr == 0 else 0
                    act.wait_ge(sums, u + 1)
                    if u >= 2:
                        act.wait_ge(last_made, u - 1)
                        if ny(u - 1):
                            act.wait_ge(seg_made, ny(u - 1))
                        act.wait_ge(kept, u - 1)
                    act.activation(acs[:, u % 2, :], g.ps[:, 2, 0:H], ACT.Copy).then_inc(acs_out, 1)
                    done = act.activation(whole[:, u % 2, :], acs_ps[:, :, end], ACT.Exp)
                    if u in Y:
                        i = Y[u]
                        if i >= 2:
                            act.wait_ge(y_product, i - 1)
                        done = act.activation(ea[:, i % 2], acs_ps, ACT.Exp)
                    done.then_inc(act_read, 1)
                    act.wait_ge(last_made, u + 1)
                    if u >= 2:
                        act.wait_ge(weighted, u - 1)
                    act.activation(dec[:, u % 2, :], last[:, u % 2, :], ACT.Exp).then_inc(decay_done, 1)
                    if u in Y:
                        act.wait_ge(clamped, i + 1)
                        act.activation(seg[:, i % 2], seg[:, i % 2], ACT.Exp).then_inc(seg_exp, 1)

            @block.gpsimd
            def _(pool):
                def spread_adt(u):
                    dr, c = units[u]
                    if u >= 2:
                        pool.wait_ge(sums, u - 1)
                    pool.tensor_tensor(au[:, u % 2], tri[:, dr, :].unsqueeze(1).to_broadcast(HL),
                                      by_head(adt[:, c, 8 * dr:8 * dr + 8], HL), ALU.mult).then_inc(spread, 1)

                def x_by_dt(u):
                    dr, c = units[u]
                    i = Y[u]
                    if i >= 2:
                        pool.wait_ge(y_product, i - 1)
                    xh = xt[:, c, :].rearrange("p (h x) -> p h x", x=HD)
                    pool.tensor_tensor(xd[:, i % 2], xh, by_head(dt[:, c, 8 * dr:8 * dr + 8], HX), ALU.mult).then_inc(x_dt, 1)

                spread_adt(0)
                for u, (dr, c) in enumerate(units):
                    if u + 1 < U:
                        spread_adt(u + 1)
                    if u in Y:
                        x_by_dt(u)

            @block.vector
            def _(dve):
                dve.memset(st[:], 0.0).then_inc(cleared, 1)
                dve.wait_ge(cleared, 1)
                for u, (dr, c) in enumerate(units):
                    end = CH - 1 if dr == 0 else 0
                    tok = slice(c * CH, (c + 1) * CH)
                    dve.wait_ge(acs_out, u + 1)
                    dve.wait_ge(act_read, u + 1)
                    if u >= 2:
                        dve.wait_ge(decay_done, u - 1)
                    dve.tensor_tensor(last[:, u % 2, :], acs_ps[:, :, end], acs[:, u % 2, :], ALU.subtract).then_inc(last_made, 1)
                    if u in Y:
                        i = Y[u]
                        if i >= 2:
                            dve.wait_ge(y_product, i - 1)
                        dve.tensor_tensor(seg[:, i % 2], acs_ps, by_head(acs[:, u % 2, :], HL), ALU.subtract).then_inc(seg_made, 1)
                    dve.wait_ge(decay_done, u + 1)
                    dve.tensor_tensor(dec[:, u % 2, :], dec[:, u % 2, :], dt[:, c, 8 * dr:8 * dr + 8], ALU.mult).then_inc(decay_dt, 1)
                    dve.wait_ge(decay_dt, u + 1)
                    if u >= 2:
                        dve.wait_ge(state_product, u - 1)
                    xh = xt[:, c, :].rearrange("p (h x) -> p h x", x=HD)
                    dve.tensor_tensor(xw[:, u % 2], xh, by_head(dec[:, u % 2, :], HX), ALU.mult).then_inc(weighted, 1)
                    if u in Y:
                        dve.wait_ge(seg_made, i + 1)
                        dve.tensor_scalar(seg[:, i % 2], seg[:, i % 2], 0.0, None, ALU.min).then_inc(clamped, 1)
                    if u in Y:
                        dve.wait_ge(act_read, u + 1)
                        grouped = [P, G, H // G, CH]
                        ea4 = ea[:, i % 2].rearrange("p (g e) l -> p g e l", g=G)
                        dve.tensor_tensor(ea4, ea4, by_head(xbc[:, 6:8, tok], grouped), ALU.mult).then_inc(c_scaled, 1)
                        dve.wait_ge(gram, i + 1)
                        g2 = g.ps[:, 4, 0:G * CH].rearrange("p (g l) -> p g l", g=G)
                        dve.tensor_tensor(gm[:, i % 2], g2, tri[:, dr, :].unsqueeze(1).to_broadcast([P, G, CH]), ALU.mult).then_inc(masked, 1)
                        dve.wait_ge(masked, i + 1)
                        dve.wait_ge(seg_exp, i + 1)
                        s4 = seg[:, i % 2].rearrange("p (g e) l -> p g e l", g=G)
                        dve.tensor_tensor(s4, s4, by_head(gm[:, i % 2], grouped), ALU.mult).then_inc(attended, 1)
                    dve.wait_ge(act_read, u + 1)
                    if u >= 2:
                        dve.wait_ge(state, u - 1)
                    old, new = st[:, dr, (u // 2) % 2], st[:, dr, (u // 2 + 1) % 2]
                    dve.tensor_tensor(tmp[:], old, by_head(whole[:, u % 2, :], HX), ALU.mult).then_inc(kept, 1)
                    dve.wait_ge(kept, u + 1)
                    dve.wait_ge(state_product, u + 1)
                    if u - 2 in Y:
                        dve.wait_ge(y_product, Y[u - 2] + 1)
                    dve.tensor_tensor(new, tmp[:], g.ps[:, 3, :].rearrange("p (h x) -> p h x", x=HD), ALU.add).then_inc(state, 1)
                    if u in Y and i >= 1:
                        y_read(dve, i - 1)
                y_read(dve, len(ys) - 1)


def gate_norm(nc, g, xbc, gate, y, out):
    T = 4
    with stage(nc, "skipped gated squared square_used logged rstd normed") as (mem, (skipped, gated, squared, square_used, logged, rstd, normed)):
        sq = tile(nc, mem, "norm_sq", [P, 2, LAT])
        rs = tile(nc, mem, "norm_rs", [P, LAT])
        total = g.ps[:, 0:2, :].rearrange("p b n -> p (b n)")
        with nc.Block() as block:
            @block.vector
            def _(dve):
                for t in range(T):
                    dve.scalar_tensor_tensor(out=y[:, t, :], in0=xbc[:, t, 0:LAT], scalar=vec(g, "d_skip", t), in1=y[:, t, :], op0=ALU.mult, op1=ALU.add).then_inc(skipped, 1)
                    dve.wait_ge(skipped, t + 1)
                    dve.tensor_tensor(y[:, t, :], y[:, t, :], gate[:, t, :], ALU.mult).then_inc(gated, 1)
                dve.wait_ge(rstd, 1)
                for t in range(T):
                    dve.scalar_tensor_tensor(out=out[:, t, 0:LAT], in0=y[:, t, :], scalar=vec(g, "mb_norm", t), in1=rs[:], op0=ALU.mult, op1=ALU.mult).then_inc(normed, 1)

            @block.scalar
            def _(act):
                act.preload_act_table_set("natural_log_exp_and_others")
                for t in range(T):
                    act.wait_ge(gated, t + 1)
                    if t >= 2:
                        act.wait_ge(square_used, t - 1)
                    act.activation(sq[:, t % 2, :], y[:, t, :], ACT.Square).then_inc(squared, 1)
                act.wait_ge(square_used, T)
                act.activation(rs[:], total, ACT.Ln, bias=g.eps[:], scale=1.0 / (T * P)).then_inc(logged, 1)
                act.wait_ge(logged, 1)
                act.activation(rs[:], rs[:], ACT.Exp, scale=-0.5).then_inc(rstd, 1)

            @block.tensor
            def _(pe):
                for t in range(T):
                    pe.wait_ge(squared, t + 1)
                    for a, n in CHUNKS[:2]:
                        mm = pe.matmul(total[:, a:a + n], g.ones[:], sq[:, t % 2, a:a + n], start=(t == 0), stop=(t == T - 1))
                    mm.then_inc(square_used, 1)


FOLD = LAT // 2
FT = FOLD // P
W_HY = 512
PARTS = [("cos_even", "sum", True), ("sin_even", "diff", False), ("cos_odd", "diff", False), ("sin_odd", "sum", True)]
PI2_A, PI2_B = 6.28125, 0.0019350051879882812
PI2_C = 2 * math.pi - PI2_A - PI2_B
ROUND = 1.5 * 2 ** 23
BELOW_PI = 3.1415925


def hyena_spectra(nc, g, d, spectra):
    ORD = 2
    HID = 64
    w3, dec, dec_row, tabs = spectra.w3, spectra.decay, spectra.decay_row, spectra.tabs
    alt_row, alt_col = spectra.alt_row, spectra.alt_col
    with stage(nc, "loaded tables_in product biased reduced sines flipped zeroed") as (mem, (loaded, tables_in, product, biased, reduced, sines, flipped, zeroed)):
        w1, w2 = tile(nc, mem, "hy_w1", [P, HID]), tile(nc, mem, "hy_w2", [P, HID])
        zt = tile(nc, mem, "positions", [P, LAT])
        h1 = tile(nc, mem, "hy_h1", [P, LAT])
        ang, turns = tile(nc, mem, "angles", [P, LAT]), tile(nc, mem, "turns", [P, LAT])
        h2, h2r, h2b = spectra.h2, spectra.h2r, spectra.h2b
        rows = slice(0, HID)
        with nc.Block() as block:
            @block.sync
            def _(sp):
                sp.dma_start(w1[0:33, :], d["hy_w1"]).then_inc(loaded, 16)
                sp.dma_start(w2[rows, :], d["hy_w2"]).then_inc(loaded, 16)
                sp.dma_start(zt[0:33, :], d["positions"]).then_inc(loaded, 16)
                tables = ((w3[0:HID, :], d["hy_w3"]), (dec[:], d["decay"]), (dec_row[:], d["decay_middle"]), (tabs[:], d["dft"]),
                          (alt_row[:], d["alt_row"]), (alt_col[:], d["alt_col"]))
                for dst, src in tables:
                    sp.dma_start(dst, src).then_inc(tables_in, 16)
                sp.wait_ge(tables_in, 16 * len(tables))

            @block.tensor
            def _(pe):
                pe.wait_ge(loaded, 48)
                for layer in range(2):
                    for c in range(2):
                        if layer:
                            pe.wait_ge(sines, 1)
                        w, src, kk = ((w1, zt, 33), (w2, h1, HID))[layer]
                        mm = pe.matmul(g.ps[rows, 2 * layer + c, :], w[0:kk, :], src[0:kk, c * BANK:(c + 1) * BANK], start=True, stop=True)
                    mm.then_inc(product, 1)

            @block.vector
            def _(dve):
                dve.memset(h2[rows, LAT:LAT + 1], 0.0).then_inc(zeroed, 1)
                n = 0
                for layer in range(2):
                    dve.wait_ge(product, layer + 1)
                    flat = g.ps[rows, 2 * layer:2 * layer + 2, :].rearrange("p b n -> p (b n)")
                    a, k = ang[rows, :], turns[rows, :]
                    b = vec(g, ("hy_b1", "hy_b2")[layer])[rows, :]
                    dve.tensor_scalar(a, flat, b, vec(g, "freq")[rows, :], ALU.add, ALU.mult).then_inc(biased, 1)
                    dve.wait_ge(biased, layer + 1)
                    dve.tensor_scalar(k, a, 1 / (2 * math.pi), ROUND, ALU.mult, ALU.add).then_inc(reduced, 1)
                    dve.wait_ge(reduced, n + 1)
                    dve.tensor_scalar(k, k, -ROUND, None, ALU.add).then_inc(reduced, 1)
                    dve.wait_ge(reduced, n + 2)
                    for j, part in enumerate((PI2_A, PI2_B, PI2_C)):
                        dve.scalar_tensor_tensor(out=a, in0=k, scalar=-part, in1=a, op0=ALU.mult, op1=ALU.add).then_inc(reduced, 1)
                        dve.wait_ge(reduced, n + 3 + j)
                    dve.tensor_scalar(a, a, BELOW_PI, -BELOW_PI, ALU.min, ALU.max).then_inc(reduced, 1)
                    n += 6
                dve.wait_ge(sines, 2)
                dve.wait_ge(zeroed, 1)
                dve.tensor_copy(h2r[rows, :], h2[rows, LAT:LAT - FOLD:-1]).then_inc(flipped, 1)
                dve.tensor_copy(h2b[rows, :], h2[rows, 0:P]).then_inc(flipped, 1)
                dve.wait_ge(flipped, 2)
                dve.memset(h2b[rows, 0:1], 0.0).then_inc(flipped, 1)

            @block.scalar
            def _(act):
                for layer in range(2):
                    act.wait_ge(reduced, 6 * (layer + 1))
                    act.activation((h1, h2)[layer][rows, 0:LAT], ang[rows, :], ACT.Sin).then_inc(sines, 1)

    names = "taps row_taps weighed row_weighed paired row_paired folded product read_out halved stored0 stored1 stored2"
    with stage(nc, names) as (mem, sems):
        taps, row_taps, weighed, row_weighed, paired, row_paired, folded, product, read_out, halved = sems[:10]
        stored = sems[10:]
        four = tile(nc, mem, "taps_weighed", [P, 4, W_HY])
        two = tile(nc, mem, "taps_paired", [P, 4, W_HY])
        pm = tile(nc, mem, "taps_folded", [P, 4, ORD, FT, W_HY])
        mid = tile(nc, mem, "taps_middle", [1, 2, W_HY])
        mid_sum = tile(nc, mem, "taps_middle_paired", [1, ORD, 2, W_HY])
        sp_out = tile(nc, mem, "spectrum_out", [P, 3, W_HY])
        SRC = {"cos_even": 0, "cos_odd": 1, "sin_odd": 2, "sin_even": 3}
        units = [(o, i, q) for o in range(ORD) for i in range(FT) for q in range(4)]
        per_order = 4 * FT + 1
        rows = slice(0, 64)
        with nc.Block() as block:
            @block.sync
            def _(sp):
                for o in range(ORD):
                    for n in range(per_order):
                        e = o * per_order + n
                        sp.wait_ge(halved, o + 1) if n == 0 else sp.wait_ge(read_out, e + 1)
                        if n < 4 * FT:
                            i, q = divmod(n, 4)
                            parity, kind = q // 2, q % 2
                            sp.dma_start(spectra.h[o, parity * 8 + kind * 4 + i], sp_out[:, e % 3, :]).then_inc(stored[e % 3], 16)
                        else:
                            sp.dma_start(spectra.last[o:o + 1], sp_out[0:1, e % 3, :]).then_inc(stored[e % 3], 16)
                E = ORD * per_order
                for s in range(3):
                    sp.wait_ge(stored[s], 16 * len(range(s, E, 3)))

            @block.tensor
            def _(pe):

                def tap_products(o, jt):
                    q = o * FT + jt
                    if q:
                        pe.wait_ge(weighed, 4 * q)
                    f, b = w3[rows, (2 * o) * W_HY:(2 * o + 1) * W_HY], w3[rows, (2 * o + 1) * W_HY:(2 * o + 2) * W_HY]
                    js = slice(jt * P, (jt + 1) * P)
                    pe.matmul(g.ps[:, 0, :], h2[rows, js], f, start=True, stop=True)
                    pe.matmul(g.ps[:, 1, :], h2b[rows, :] if jt == 0 else h2[rows, js], b, start=True, stop=True)
                    pe.matmul(g.ps[:, 2, :], h2r[rows, js], f, start=True, stop=True)
                    pe.matmul(g.ps[:, 3, :], h2r[rows, js], b, start=True, stop=True).then_inc(taps, 1)

                def middle_products(o):
                    for n in range(2):
                        if 2 * o + n:
                            pe.wait_ge(row_weighed, 2 * o + n)
                        pe.matmul(g.ps[0:1, 4, :], h2[rows, FOLD:FOLD + 1], w3[rows, (2 * o + n) * W_HY:(2 * o + n + 1) * W_HY],
                                  start=True, stop=True).then_inc(row_taps, 1)

                def spectrum(o, n):
                    e = o * per_order + n
                    if e >= 3:
                        pe.wait_ge(read_out, e - 2)
                    if n == 0:
                        pe.wait_ge(folded, 4 * FT * (o + 1))
                        pe.wait_ge(row_paired, 2 * (o + 1))
                    bank = 5 + e % 3
                    if n < 4 * FT:
                        i, q = divmod(n, 4)
                        part, fold, middle = PARTS[q]
                        for jt in range(FT):
                            mm = pe.matmul(g.ps[:, bank, :], tabs[:, q, jt, i * P:(i + 1) * P], pm[:, SRC[part], o, jt, :], start=(jt == 0), stop=(jt == FT - 1 and not middle))
                        if middle:
                            mm = pe.matmul(g.ps[:, bank, :], alt_row[:, 0:P], mid_sum[:, o, 0 if part == "cos_even" else 1, :], start=False, stop=True)
                    else:
                        for jt in range(FT):
                            pe.matmul(g.ps[0:1, bank, :], alt_col[:], pm[:, 0, o, jt, :], start=(jt == 0), stop=False)
                        mm = pe.matmul(g.ps[0:1, bank, :], alt_row[:, 0:1], mid_sum[:, o, 0, :], start=False, stop=True)
                    mm.then_inc(product, 1)

                for jt in range(FT):
                    tap_products(0, jt)
                middle_products(0)
                for n in range(per_order):
                    if n % 4 == 0 and n // 4 < FT:
                        tap_products(1, n // 4)
                    spectrum(0, n)
                middle_products(1)
                for n in range(per_order):
                    spectrum(1, n)

            @block.scalar
            def _(act):
                for e in range(ORD * per_order):
                    o, n = divmod(e, per_order)
                    act.wait_ge(product, e + 1)
                    if e >= 3:
                        act.wait_ge(stored[e % 3], 16 * (e // 3))
                    if n < 4 * FT:
                        act.activation(sp_out[:, e % 3, :], g.ps[:, 5 + e % 3, :], ACT.Copy, scale=1.0 / LAT).then_inc(read_out, 1)
                        if n == 0:
                            act.wait_ge(read_out, e + 1)
                            act.activation(sp_out[0:1, e % 3, :], sp_out[0:1, e % 3, :], ACT.Copy, scale=0.5).then_inc(halved, 1)
                    else:
                        act.activation(sp_out[0:1, e % 3, :], g.ps[0:1, 5 + e % 3, :], ACT.Copy, scale=0.5 / LAT).then_inc(read_out, 1)

            @block.vector
            def _(dve):
                for o in range(ORD):
                    for jt in range(FT):
                        q = o * FT + jt
                        dve.wait_ge(taps, q + 1)
                        if q:
                            dve.wait_ge(paired, 4 * q)
                            dve.wait_ge(folded, 4 * q)
                        for n in range(4):
                            dve.tensor_tensor(four[:, n, :], g.ps[:, n, :], dec[:, n // 2, jt, :], ALU.mult).then_inc(weighed, 1)
                        dve.wait_ge(weighed, 4 * (q + 1))
                        for n, (x, op) in enumerate(((0, ALU.add), (2, ALU.add), (0, ALU.subtract), (2, ALU.subtract))):
                            dve.tensor_tensor(two[:, n, :], four[:, x, :], four[:, x + 1, :], op).then_inc(paired, 1)
                        dve.wait_ge(paired, 4 * (q + 1))
                        for n, (x, op) in enumerate(((0, ALU.add), (0, ALU.subtract), (2, ALU.add), (2, ALU.subtract))):
                            dve.tensor_tensor(pm[:, n, o, jt, :], two[:, x, :], two[:, x + 1, :], op).then_inc(folded, 1)
                    for n in range(2):
                        dve.wait_ge(row_taps, 2 * o + n + 1)
                        if o and n == 0:
                            dve.wait_ge(row_paired, 2 * o)
                        dve.tensor_tensor(mid[:, n, :], g.ps[0:1, 4, :], dec_row[:], ALU.mult).then_inc(row_weighed, 1)
                    dve.wait_ge(row_weighed, 2 * (o + 1))
                    dve.tensor_tensor(mid_sum[:, o, 0, :], mid[:, 0, :], mid[:, 1, :], ALU.add).then_inc(row_paired, 1)
                    dve.tensor_tensor(mid_sum[:, o, 1, :], mid[:, 0, :], mid[:, 1, :], ALU.subtract).then_inc(row_paired, 1)


def project_hyena(nc, g, d, high, low, u3):
    TILES, BANKS = 12, 8
    units = [(t, a, n) for t in range(TILES) for a, n in CHUNKS[:2]]
    C = 2
    with stage(nc, "raw_in0 raw_in1 w_rounded w_split product raw_out padded steps conv stored0 stored1") as (mem, sems):
        w_sems, (product, raw_out, padded, steps, conv), stored = sems[:4], sems[4:9], sems[9:]
        ring = WeightRing(nc, mem, w_sems, product, [C * (t + 1) for t in range(TILES)])
        raw = tile(nc, mem, "hy_raw", [P, 2, LAT + 2])
        res = tile(nc, mem, "hy_conv", [P, 2, LAT])
        with nc.Block() as block:
            @block.sync
            def _(sp):
                for t in range(TILES + 3):
                    if t < TILES:
                        ring.load(sp, t, d["w_hy"][t])
                    if t >= 3:
                        v = t - 3
                        sp.wait_ge(conv, v + 1)
                        sp.dma_start(u3[:, v, :], res[:, v % 2, :]).then_inc(stored[v % 2], 16)
                for s in range(2):
                    sp.wait_ge(stored[s], 16 * (TILES // 2))

            @block.tensor
            def _(pe):
                for u, (t, a, n) in enumerate(units):
                    if u % C == 0:
                        pe.wait_ge(ring.split, t + 1)
                    if u >= BANKS:
                        pe.wait_ge(raw_out, u - BANKS + 1)
                    ring.product_of(pe, g.ps[:, u % BANKS, 0:n], t, high, low, a, n).then_inc(product, 1)

            @block.scalar
            def _(act):
                ring.round_piece(act, 0)
                act.wait_ge(padded, 1)
                for u, (t, a, n) in enumerate(units):
                    if u % C == 0:
                        ring.round_piece(act, t + 1)
                    act.wait_ge(product, u + 1)
                    if t >= 2 and u % C == 0:
                        act.wait_ge(conv, t - 1)
                    act.activation(raw[:, t % 2, 1 + a:1 + a + n], g.ps[:, u % BANKS, 0:n], ACT.Copy).then_inc(raw_out, 1)

            @block.vector
            def _(dve):
                dve.memset(raw[:], 0.0).then_inc(padded, 1)
                ring.split_piece(dve, 0)
                for t in range(TILES):
                    ring.split_piece(dve, t + 1)
                    dve.wait_ge(raw_out, C * (t + 1))
                    if t >= 2:
                        dve.wait_ge(stored[t % 2], 16 * (t // 2))
                    tap = lambda i: vec(g, "short_w", i * TILES + t)
                    dve.tensor_scalar(res[:, t % 2, :], raw[:, t % 2, 0:LAT], tap(0), vec(g, "short_b", t), ALU.mult, ALU.add).then_inc(steps, 1)
                    dve.wait_ge(steps, 2 * t + 1)
                    dve.scalar_tensor_tensor(out=res[:, t % 2, :], in0=raw[:, t % 2, 1:1 + LAT], scalar=tap(1), in1=res[:, t % 2, :], op0=ALU.mult, op1=ALU.add).then_inc(steps, 1)
                    dve.wait_ge(steps, 2 * t + 2)
                    dve.scalar_tensor_tensor(out=res[:, t % 2, :], in0=raw[:, t % 2, 2:2 + LAT], scalar=tap(2), in1=res[:, t % 2, :], op0=ALU.mult, op1=ALU.add).then_inc(conv, 1)


def long_convs(nc, g, d, spectra, u3_src, u3):
    ORD, CT = 2, W_HY // P
    names = ("back_in u3_in0 u3_in1 u3_in2 h_in0 h_in1 h_in2 last_in folded first_copied turned turned_out mid_turned mid_out product mult combined last_made "
             "inverse sym_out times mirrored middle skipped gated")
    with stage(nc, names) as (mem, sems):
        (back_in, u3_in0, u3_in1, u3_in2, h_in0, h_in1, h_in2, last_in, folded, first_copied, turned, turned_out, mid_turned, mid_out, product, mult, combined, last_made,
         inverse, sym_out, times, mirrored, middle, skipped, gated) = sems
        u3_in, h_in = (u3_in0, u3_in1, u3_in2), (h_in0, h_in1, h_in2)
        tabs = spectra.tabs
        back = tile(nc, mem, "dft_back", [P, 2, FT, FOLD])
        alt_row, alt_col = spectra.alt_row, spectra.alt_col
        fold = tile(nc, mem, "folded", [P, 2, CT, FOLD])
        tim = tile(nc, mem, "folded_turned", [P, 2, FT, W_HY])
        mid = tile(nc, mem, "middle_time", [1, W_HY])
        h = tile(nc, mem, "filter_ring", [P, 3, 2, W_HY])
        hl = tile(nc, mem, "filter_last", [1, W_HY])
        yv = tile(nc, mem, "output_spectrum", [P, 4, FT, W_HY])
        yl = tile(nc, mem, "output_last", [1, W_HY])
        pr = tile(nc, mem, "products", [P, 4, W_HY])
        sym = tile(nc, mem, "symmetric", [P, 2, FOLD + 1])
        tm = tile(nc, mem, "convolved", [P, 2, LAT])
        z = u3
        with nc.Block() as block:
            @block.sync
            def _(sp):
                sp.dma_start(u3[:, 0:CT, :], u3_src[:, 0:CT, :]).then_inc(u3_in[0], 16)
                for o in range(ORD):
                    if o:
                        sp.wait_ge(last_made, 1)
                    sp.dma_start(hl[:], spectra.last[o:o + 1]).then_inc(last_in, 16)
                    filters = spectra.h[o].rearrange("(q k i) p n -> q i p k n", q=2, k=2)
                    for n in range(2 * FT):
                        w = o * 2 * FT + n
                        if w >= 3:
                            sp.wait_ge(mult, 4 * (w - 2))
                        sp.dma_start(h[:, w % 3], filters[n // FT, n % FT]).then_inc(h_in[w % 3], 16)
                        if w == 2:
                            sp.dma_start(back[:], d["dft_back"]).then_inc(back_in, 16)
                        if w in (3, 4):
                            sp.dma_start(u3[:, CT * (w - 2):CT * (w - 1), :], u3_src[:, CT * (w - 2):CT * (w - 1), :]).then_inc(u3_in[w - 2], 16)

            @block.tensor
            def _(pe):
                n_turn = 0
                for o in range(ORD):
                    for s in range(2):
                        for jt in range(FT):
                            pe.wait_ge(folded, 2 * CT * (o + 1))
                            if n_turn >= 2:
                                pe.wait_ge(turned_out, n_turn - 1)
                            for ct in range(CT):
                                mm = pe.transpose(g.ps[:, n_turn % 2, ct * P:(ct + 1) * P], fold[:, s, ct, jt * P:(jt + 1) * P], g.ident[:])
                            mm.then_inc(turned, 1)
                            n_turn += 1
                    for ct in range(CT):
                        src = z[:, ct, FOLD:FOLD + 1]
                        mm = pe.transpose(g.ps[0:1, 2, ct * P:(ct + 1) * P], src, g.ident[:])
                    mm.then_inc(mid_turned, 1)
                    pe.wait_ge(turned_out, 2 * FT * (o + 1))
                    pe.wait_ge(mid_out, o + 1)
                    n = 0
                    for parity in range(2):
                        for i in range(FT):
                            w = o * 2 * FT + n
                            for kind in range(2):
                                q = 2 * parity + kind
                                part, src, middle_counts = PARTS[q]
                                bank = 3 + 2 * (n % 2) + kind
                                if n >= 2 and kind == 0:
                                    pe.wait_ge(mult, 4 * (w - 1))
                                for jt in range(FT):
                                    mm = pe.matmul(g.ps[:, bank, :], tabs[:, q, jt, i * P:(i + 1) * P], tim[:, 0 if src == "sum" else 1, jt, :],
                                                   start=(jt == 0), stop=(jt == FT - 1 and not middle_counts))
                                if middle_counts:
                                    mm = pe.matmul(g.ps[:, bank, :], alt_row[:, 0:P], mid[:], start=False, stop=True)
                            mm.then_inc(product, 1)
                            n += 1
                    for jt in range(FT):
                        pe.matmul(g.ps[0:1, 7, :], alt_col[:], tim[:, 0, jt, :], start=(jt == 0), stop=False)
                    pe.matmul(g.ps[0:1, 7, :], alt_row[:, 0:1], mid[:], start=False, stop=True).then_inc(product, 1)
                    pe.wait_ge(back_in, 16)
                    pe.wait_ge(combined, 4 * FT * (o + 1))
                    pe.wait_ge(last_made, o + 1)
                    for ct in range(CT):
                        v = o * CT + ct
                        cs = slice(ct * P, (ct + 1) * P)
                        a_bank, b_bank, c_bank = (0, 1, 2) if v % 2 == 0 else (3, 4, 5)
                        if ct >= 2:
                            pe.wait_ge(mirrored, v - 1)
                            pe.wait_ge(sym_out, 2 * (v - 1))
                        for bank, (p0, t0), (p1, t1) in ((a_bank, (0, tabs[:, 0]), (3, back[:, 1])), (b_bank, (2, back[:, 0]), (1, tabs[:, 1]))):
                            for pp, tab in ((p0, t0), (p1, t1)):
                                for i in range(FT):
                                    mm = pe.matmul(g.ps[:, bank, :], yv[:, pp, i, cs], tab[:, i, :], start=(pp == p0 and i == 0),
                                                   stop=(bank == b_bank and pp == p1 and i == FT - 1))
                            if bank == a_bank:
                                pe.matmul(g.ps[:, bank, :], yl[:, cs], alt_row[:], start=False, stop=True)
                        for pp in (0, 3):
                            for i in range(FT):
                                pe.matmul(g.ps[:, c_bank, 0:1], yv[:, pp, i, cs], alt_col[:], start=(pp == 0 and i == 0), stop=False)
                        pe.matmul(g.ps[:, c_bank, 0:1], yl[:, cs], alt_row[:, 0:1], start=False, stop=True).then_inc(inverse, 1)

            @block.scalar
            def _(act):
                n_turn = 0
                for o in range(ORD):
                    for s in range(2):
                        for jt in range(FT):
                            act.wait_ge(turned, n_turn + 1)
                            if o and n_turn == 2 * FT:
                                act.wait_ge(product, 2 * FT + 1)
                            act.activation(tim[:, s, jt, :], g.ps[:, n_turn % 2, :], ACT.Copy).then_inc(turned_out, 1)
                            n_turn += 1
                    act.wait_ge(mid_turned, o + 1)
                    act.activation(mid[:], g.ps[0:1, 2, :], ACT.Copy).then_inc(mid_out, 1)
                    for ct in range(CT):
                        v = o * CT + ct
                        act.wait_ge(inverse, v + 1)
                        if v >= 2:
                            act.wait_ge(mirrored, v - 1)
                            act.wait_ge(middle, v - 1)
                        a_bank, c_bank = (0, 2) if v % 2 == 0 else (3, 5)
                        act.activation(sym[:, v % 2, 0:FOLD], g.ps[:, a_bank, :], ACT.Copy).then_inc(sym_out, 1)
                        act.activation(sym[:, v % 2, FOLD:FOLD + 1], g.ps[:, c_bank, 0:1], ACT.Copy).then_inc(sym_out, 1)

            @block.vector
            def _(dve):
                def fold_tile(src, ct):
                    x = src[:, ct, :]
                    head, tail = x[:, 1:FOLD], x[:, LAT - 1:FOLD:-1]
                    dve.tensor_tensor(fold[:, 0, ct, 1:FOLD], head, tail, ALU.add).then_inc(first_copied, 1)
                    dve.tensor_tensor(fold[:, 1, ct, 1:FOLD], head, tail, ALU.subtract).then_inc(first_copied, 1)
                    dve.tensor_copy(fold[:, 0, ct, 0:1], x[:, 0:1]).then_inc(folded, 1)
                    dve.tensor_copy(fold[:, 1, ct, 0:1], x[:, 0:1]).then_inc(folded, 1)

                dve.wait_ge(u3_in[0], 16)
                for ct in range(CT):
                    fold_tile(z, ct)
                for o in range(ORD):
                    n = 0
                    for parity in range(2):
                        for i in range(FT):
                            w = o * 2 * FT + n
                            dve.wait_ge(product, o * (2 * FT + 1) + n + 1)
                            dve.wait_ge(h_in[w % 3], 16 * (w // 3 + 1))
                            if w:
                                dve.wait_ge(combined, 2 * w)
                            if o and n == 0:
                                dve.wait_ge(inverse, CT * o)
                            c_ps, s_ps = g.ps[:, 3 + 2 * (n % 2), :], g.ps[:, 4 + 2 * (n % 2), :]
                            ch, sh = h[:, w % 3, 0, :], h[:, w % 3, 1, :]
                            for m, (x, y_) in enumerate(((c_ps, ch), (s_ps, sh), (c_ps, sh), (s_ps, ch))):
                                dve.tensor_tensor(pr[:, m, :], x, y_, ALU.mult).then_inc(mult, 1)
                            dve.wait_ge(mult, 4 * (w + 1))
                            dve.tensor_tensor(yv[:, 2 * parity, i, :], pr[:, 0, :], pr[:, 1, :], ALU.subtract).then_inc(combined, 1)
                            dve.tensor_tensor(yv[:, 2 * parity + 1, i, :], pr[:, 2, :], pr[:, 3, :], ALU.add).then_inc(combined, 1)
                            n += 1
                    dve.wait_ge(product, (o + 1) * (2 * FT + 1))
                    dve.wait_ge(last_in, 16 * (o + 1))
                    if o:
                        dve.wait_ge(inverse, CT * o)
                    dve.tensor_tensor(yl[:], g.ps[0:1, 7, :], hl[:], ALU.mult).then_inc(last_made, 1)
                    dve.wait_ge(u3_in[o + 1], 16)
                    for ct in range(CT):
                        v = o * CT + ct
                        b_bank = 1 if v % 2 == 0 else 4
                        dve.wait_ge(sym_out, 2 * (v + 1))
                        if v >= 2:
                            dve.wait_ge(skipped, v - 1)
                        t = tm[:, v % 2, :]
                        dve.tensor_tensor(t[:, 0:FOLD], sym[:, v % 2, 0:FOLD], g.ps[:, b_bank, :], ALU.add).then_inc(times, 1)
                        dve.tensor_copy(t[:, FOLD:FOLD + 1], sym[:, v % 2, FOLD:FOLD + 1]).then_inc(middle, 1)
                        dve.tensor_tensor(t[:, LAT - 1:FOLD:-1], sym[:, v % 2, 1:FOLD], g.ps[:, b_bank, 1:FOLD], ALU.subtract).then_inc(mirrored, 1)
                        dve.wait_ge(times, v + 1)
                        dve.wait_ge(middle, v + 1)
                        dve.wait_ge(mirrored, v + 1)
                        prev = z[:, ct, :]
                        if o:
                            dve.wait_ge(gated, ct + 1)
                        dve.scalar_tensor_tensor(out=t, in0=prev, scalar=vec(g, "skip", 4 * o + ct), in1=t, op0=ALU.mult, op1=ALU.add).then_inc(skipped, 1)
                        dve.wait_ge(skipped, v + 1)
                        dve.tensor_tensor(z[:, ct, :], t, u3[:, CT * (o + 1) + ct, :], ALU.mult).then_inc(gated, 1)
                        if o == 0:
                            dve.wait_ge(gated, v + 1)
                            if ct == 0:
                                dve.wait_ge(mid_turned, 1)
                            fold_tile(z, ct)


def build_program(nc, d):
    g = Globals()
    STAGES.clear()
    with ExitStack() as mem:
        def sb(name, shape):
            return tile(nc, mem, name, shape)

        g.ps = mem.enter_context(nc.psum_tensor("psum", [P, 8, BANK], F32))
        g.vec = sb("small_vectors", [P, NVEC])
        g.ident = sb("identity", [P, P])
        g.ones = sb("all_ones", [P, P])
        g.cond = sb("conditioning", [P, KT, 32])
        g.mod = sb("modulation", [P, 2, 6, KT, 2])
        g.eps = sb("epsilon", [P, 1])

        sc = Globals()
        def scratch(name, shape):
            return nc.dram_tensor(name, shape, F32, kind="Internal").ap()
        sc.qk_a = scratch("scratch_qk_a", [5, P, TOK])
        sc.v_a = scratch("scratch_v_a", [P, KTILES, P])
        sc.q_b = scratch("scratch_q_b", [B_HEADS, B_DK, TOK])
        sc.k_b = scratch("scratch_k_b", [B_HEADS, B_DK, TOK])
        sc.v_b = scratch("scratch_v_b", [P, KTILES, B_HEADS * B_V])

        sc.x = scratch("scratch_x", [P, KT, TOK])
        sc.u3 = scratch("scratch_hyena", [P, 12, LAT])
        sc.y = scratch("scratch_ssd", [P, 4, LAT])
        sc.h = scratch("scratch_spectra", [2, 16, P, W_HY])
        sc.last = scratch("scratch_last", [2, W_HY])

        load_constants(nc, g, d)
        adaln_0(nc, g, d)
        layer_0(nc, g, d, sc)
        layer_1(nc, g, d, sc)


def layer_0(nc, g, d, sc):
    allocate_parts(nc, g, TOK)
    residual_norm(nc, g, d["x"], None, None, None, (0, SCALE_A, SHIFT_A), TOK)
    with ExitStack() as sc.mem:
        project_attention(nc, g, d, sc)
    g.parts_memory.close()
    with ExitStack() as attended:
        mixed = tile(nc, attended, "mixed", [P, KT, TOK], "right")
        attention(nc, g, sc, mixed)
        allocate_parts(nc, g, TOK)
        out = tile(nc, g.out_memory, "out", [P, KT, TOK])
        project_out(nc, g, mixed, d["w_out0"], out, TOK)
    residual_norm(nc, g, d["x"], sc.x, out, (0, GATE_A), (0, SCALE_M, SHIFT_M), TOK, True)
    mlp(nc, g, out, g.high, g.low, d["ff_w"][0], TOK)
    residual_norm(nc, g, sc.x, sc.x, out, (0, GATE_M), (1, SCALE_A, SHIFT_A), TOK)
    g.out_memory.close()


def allocate_parts(nc, g, tokens, side="left"):
    g.parts_memory, g.out_memory = ExitStack(), ExitStack()
    g.high, g.low = tile_r(nc, g.parts_memory, "h_high", [P, KT, tokens], side), tile_r(nc, g.parts_memory, "h_low", [P, KT, tokens], side)


def layer_1(nc, g, d, sc):
    with ExitStack() as memory:
        project_hyena(nc, g, d, g.high, g.low, sc.u3)
        y = tile(nc, memory, "ssd_out", [P, 4, LAT], "right")
        xbc = tile(nc, memory, "xbc", [P, 8, TOK], "right")
        gate = tile(nc, memory, "gate", [P, 4, LAT], "right")
        dt, adt = tile(nc, memory, "dt", [P, KTILES, 16], "right"), tile(nc, memory, "adt", [P, KTILES, 16], "right")
        project_mamba(nc, g, d, g.high, g.low, xbc, gate, dt, adt)
        g.parts_memory.close()
        with ExitStack() as tokens_first:
            ssd = Globals()
            ssd.mem, ssd.y = tokens_first, y
            scan_states(nc, g, d, xbc, gate, dt, adt, ssd)
        gate_norm(nc, g, xbc, gate, y, y)
        store(nc, y, sc.y)
    spectra = Globals()
    spectra.h, spectra.last = sc.h, sc.last
    with ExitStack() as memory:
        spectra.alt_row = tile(nc, memory, "alternate_row", [1, FOLD])
        spectra.alt_col = tile(nc, memory, "alternate_column", [P, 1])
        tables = ExitStack()
        spectra.tabs = tile(nc, tables, "dft", [P, 4, FT, FOLD], "right")
        with ExitStack() as features:
            spectra.w3 = tile(nc, features, "hy_w3", [P, 2 * 2 * W_HY])
            spectra.decay = tile(nc, features, "decay", [P, 2, FT, W_HY])
            spectra.decay_row = tile(nc, features, "decay_middle", [1, W_HY])
            spectra.h2 = tile(nc, features, "hy_h2", [P, LAT + 1])
            spectra.h2r = tile(nc, features, "hy_h2_flipped", [P, FOLD])
            spectra.h2b = tile(nc, features, "hy_h2_behind", [P, P])
            hyena_spectra(nc, g, d, spectra)
        memory_left = ExitStack()
        u3 = tile(nc, memory_left, "hyena_parts", [P, 12, LAT])
        long_convs(nc, g, d, spectra, sc.u3, u3)
        tables.close()
        mixed = u3[:, 0:KT, :]
        load(nc, [(mixed[:, 4:KT, :], sc.y)])
        out = tile(nc, memory, "out", [P, KT, LAT], "right")
        allocate_parts(nc, g, LAT, "right")
        project_out(nc, g, mixed, d["w_out1"], out, LAT)
        memory_left.close()
        residual_norm(nc, g, sc.x, sc.x, out, (1, GATE_A), (1, SCALE_M, SHIFT_M), LAT, True)
        mlp(nc, g, out, g.high, g.low, d["ff_w"][1], LAT)
        g.parts_memory.close()
        residual_norm(nc, g, sc.x, d["out"], out, (1, GATE_M), None, LAT)


def store(nc, src, dst):
    with stage(nc, "stored") as (mem, (stored,)):
        with nc.Block() as block:
            @block.sync
            def _(sp):
                sp.dma_start(dst, src[:]).then_inc(stored, 16)
                sp.wait_ge(stored, 16)


def feature_tiles(v):
    return np.ascontiguousarray(v.reshape(-1, P).T)


def k_major(w):
    return w.reshape(-1, P, w.shape[1]).transpose(1, 0, 2)


def pieces(w, width=256):
    kk = k_major(w)
    return np.ascontiguousarray(kk.reshape(P, kk.shape[1], -1, width).transpose(2, 0, 1, 3))


def rope_tables():
    t = np.arange(LAT)
    t_row, t_col = (t // GRID_W).astype(np.float32), (t % GRID_W).astype(np.float32)
    def angles(rot):
        quarter = rot // 4
        inv = np.float32(THETA) ** (-np.arange(quarter, dtype=np.float32) / np.float32(quarter))
        return np.concatenate([t_row[None, :] * inv[:, None], t_col[None, :] * inv[:, None]]).astype(np.float32)
    a = {}
    for tag, first, rot, heads in (("a", 0, A_DIM, 2), ("b", B_NOPE, B_ROPE, 1)):
        ang, half = angles(rot), rot // 2
        cos, sin, swap = np.ones((P, TOK), np.float32), np.zeros((P, TOK), np.float32), np.zeros((P, P), np.float32)
        for h in range(heads):
            at = first + h * rot
            for part, sign in ((0, -1), (1, 1)):
                r = np.arange(at + part * half, at + (part + 1) * half)
                cos[r, :LAT] = np.cos(ang)
                sin[r, :LAT] = sign * np.sin(ang)
                swap[r + (half if part == 0 else -half), r] = 1
        a[f"cos_{tag}"], a[f"sin_{tag}"], a[f"swap_{tag}"] = cos, sin, swap
    a["by_head"] = np.kron(np.eye(2), np.ones((A_DIM, A_DIM))).astype(np.float32)
    return a


def hyena_tables():
    f32 = np.float32
    a = {}
    bands = 16
    t = np.linspace(0.0, 1.0, LAT, dtype=f32)
    w = (f32(2.0 * math.pi) * np.arange(LAT, dtype=f32) / f32(LAT)).astype(f32)
    ph = w[:, None] * np.linspace(1e-4, bands - 1, bands, dtype=f32)[None, :]
    a["positions"] = np.ascontiguousarray(np.concatenate([t[:, None], np.cos(ph), -np.sin(ph)], axis=1).T.astype(f32))
    deltas = np.abs(np.linspace(math.log(1e-2) / 1.5, math.log(1e-2) / 0.3, W_HY, dtype=f32))
    decay = np.exp(-t[:, None] * deltas[None, :]).astype(f32)
    tiles = lambda x: x.reshape(FT, P, -1).transpose(1, 0, 2)
    ahead = np.concatenate([np.zeros((1, W_HY), f32), decay[:FOLD:-1]])
    a["decay"] = np.ascontiguousarray(np.stack([tiles(decay[:FOLD]), tiles(ahead)], axis=1))
    a["decay_middle"] = np.ascontiguousarray(decay[FOLD:FOLD + 1])
    j, m = np.arange(FOLD)[:, None], np.arange(FOLD)[None, :]
    even, odd = 2 * np.pi * (m * j % LAT) / LAT, np.pi * (j * (2 * m + 1) % (2 * LAT)) / LAT
    forms = [np.cos(even), np.sin(even), np.cos(odd), np.sin(odd)]
    a["dft"] = np.ascontiguousarray(np.stack([tiles(x) for x in forms], axis=1).astype(f32))
    a["dft_back"] = np.ascontiguousarray(np.stack([tiles(x.T) for x in forms[2:]], axis=1).astype(f32))
    a["alt_row"] = ((-1.0) ** np.arange(FOLD)).astype(f32)[None, :]
    a["alt_col"] = ((-1.0) ** np.arange(P)).astype(f32)[:, None]
    s, l = np.arange(P)[:, None], np.arange(P)[None, :]
    a["triangles"] = np.ascontiguousarray(np.stack([s <= l, s >= l], axis=1).astype(f32))
    return a


def lay_out(i):
    a = {}
    tokens = np.concatenate([i["x"][0], i["ctx"][0]], axis=0)
    a["x"] = np.ascontiguousarray(tokens.T.reshape(KT, P, TOK).transpose(1, 0, 2))
    a["cond"] = np.zeros((P, KT, 32), np.float32)
    a["cond"][:, :, 0:2] = np.stack([i["c"][0], i["c_ctx"]], axis=1).reshape(KT, P, 2).transpose(1, 0, 2)
    a["group_selector"] = np.tile(np.eye(32, 2, dtype=np.float32), (4, 1))
    a["ident"] = np.eye(P, dtype=np.float32)
    a["ones"] = np.ones((P, P), np.float32)
    a["ada_w"] = np.concatenate([pieces(i["ada_w"][l], BANK) for l in range(2)])
    def eighths(w1, w2):
        up = pieces(w1, P).reshape(8, 4, P, KT, P)
        down = [pieces(w2[e * 512:(e + 1) * 512]).reshape(4, P, KT, P) for e in range(8)]
        return np.concatenate([up, np.stack(down)], axis=1).reshape(64, P, KT, P)
    a["ff_w"] = np.stack([eighths(i["ff_w1"][l], i["ff_w2"][l]) for l in range(2)])

    w = i["at_w_in"][0]
    k_a, v_a, low, key, q_a, q_low = np.split(w, np.cumsum([128, 128, 128, 32, 512]), axis=1)
    a["w_qk"] = pieces(np.concatenate([k_a, q_a], axis=1), P)
    a["w_low"] = np.ascontiguousarray(np.stack([k_major(x) for x in (q_low[:, :P], q_low[:, P:], low, v_a)], axis=1))
    a["w_key"] = np.ascontiguousarray(k_major(key))
    up = i["ml_w_kv_up"][0].reshape(P, B_HEADS, B_NOPE + B_V)
    a["w_k_up"] = np.ascontiguousarray(up[:, :, :B_NOPE].reshape(P, -1))
    a["w_v_up"] = np.ascontiguousarray(up[:, :, B_NOPE:].reshape(P, -1))
    a["w_q_up"] = np.ascontiguousarray(k_major(i["ml_w_q_up"][0]))
    a["w_out0"] = pieces(i["at_w_out"][0], P)
    w_hy, w_z, w_xbc, w_dt = np.split(i["lc_w_in"][0], np.cumsum([1536, 512, 1024]), axis=1)
    a["w_hy"], a["w_z"], a["w_xbc"] = pieces(w_hy, P), pieces(w_z, P), pieces(w_xbc, P)
    a["w_dt"] = np.ascontiguousarray(k_major(w_dt))
    a["w_out1"] = pieces(i["lc_w_out"][0], P)
    a["hy_w1"], a["hy_w2"], a["hy_w3"] = (np.ascontiguousarray(i[n][0]) for n in ("hy_w1", "hy_w2", "hy_w3"))
    a.update(hyena_tables())
    a.update(rope_tables())

    v = np.zeros((P, NVEC), np.float32)
    def put(name, cols, at=0):
        v[:cols.shape[0], VEC[name][0] + at:VEC[name][0] + at + cols.shape[1]] = cols
    put("ada_b", np.repeat(feature_tiles(i["ada_b"]), 2, axis=1))
    put("norm_g", np.repeat(feature_tiles(i["norm_g"]), 2, axis=1))
    put("gain_k", np.tile(i["ga_k_norm"][0], 2)[:, None])
    put("gain_q", np.tile(i["ga_q_norm"][0], 2)[:, None])
    put("mlq", feature_tiles(i["ml_q_norm"][0]))
    put("mlkv", feature_tiles(i["ml_kv_norm"][0]))
    put("short_w", feature_tiles(i["hy_short_w"][0]))
    put("short_b", feature_tiles(i["hy_short_b"][0]))
    put("skip", feature_tiles(i["hy_skip"][0]))
    put("conv_w", feature_tiles(i["mb_conv_w"][0]))
    put("conv_b", feature_tiles(i["mb_conv_b"][0]))
    put("d_skip", feature_tiles(np.repeat(i["mb_d_skip"][0], 64)))
    put("mb_norm", feature_tiles(i["mb_norm"][0]))
    put("dt_bias", np.tile(i["mb_dt_bias"][0].reshape(1, 16), (P, 1)))
    put("a_log", np.tile(i["mb_a_log"][0].reshape(1, 16), (P, 1)))
    put("hy_b1", i["hy_b1"][0][:, None])
    put("hy_b2", i["hy_b2"][0][:, None])
    put("freq", i["hy_freq"][0][:, None])
    a["vec"] = v
    return a


def kernel(**inputs):
    import concourse.bacc as bacc
    from concourse.bass_utils import run_bass_kernel_spmd

    nc = bacc.Bacc("TRN2", target_bir_lowering=False, num_devices=1)
    laid_out = lay_out({name: np.asarray(a) for name, a in inputs.items()})
    d, arrays = {}, {}
    for name, a in laid_out.items():
        arrays[f"in_{name}_dram"] = a
        d[name] = nc.dram_tensor(f"in_{name}_dram", a.shape, mybir.dt.from_np(a.dtype), kind="ExternalInput").ap()
    d["out"] = nc.dram_tensor("out_0_dram", (P, KT, LAT), F32, kind="ExternalOutput").ap()
    build_program(nc, d)
    r = run_bass_kernel_spmd(nc, [arrays], core_ids=[0])
    got = r.results[0]["out_0_dram"]
    return np.ascontiguousarray(got.transpose(2, 1, 0).reshape(1, LAT, D))
```
